# Optimizing a Trainium2 kernel written in Bass

```python
import math
import jax, jax.numpy as jnp
from jax import lax
import numpy as np

D_MODEL = 1024
BATCH = 1
SEQ = 128
DEPTH = 2
DEC_BATCH = 1
DEC_SEQ = 512
PAST_LEN = 256

GRID_W = 64
N_EVEN = (DEPTH + 1) // 2
N_ODD = DEPTH // 2
A_HEADS = 4
A_DK = 128
A_DV = 128
A_QK = A_HEADS * A_DK
A_WIDTH = A_HEADS * A_DV
HGRN_CHUNK = 16
B_HEADS = 4
B_DH = 64
B_DV = 2 * B_DH
B_QK = B_HEADS * 2 * B_DH
B_WIDTH = B_HEADS * B_DV
C_HEADS = 16
C_KV_HEADS = 4
C_GROUP = C_HEADS // C_KV_HEADS
C_DH = 64
WINDOW = 128
BLOCK = 128
EVEN_SPLITS = [A_QK, 2 * A_QK, 3 * A_QK, 3 * A_QK + A_WIDTH, 3 * A_QK + 2 * A_WIDTH,
               3 * A_QK + 2 * A_WIDTH + B_QK, 3 * A_QK + 2 * A_WIDTH + 2 * B_QK]
EVEN_IN = 3 * A_QK + 2 * A_WIDTH + 2 * B_QK + B_WIDTH
EVEN_MIX = A_WIDTH + B_WIDTH
ODD_SPLITS = [C_HEADS * C_DH, C_HEADS * C_DH + C_KV_HEADS * C_DH]
ODD_IN = C_HEADS * C_DH + 2 * C_KV_HEADS * C_DH
ODD_MIX = C_HEADS * C_DH
N_EXPERTS = 16
CAP_FACTOR = 2
EXPERT_FF = 1024
ALPHA = (2 * DEPTH) ** 0.25
BETA = (8 * DEPTH) ** -0.25
LN_EPS = 1e-5
ROPE_BASE = 10000.0
NEG_INF = -1e30
F32 = jnp.float32

kernel_name = 'hybrid_diffusion_hgrn2_diffattn_swa_ecmoe_step'

def to_heads(x, n_heads):
    B, L, _ = x.shape
    return x.reshape(B, L, n_heads, -1).transpose(0, 2, 1, 3)

def from_heads(x):
    B, H, L, d = x.shape
    return x.transpose(0, 2, 1, 3).reshape(B, L, H * d)

def layer_norm(x, g, b):
    xf = x.astype(F32)
    mu = jnp.mean(xf, -1, keepdims=True)
    var = jnp.mean(jnp.square(xf - mu), -1, keepdims=True)
    return ((xf - mu) * lax.rsqrt(var + LN_EPS) * g.astype(F32) + b.astype(F32)).astype(x.dtype)

def rms_norm(x, g):
    xf = x.astype(F32)
    return xf * lax.rsqrt(jnp.mean(jnp.square(xf), -1, keepdims=True) + LN_EPS) * g.astype(F32)

def rope_2d(x):
    L, d = x.shape[-2], x.shape[-1]
    half, quarter = d // 2, d // 4
    t = jnp.arange(L)
    rows = (t // GRID_W).astype(F32)
    cols = (t % GRID_W).astype(F32)
    inv = ROPE_BASE ** (-jnp.arange(quarter, dtype=F32) / quarter)

    def rot(xh, pos):
        ang = pos[:, None] * inv[None, :]
        cos, sin = jnp.cos(ang).astype(x.dtype), jnp.sin(ang).astype(x.dtype)
        x1, x2 = xh[..., :quarter], xh[..., quarter:]
        return jnp.concatenate([x1 * cos - x2 * sin, x1 * sin + x2 * cos], -1)

    return jnp.concatenate([rot(x[..., :half], rows), rot(x[..., half:], cols)], -1)

def modulation(cvec, w, b):
    m = jnp.einsum('nd,de->ne', jax.nn.silu(cvec), w) + b
    return [t[:, None, :] for t in jnp.split(m, 6, axis=-1)]

def softmax_attend(q, k, v, sink=None):
    B, Hk, G, Nq, d = q.shape
    nblk = Nq // BLOCK
    qb = jnp.moveaxis(q.reshape(B, Hk, G, nblk, BLOCK, d), 3, 0)
    scale = d ** -0.5

    def one_block(qblk):
        s = jnp.einsum('bhgqd,bhkd->bhgqk', qblk, k).astype(F32) * scale
        if sink is not None:
            col = jnp.broadcast_to(sink.astype(F32)[None, :, :, None, None], s.shape[:-1] + (1,))
            p = jax.nn.softmax(jnp.concatenate([s, col], -1), axis=-1)[..., :-1]
        else:
            p = jax.nn.softmax(s, axis=-1)
        return jnp.einsum('bhgqk,bhkd->bhgqd', p.astype(v.dtype), v)

    out = lax.map(one_block, qb)
    return jnp.moveaxis(out, 0, 3).reshape(B, Hk, G, Nq, v.shape[-1])

def window_attend(q, k, v, k_ctx, v_ctx, sink):
    B, Hk, G, L, d = q.shape
    nb = L // BLOCK
    scale = d ** -0.5

    def banded(t):
        tp = jnp.pad(t, ((0, 0), (0, 0), (BLOCK, BLOCK), (0, 0))).reshape(B, Hk, nb + 2, BLOCK, t.shape[-1])
        return jnp.concatenate([tp[:, :, :nb], tp[:, :, 1:nb + 1], tp[:, :, 2:]], axis=3)

    kw, vw = banded(k), banded(v)
    qb = q.reshape(B, Hk, G, nb, BLOCK, d)
    s_loc = jnp.einsum('bhgnqd,bhnkd->bhgnqk', qb, kw).astype(F32) * scale
    q_off = jnp.arange(BLOCK)
    k_off = jnp.arange(3 * BLOCK) - BLOCK
    k_abs = jnp.arange(nb)[:, None] * BLOCK + k_off[None, :]
    in_window = jnp.abs(k_off[None, :] - q_off[:, None]) <= WINDOW
    valid = in_window[None] & ((k_abs >= 0) & (k_abs < L))[:, None, :]
    s_loc = jnp.where(valid, s_loc, NEG_INF)
    s_ctx = jnp.einsum('bhgnqd,bhkd->bhgnqk', qb, k_ctx).astype(F32) * scale
    col = jnp.broadcast_to(sink.astype(F32)[None, :, :, None, None, None], s_loc.shape[:-1] + (1,))
    p = jax.nn.softmax(jnp.concatenate([s_loc, s_ctx, col], -1), axis=-1)
    n_loc, n_ctx = 3 * BLOCK, k_ctx.shape[2]
    out = (jnp.einsum('bhgnqk,bhnkd->bhgnqd', p[..., :n_loc].astype(v.dtype), vw)
           + jnp.einsum('bhgnqk,bhkd->bhgnqd', p[..., n_loc:n_loc + n_ctx].astype(v.dtype), v_ctx))
    return out.reshape(B, Hk, G, L, v.shape[-1])

def hgrn_scan(q, k, v, log_f, s0):
    B, H, L, dk = q.shape
    dv = v.shape[-1]
    nc = L // HGRN_CHUNK

    def chunked(t):
        return jnp.moveaxis(t.astype(F32).reshape(B, H, nc, HGRN_CHUNK, t.shape[-1]), 2, 0)

    causal = jnp.tril(jnp.ones((HGRN_CHUNK, HGRN_CHUNK), dtype=bool))

    def step(S, inp):
        qc, kc, vc, gc = inp
        b = jnp.cumsum(gc, axis=2)
        b_end = b[:, :, -1:, :]
        q_dec = qc * jnp.exp(b)
        k_dec = kc * jnp.exp(-b)
        scores = jnp.where(causal, jnp.einsum('bhcd,bhsd->bhcs', q_dec, k_dec), 0.0)
        o = jnp.einsum('bhcd,bhde->bhce', q_dec, S) + jnp.einsum('bhcs,bhse->bhce', scores, vc)
        S_new = (jnp.exp(b_end[:, :, 0, :])[..., None] * S
                 + jnp.einsum('bhsd,bhse->bhde', kc * jnp.exp(b_end - b), vc))
        return S_new, o

    S_fin, o = lax.scan(step, s0.astype(F32), (chunked(q), chunked(k), chunked(v), chunked(log_f)))
    return jnp.moveaxis(o, 0, 2).reshape(B, H, L, dv), S_fin

def even_mixer(h, lb, hgrn_g, lam, lam_init, diff_g, w_in, w_out, ctx_state=None):
    B, L, _ = h.shape
    p = jnp.einsum('bld,de->ble', h, w_in)
    q_a, f_fw, f_bw, i_a, g_a, q_b, k_b, v_b = jnp.split(p, EVEN_SPLITS, axis=-1)
    q_a, f_fw, f_bw, i_a, g_a = (to_heads(q_a, A_HEADS), to_heads(f_fw, A_HEADS), to_heads(f_bw, A_HEADS),
                                 to_heads(i_a, A_HEADS), to_heads(g_a, A_HEADS))
    q_b, k_b, v_b = to_heads(q_b, B_HEADS), to_heads(k_b, B_HEADS), to_heads(v_b, B_HEADS)
    lbr = lb.reshape(1, A_HEADS, 1, A_DK)

    def gates(z):
        z = z.astype(F32)
        return jnp.log(lbr + (1.0 - lbr) * jax.nn.sigmoid(z)), (1.0 - lbr) * jax.nn.sigmoid(-z)

    logf_fw, key_fw = gates(f_fw)
    logf_bw, key_bw = gates(f_bw)
    if ctx_state is None:
        s0_fw = jnp.zeros((B, A_HEADS, A_DK, A_DV), F32)
        s0_bw = jnp.zeros((B, A_HEADS, A_DK, A_DV), F32)
    else:
        s_hgrn, k_ctx, v_ctx = ctx_state
        s0_fw, s0_bw = s_hgrn[:, 0], s_hgrn[:, 1]
    flip = lambda t: jnp.flip(t, axis=2)
    o_fw, s_fw = hgrn_scan(q_a, key_fw, i_a, logf_fw, s0_fw)
    o_bw, s_bw = hgrn_scan(flip(q_a), flip(key_bw), flip(i_a), flip(logf_bw), s0_bw)
    o_a = rms_norm(o_fw + flip(o_bw), hgrn_g) * jax.nn.silu(g_a.astype(F32))
    if ctx_state is None:
        q1, q2 = q_b[..., :B_DH], q_b[..., B_DH:]
        k_keys, v_keys = k_b, v_b
    else:
        q1, q2 = rope_2d(q_b[..., :B_DH]), rope_2d(q_b[..., B_DH:])
        k_lat = jnp.concatenate([rope_2d(k_b[..., :B_DH]), rope_2d(k_b[..., B_DH:])], -1)
        k_keys = jnp.concatenate([k_ctx, k_lat], axis=2)
        v_keys = jnp.concatenate([v_ctx, v_b], axis=2)
    k1, k2 = k_keys[..., :B_DH], k_keys[..., B_DH:]
    lam = lam.astype(F32)
    lam_full = jnp.exp(jnp.sum(lam[0] * lam[1])) - jnp.exp(jnp.sum(lam[2] * lam[3])) + lam_init
    o1 = softmax_attend(q1[:, :, None], k1, v_keys)[:, :, 0]
    o2 = softmax_attend(q2[:, :, None], k2, v_keys)[:, :, 0]
    o_b = rms_norm(o1.astype(F32) - lam_full * o2.astype(F32), diff_g) * (1.0 - lam_init)
    mixed = jnp.concatenate([from_heads(o_a), from_heads(o_b)], -1).astype(h.dtype)
    out = jnp.einsum('ble,ed->bld', mixed, w_out)
    if ctx_state is None:
        return out, jnp.stack([s_fw, s_bw], axis=1).astype(h.dtype), k_b, v_b
    return out

def odd_mixer(h, sink, w_in, w_out, ctx_kv=None):
    B, L, _ = h.shape
    p = jnp.einsum('bld,de->ble', h, w_in)
    q, k, v = jnp.split(p, ODD_SPLITS, axis=-1)
    q = q.reshape(B, L, C_KV_HEADS, C_GROUP, C_DH).transpose(0, 2, 3, 1, 4)
    k, v = to_heads(k, C_KV_HEADS), to_heads(v, C_KV_HEADS)
    sink = sink.reshape(C_KV_HEADS, C_GROUP)
    if ctx_kv is None:
        o = softmax_attend(q, k, v, sink)
    else:
        o = window_attend(rope_2d(q), rope_2d(k), v, ctx_kv[0], ctx_kv[1], sink)
    o = o.transpose(0, 3, 1, 2, 4).reshape(B, L, ODD_MIX)
    out = jnp.einsum('ble,ed->bld', o, w_out)
    if ctx_kv is None:
        return out, k, v
    return out

def expert_choice_ffn(h, w_router, w_gate, w_up, w_down):
    B, N, D = h.shape
    cap = (CAP_FACTOR * N) // N_EXPERTS
    aff = jax.nn.softmax(jnp.einsum('bnd,de->bne', h, w_router).astype(F32), axis=-1)
    gates, idx = lax.top_k(jnp.swapaxes(aff, 1, 2), cap)
    bidx = jnp.arange(B)[:, None, None]
    xs = h[bidx, idx]
    hid = jax.nn.silu(jnp.einsum('becd,edf->becf', xs, w_gate)) * jnp.einsum('becd,edf->becf', xs, w_up)
    out = (jnp.einsum('becf,efd->becd', hid, w_down) * gates[..., None]).astype(h.dtype)
    return jnp.zeros_like(h).at[bidx, idx].add(out)

def setup_inputs(seed: int = 0) -> dict:
    key = jax.random.key(seed)
    ks = jax.random.split(key, 32)
    D = D_MODEL

    def nrm(k, shape, s):
        return jax.random.normal(k, shape, F32) * s

    return {
        'x_prompt': nrm(ks[0], (BATCH, SEQ, D), 1.0),
        'x_sample': nrm(ks[1], (DEC_BATCH, DEC_SEQ, D), 1.0),
        'state_hgrn': nrm(ks[2], (DEC_BATCH, N_EVEN, 2, A_HEADS, A_DK, A_DV), 0.5),
        'cache_diff_k': nrm(ks[3], (DEC_BATCH, N_EVEN, B_HEADS, PAST_LEN, 2 * B_DH), 1.0),
        'cache_diff_v': nrm(ks[4], (DEC_BATCH, N_EVEN, B_HEADS, PAST_LEN, B_DV), 1.0),
        'cache_win_k': nrm(ks[5], (DEC_BATCH, N_ODD, C_KV_HEADS, PAST_LEN, C_DH), 1.0),
        'cache_win_v': nrm(ks[6], (DEC_BATCH, N_ODD, C_KV_HEADS, PAST_LEN, C_DH), 1.0),
        'c': nrm(ks[7], (DEC_BATCH, D), 1.0),
        'c_ctx': nrm(ks[8], (D,), 1.0),
        'w_mod': nrm(ks[9], (DEPTH, D, 6 * D), D ** -0.5),
        'b_mod': nrm(ks[10], (DEPTH, 6 * D), 0.01),
        'ln_g': 1.0 + nrm(ks[11], (DEPTH, 2, D), 0.02),
        'ln_b': nrm(ks[12], (DEPTH, 2, D), 0.02),
        'w_in_even': nrm(ks[13], (N_EVEN, D, EVEN_IN), D ** -0.5),
        'w_out_even': nrm(ks[14], (N_EVEN, EVEN_MIX, D), EVEN_MIX ** -0.5 * BETA),
        'hgrn_lb_logits': nrm(ks[15], (DEPTH + 1, A_QK), 0.5),
        'hgrn_norm_g': 1.0 + nrm(ks[16], (N_EVEN, A_DV), 0.02),
        'diff_lambda': nrm(ks[17], (N_EVEN, 4, B_DH), 0.1),
        'diff_norm_g': 1.0 + nrm(ks[18], (N_EVEN, B_DV), 0.02),
        'w_in_odd': nrm(ks[19], (N_ODD, D, ODD_IN), D ** -0.5),
        'w_out_odd': nrm(ks[20], (N_ODD, ODD_MIX, D), ODD_MIX ** -0.5 * BETA),
        'win_sink': nrm(ks[21], (N_ODD, C_HEADS), 0.5),
        'w_router': nrm(ks[22], (DEPTH, D, N_EXPERTS), D ** -0.5),
        'w_exp_gate': nrm(ks[23], (DEPTH, N_EXPERTS, D, EXPERT_FF), D ** -0.5),
        'w_exp_up': nrm(ks[24], (DEPTH, N_EXPERTS, D, EXPERT_FF), D ** -0.5),
        'w_exp_down': nrm(ks[25], (DEPTH, N_EXPERTS, EXPERT_FF, D), EXPERT_FF ** -0.5 * BETA),
    }

def reference(x_prompt, x_sample, state_hgrn, cache_diff_k, cache_diff_v, cache_win_k, cache_win_v,
              c, c_ctx, w_mod, b_mod, ln_g, ln_b, w_in_even, w_out_even, hgrn_lb_logits, hgrn_norm_g,
              diff_lambda, diff_norm_g, w_in_odd, w_out_odd, win_sink, w_router, w_exp_gate, w_exp_up,
              w_exp_down):
    yp, ys = x_prompt, x_sample
    lb_all = jnp.cumsum(jax.nn.softmax(hgrn_lb_logits.astype(F32), axis=0), axis=0)
    st_h, st_dk, st_dv, st_wk, st_wv = [], [], [], [], []
    for l in range(DEPTH):
        mp = modulation(c_ctx[None, :], w_mod[l], b_mod[l])
        ms = modulation(c, w_mod[l], b_mod[l])
        hp = yp * (1 + mp[1]) + mp[0]
        hs = ys * (1 + ms[1]) + ms[0]
        j = l // 2
        if l % 2 == 0:
            lam_init = 0.8 - 0.6 * math.exp(-0.3 * l)
            args = (lb_all[l], hgrn_norm_g[j], diff_lambda[j], lam_init, diff_norm_g[j], w_in_even[j], w_out_even[j])
            out_p, s_ctx, k_ctx, v_ctx = even_mixer(hp, *args)
            out_s = even_mixer(hs, *args, ctx_state=(state_hgrn[:, j], cache_diff_k[:, j], cache_diff_v[:, j]))
            st_h.append(s_ctx)
            st_dk.append(k_ctx)
            st_dv.append(v_ctx)
        else:
            out_p, k_ctx, v_ctx = odd_mixer(hp, win_sink[j], w_in_odd[j], w_out_odd[j])
            out_s = odd_mixer(hs, win_sink[j], w_in_odd[j], w_out_odd[j], ctx_kv=(cache_win_k[:, j], cache_win_v[:, j]))
            st_wk.append(k_ctx)
            st_wv.append(v_ctx)
        yp = layer_norm(ALPHA * yp + mp[2] * out_p, ln_g[l, 0], ln_b[l, 0])
        ys = layer_norm(ALPHA * ys + ms[2] * out_s, ln_g[l, 0], ln_b[l, 0])
        hp = yp * (1 + mp[4]) + mp[3]
        hs = ys * (1 + ms[4]) + ms[3]
        ffp = expert_choice_ffn(hp, w_router[l], w_exp_gate[l], w_exp_up[l], w_exp_down[l])
        ffs = expert_choice_ffn(hs, w_router[l], w_exp_gate[l], w_exp_up[l], w_exp_down[l])
        yp = layer_norm(ALPHA * yp + mp[5] * ffp, ln_g[l, 1], ln_b[l, 1])
        ys = layer_norm(ALPHA * ys + ms[5] * ffs, ln_g[l, 1], ln_b[l, 1])
    new_state_hgrn = jnp.stack(st_h, axis=1)
    new_cache_diff_k = jnp.stack(st_dk, axis=1)
    new_cache_diff_v = jnp.stack(st_dv, axis=1)
    new_cache_win_k = jnp.stack(st_wk, axis=1)
    new_cache_win_v = jnp.stack(st_wv, axis=1)
    return (yp, ys, new_state_hgrn, new_cache_diff_k, new_cache_diff_v, new_cache_win_k, new_cache_win_v)


_drawn_inputs = setup_inputs


def setup_inputs(seed=0):
    import zlib

    import numpy as np

    out = dict(_drawn_inputs(seed))
    spreads = {}
    factors = {'state_hgrn': 8.0,
     'cache_diff_k': 3.508,
     'cache_diff_v': 3.334,
     'cache_win_k': 4.291,
     'cache_win_v': 4.175,
     'b_mod': 3.683,
     'hgrn_norm_g': 68.247,
     'diff_lambda': 8.0,
     'diff_norm_g': 70.023,
     'win_sink': 39.43}
    for name, (base, spread) in spreads.items():
        noise = np.random.default_rng([zlib.crc32(name.encode()), seed]).standard_normal(out[name].shape)
        drawn = base * np.exp(spread * noise) if base else spread * noise
        out[name] = __import__('jax').numpy.asarray(drawn.astype(out[name].dtype))
    for name, factor in factors.items():
        out[name] = (out[name] * factor).astype(out[name].dtype)
    return out
```

```python
from contextlib import ExitStack

import numpy as np

import concourse.bass as bass
import concourse.mybir as mybir

F32 = mybir.dt.float32
I32 = mybir.dt.int32
U32 = mybir.dt.uint32
ALU = mybir.AluOpType
ACT = mybir.ActivationFunctionType
AX = mybir.AxisListType.X

P = 128
D = 1024
KC = D // P
NS, NP_ = 512, 128
NT = NS + NP_
TILES = NT // P
LAT_TILES = NS // P
PAST = 256
DEPTH = 2
HEADS_A = 4
HEADS_B = 4
E = 16
CAP_S, CAP_P = 2 * NS // E, 2 * NP_ // E
SLOTS = CAP_S + CAP_P
FF = 1024
ALPHA = float((2 * DEPTH) ** 0.25)
LN_EPS = 1e-5
LAM_INIT = 0.2
DH = 64
SCALE = DH ** -0.5
NEG = -1e30
UNIT = 256
WSLOTS = 4
SUB = 16
CH = 2 * SUB
GATES = 2 * HEADS_A

ROW_BMOD, ROW_C, ROW_CCTX, ROW_LB, ROW_HG, ROW_DG, N_ROWS = 0, 96, 104, 112, 124, 125, 126
SH1, SC1, GA1, SH2, SC2, GA2 = (8 * j for j in range(6))


class Ctx:

    def __init__(self, nc, stack, dram):
        self.nc, self.stack, self.dram = nc, stack, dram
        self.phase_sems = []
        self.big = stack.enter_context(nc.sbuf_tensor("memory", [P, 53200], F32))
        self.pt = [stack.enter_context(nc.psum_tensor(f"psum{i}", [P, 1024], F32)) for i in range(4)]
        self.RING, self.WST, self.Y, self.H, self.MX, self.MISC = 0, 24576, 32768, 37888, 43008, 48128
        self.ring = [self.at(self.RING + 4096 * s, 4096).rearrange("p (c n) -> p c n", c=KC) for s in range(6)]
        self.wst = [self.at(self.WST + 2048 * s, 2048).rearrange("p (c n) -> p c n", c=KC) for s in range(WSLOTS)]
        self.y = self.at(self.Y, 5120).rearrange("p (t n) -> p t n", t=TILES)
        self.h = self.at(self.H, 5120).rearrange("p (c n) -> p c n", c=KC)
        self.mx = self.at(self.MX, 5120).rearrange("p (c n) -> p c n", c=KC)
        self.ident = self.at(self.MISC, 128)
        self.perm = self.at(self.MISC + 128, 128)
        self.cols = self.at(self.MISC + 256, 126)
        self.mod = [self.at(self.MISC + 384 + 96 * l, 96).rearrange("p (c g) -> p c g", g=2) for l in range(DEPTH)]
        self.scr = self.MISC + 576
        self.w_landed = [self.sem(f"w_landed{s}") for s in range(WSLOTS)]
        self.w_free = self.sem("w_free")
        self.w_seen = 0
        self.r_landed = [self.sem(f"ring_landed{s}") for s in range(6)]
        self.eps = LN_EPS
        self.r_free = self.sem("ring_free")
        self.phase_sems = []

    def at(self, start, size):
        return self.big[:, start:start + size]

    def sem(self, name):
        self.phase_sems.append(self.nc.alloc_semaphore(name))
        return self.phase_sems[-1]

    def clear(self):
        self.nc.all_engine_barrier()
        self.nc.clear_and_free_semaphores(self.phase_sems)
        self.phase_sems = []
        self.nc.all_engine_barrier()

    def bank(self, i):
        return self.pt[i // 2][:, (i % 2) * 512:(i % 2) * 512 + 512]


class Chain:

    def __init__(self, k, engine, name):
        self.sem, self.engine, self.n, self.base = k.sem(name), engine, 0, 0

    def enter(self, i, per):
        self.saved, self.per, self.n0 = self.n, per, self.n
        self.base, self.n = i * per + self.n, 0

    def leave(self, times):
        assert self.n == self.per, (self.n, self.per)
        self.n, self.base = self.saved + times * self.per, 0

    def link(self, instruction):
        instruction.then_inc(self.sem, 1)
        self.n += 1
        self.engine.wait_ge(self.sem, self.base + self.n)


def bcast_rows(ap, offset, dims):
    return bass.AP(tensor=ap.tensor, offset=offset, ap=[[0, P]] + dims)


def w_units(weight, first, count):
    v = weight.rearrange("(c p) (u n) -> u p c n", p=P, n=UNIT)
    return [v[u] for u in range(first, first + count)]


def feed(k, sp, number, source, reader=None):
    if reader:
        sp.wait_ge(*reader)
    sp.dma_start(k.wst[number % WSLOTS], source).then_inc(k.w_landed[number % WSLOTS], 16)


MOD_UNITS = 6 * D // UNIT
N_IN0, N_OUT, N_IN1 = 16, 4, 6
BASE_MOD = [0, MOD_UNITS]
BASE_IN0 = 2 * MOD_UNITS
BASE_OUT0 = BASE_IN0 + N_IN0
BASE_IN1 = BASE_OUT0 + N_OUT
BASE_OUT1 = BASE_IN1 + N_IN1


def phase_modulation(k, a):
    nc = k.nc
    rows = k.at(k.scr, 128)
    brows = k.at(k.scr + 128, 256)
    sc = k.at(k.scr + 384, 16).rearrange("p (c g) -> p c g", g=2)
    consts_in, rows_in, x_in = k.sem("consts_in"), k.sem("rows_in"), k.sem("x_in")
    rows_turned, cols_ready, sc_ready = k.sem("rows_turned"), k.sem("cols_ready"), k.sem("sc_ready")
    mod_ready, mod_turned, brows_ready, brows_out = (
        k.sem(n) for n in ("mod_ready", "mod_turned", "brows_ready", "brows_out"))
    pm = k.bank(0)[:, 0:192].rearrange("p (l i x g) -> p l i x g", l=2, i=MOD_UNITS // WSLOTS, g=2)
    with nc.Block() as block:
        @block.sync
        def _(sp):
            sp.dma_start(k.ident, a["ident"]).then_inc(consts_in, 16)
            sp.dma_start(k.perm, a["perm"]).then_inc(consts_in, 16)
            sp.dma_start(rows[ROW_BMOD:ROW_C], a["b_mod"].rearrange("l (r n) -> (l r) n", n=P)).then_inc(rows_in, 16)
            sp.dma_start(rows[ROW_C:ROW_CCTX], a["c"].rearrange("b (r n) -> (b r) n", n=P)).then_inc(rows_in, 16)
            sp.dma_start(rows[ROW_CCTX:ROW_LB], a["c_ctx"].rearrange("(r n) -> r n", n=P)).then_inc(rows_in, 16)
            sp.dma_start(rows[ROW_LB:ROW_HG],
                         a["hgrn_lb_logits"].rearrange("l (r n) -> (l r) n", n=P)).then_inc(rows_in, 16)
            sp.dma_start(rows[ROW_HG:ROW_DG], a["hgrn_norm_g"]).then_inc(rows_in, 16)
            sp.dma_start(rows[ROW_DG:N_ROWS], a["diff_norm_g"]).then_inc(rows_in, 16)
            per = MOD_UNITS // WSLOTS
            w = [a["w_mod"][l].rearrange("(c p) (u n) -> u p c n", p=P, n=UNIT) for l in range(DEPTH)]
            for s in range(WSLOTS):
                feed(k, sp, s, w[0][s])
            for l in range(DEPTH):
                with sp.Fori(1, per) as i:
                    for s in range(WSLOTS):
                        sp.wait_ge(k.w_free, (i - 1) * WSLOTS + (BASE_MOD[l] + s + 1))
                        sp.dma_start(k.wst[s], w[l][i * WSLOTS + s]).then_inc(k.w_landed[s], 16)
                nxt = w_units(a["w_mod"][1], 0, 4) if l == 0 else in0_units(a)[:4]
                for s in range(WSLOTS):
                    feed(k, sp, BASE_MOD[l] + MOD_UNITS + s, nxt[s], (k.w_free, BASE_MOD[l] + MOD_UNITS - WSLOTS + s + 1))
                if l == 0:
                    for t in range(LAT_TILES):
                        sp.dma_start(k.y[:, t, :], a["x_sample"][0, t * P:(t + 1) * P, :]).then_inc(x_in, 16)
                    sp.dma_start(k.y[:, LAT_TILES, :], a["x_prompt"][0]).then_inc(x_in, 16)
            sp.wait_ge(brows_ready, 1)
            sp.dma_start(k.dram["mod_rows"].rearrange("l r n -> r l n"),
                         brows[0:96, :].rearrange("p (l n) -> p l n", l=2)).then_inc(brows_out, 16)
            sp.wait_ge(brows_out, 16)
            sp.wait_ge(x_in, 16 * TILES)

        @block.tensor
        def _(pe):
            pe.wait_ge(consts_in, 32)
            pe.wait_ge(rows_in, 96)
            nc.tensor.transpose(k.bank(1)[:, 0:N_ROWS], rows[0:N_ROWS, :], k.ident[0:N_ROWS, 0:N_ROWS]).then_inc(rows_turned, 1)
            pe.wait_ge(sc_ready, 1)
            for l in range(DEPTH):
                with pe.Fori(0, MOD_UNITS // WSLOTS) as i:
                    for s in range(WSLOTS):
                        pe.wait_ge(k.w_landed[s], i * 16 + 16 * (BASE_MOD[l] // WSLOTS + 1))
                        for e in range(2):
                            for c in range(KC):
                                last = nc.tensor.matmul(pm[:, l, i, 2 * s + e, :], k.wst[s][:, c, e * P:(e + 1) * P],
                                                        sc[:, c, :], start=(c == 0), stop=(c == KC - 1))
                        last.then_inc(k.w_free, 1)
            pe.wait_ge(mod_ready, 2)
            for l in range(DEPTH):
                last = nc.tensor.transpose(k.bank(2)[0:96, l * P:(l + 1) * P],
                                           k.at(k.MISC + 384 + 96 * l, 96), k.ident)
            last.then_inc(mod_turned, 1)

        @block.scalar
        def _(act):
            act.wait_ge(cols_ready, 1)
            nc.scalar.activation(sc, k.cols[:, ROW_C:ROW_LB].rearrange("p (g c) -> p c g", g=2),
                                 ACT.Silu).then_inc(sc_ready, 1)

        @block.vector
        def _(dve):
            chain = Chain(k, dve, "mod_dve")
            dve.wait_ge(rows_turned, 1)
            nc.vector.tensor_copy(k.cols, k.bank(1)[:, 0:N_ROWS]).then_inc(cols_ready, 1)
            dve.wait_ge(cols_ready, 1)
            dve.wait_ge(k.w_free, 2 * MOD_UNITS)
            for l in range(DEPTH):
                chain.link(nc.vector.tensor_tensor(
                    k.mod[l], k.bank(0)[:, 96 * l:96 * l + 96].rearrange("p (c g) -> p c g", g=2),
                    k.cols[:, 48 * l:48 * l + 48].rearrange("p (c o) -> p c o", o=1).broadcast_to([P, 48, 2]), ALU.add))
                chain.link(nc.vector.tensor_scalar(k.mod[l][:, SC1:SC1 + KC, :], k.mod[l][:, SC1:SC1 + KC, :],
                                                   1.0, None, ALU.add))
                nc.vector.tensor_scalar(k.mod[l][:, SC2:SC2 + KC, :], k.mod[l][:, SC2:SC2 + KC, :],
                                        1.0, None, ALU.add).then_inc(mod_ready, 1)
            dve.wait_ge(mod_turned, 1)
            nc.vector.tensor_copy(brows[0:96, :], k.bank(2)[0:96, 0:256]).then_inc(brows_ready, 1)
    k.w_seen = 2 * MOD_UNITS


def phase_modulate(k, l, shift, scale, tag):
    nc = k.nc
    turned, lat_out, ctx_out = k.sem(f"turned_{tag}"), k.sem(f"lat_out_{tag}"), k.sem(f"ctx_out_{tag}")
    with nc.Block() as block:
        @block.tensor
        def _(pe):
            for c in range(KC):
                if c >= 2:
                    pe.wait_ge(lat_out, c - 1)
                    pe.wait_ge(ctx_out, c - 1)
                for t in range(LAT_TILES):
                    nc.tensor.transpose(k.bank(c % 2)[:, t * P:(t + 1) * P], k.y[:, t, c * P:(c + 1) * P], k.ident)
                nc.tensor.transpose(k.bank(2 + c % 2)[:, 0:P], k.y[:, LAT_TILES, c * P:(c + 1) * P],
                                    k.ident).then_inc(turned, 1)

        @block.scalar
        def _(act):
            for c in range(KC):
                act.wait_ge(turned, c + 1)
                nc.scalar.activation(k.h[:, c, 0:NS], k.bank(c % 2), ACT.Identity,
                                     scale=k.mod[l][:, scale + c, 0:1], bias=k.mod[l][:, shift + c, 0:1]).then_inc(lat_out, 1)

        @block.vector
        def _(dve):
            for c in range(KC):
                dve.wait_ge(turned, c + 1)
                nc.vector.tensor_scalar(k.h[:, c, NS:NT], k.bank(2 + c % 2)[:, 0:P], k.mod[l][:, scale + c, 1:2],
                                        k.mod[l][:, shift + c, 1:2], ALU.mult, ALU.add).then_inc(ctx_out, 1)


IN0_ORDER = [0, 1, 2, 3, 4, 5, 8, 9, 10, 11, 12, 13, 6, 7, 14, 15]
CQ, CFF, CFB, CG, CQB, CKB = 0, 4, 8, 12, 16, 20


def in0_units(a):
    v = a["w_in_even"][0].rearrange("(c p) (u n) -> u p c n", p=P, n=UNIT)
    return [v[u] for u in IN0_ORDER]


def in1_units(a):
    return w_units(a["w_in_odd"][0], 0, N_IN1)


def project_feature_major(k, pe, w_slot, e, bank_lat, bank_ctx):
    nc = k.nc
    for c in range(KC):
        w = k.wst[w_slot][:, c, e * P:(e + 1) * P]
        nc.tensor.matmul(bank_lat, w, k.h[:, c, 0:NS], start=(c == 0), stop=(c == KC - 1))
        last = nc.tensor.matmul(bank_ctx, w, k.h[:, c, NS:NT], start=(c == 0), stop=(c == KC - 1))
    return last


def phase_project_even(k, a):
    nc = k.nc
    proj = k.at(k.RING, 24 * NT).rearrange("p (c n) -> p c n", n=NT)
    va = k.at(15360, 2560).rearrange("p (t n) -> p t n", t=TILES)
    vb = k.at(17920, 2560).rearrange("p (t n) -> p t n", t=TILES)
    kout = k.at(20480, 512)
    done, lat_out, ctx_out = k.sem("proj_done"), k.sem("proj_lat_out"), k.sem("proj_ctx_out")
    tok_done, tok_out, k_turned, kout_ready, stored = (
        k.sem(n) for n in ("ptok_done", "ptok_out", "k_turned", "kout_ready", "kv_stored"))
    b16 = BASE_IN0 // WSLOTS
    with nc.Block() as block:
        @block.sync
        def _(sp):
            src = in0_units(a)
            for u in range(WSLOTS, N_IN0):
                feed(k, sp, BASE_IN0 + u, src[u], (done, 2 * (u - WSLOTS) + 2))
            for u, s in enumerate(w_units(a["w_out_even"][0], 0, 4)):
                feed(k, sp, BASE_OUT0 + u, s, (tok_done, TILES * (u + 1)))
            sp.wait_ge(tok_out, 4 * TILES)
            sp.dma_start(a["out_diff_v"].rearrange("h t d -> t h d"),
                         vb[:, LAT_TILES, :].rearrange("p (h d) -> p h d", h=HEADS_B)).then_inc(stored, 16)
            sp.wait_ge(kout_ready, 1)
            sp.dma_start(a["out_diff_k"].rearrange("h t d -> t h d"),
                         kout.rearrange("p (h d) -> p h d", h=HEADS_B)).then_inc(stored, 16)
            sp.wait_ge(stored, 32)

        @block.tensor
        def _(pe):
            with pe.Fori(0, 3) as i:
                for s in range(WSLOTS):
                    pe.wait_ge(k.w_landed[s], i * 16 + 16 * (b16 + 1))
                    for e in range(2):
                        q = 2 * s + e
                        pe.wait_ge(lat_out, i * 8 + max(q - 1, 0))
                        pe.wait_ge(ctx_out, i * 8 + max(q - 1, 0))
                        last = project_feature_major(k, pe, s, e, k.bank(e), k.bank(2 + e)[:, 0:P])
                        last.then_inc(done, 1)
            for s in range(WSLOTS):
                pe.wait_ge(k.w_landed[s], 16 * (b16 + 4))
                for t in range(TILES):
                    g = s * TILES + t
                    if g >= 2:
                        pe.wait_ge(tok_out, g - 1)
                    for c in range(KC):
                        last = nc.tensor.matmul(k.bank(4 + g % 2)[:, 0:UNIT], k.h[:, c, t * P:(t + 1) * P],
                                                k.wst[s][:, c, :], start=(c == 0), stop=(c == KC - 1))
                    last.then_inc(tok_done, 1)
            pe.wait_ge(ctx_out, 24)
            for hd in range(HEADS_B):
                last = nc.tensor.transpose(k.bank(6)[:, hd * P:(hd + 1) * P], proj[:, CKB + hd, NS:NT], k.ident)
            last.then_inc(k_turned, 1)

        @block.scalar
        def _(act):
            with act.Fori(0, 3) as i:
                for q in range(8):
                    act.wait_ge(done, i * 8 + q + 1)
                    nc.scalar.copy(proj[:, i * 8 + q, 0:NS], k.bank(q % 2)).then_inc(lat_out, 1)

        @block.vector
        def _(dve):
            with dve.Fori(0, 3) as i:
                for q in range(8):
                    dve.wait_ge(done, i * 8 + q + 1)
                    nc.vector.tensor_copy(proj[:, i * 8 + q, NS:NT], k.bank(2 + q % 2)[:, 0:P]).then_inc(ctx_out, 1)
            for s in range(WSLOTS):
                for t in range(TILES):
                    g = s * TILES + t
                    dve.wait_ge(tok_done, g + 1)
                    dst = va if s < 2 else vb
                    nc.vector.tensor_copy(dst[:, t, (s % 2) * UNIT:(s % 2 + 1) * UNIT],
                                          k.bank(4 + g % 2)[:, 0:UNIT]).then_inc(tok_out, 1)
            dve.wait_ge(k_turned, 1)
            nc.vector.tensor_copy(kout, k.bank(6)).then_inc(kout_ready, 1)


def phase_hgrn(k, a):
    nc = k.nc
    proj = k.at(k.RING, 24 * NT).rearrange("p (c n) -> p c n", n=NT)
    va = k.at(15360, 2560).rearrange("p (t h n) -> p t h n", t=TILES, h=HEADS_A)
    NB = NT // CH

    class Dir:
        pass
    dirs = []
    for d, base in enumerate((k.H, 20480)):
        x = Dir()
        x.e, x.key, x.b, x.kdec, x.kend, x.qdec = (k.at(base + NT * j, NT) for j in range(6))
        x.qi, x.kh = x.key, x.b
        x.a = k.at(base + 6 * NT, NB)
        x.A, x.B = (0, 1) if d == 0 else (1, 0)
        x.end = SUB - 1 if d == 0 else 0
        x.tiles = [0, 1, 2, 3, 4] if d == 0 else [3, 2, 1, 0, 4]
        x.steps = [0, 1, 2, 3] if d == 0 else [3, 2, 1, 0]
        x.S = k.at(k.MX + 2560 + 1024 * d, 1024).rearrange("p (s n) -> p s n", s=8)
        x.S0 = k.at(k.MX + 2560 + 2048 + P * d, P)
        dirs.append(x)
    zero = k.at(k.MX + 2560 + 2304, P)
    ones = k.at(k.MX + 2560 + 2432, P)
    sig_g = k.at(k.H + 3860, NT)
    sc0 = k.scr
    keep = k.at(sc0, 641)
    masks = k.at(sc0 + 644, 384).bitcast(I32).rearrange("p (d n) -> p d n", d=2)
    vh = k.at(sc0 + 1028, NT).rearrange("p (t n) -> p t n", t=TILES)
    vblk = k.at(sc0 + 1668, 1024).rearrange("p (b j n) -> p b j n", b=2, j=4)
    scm = k.at(sc0 + 2692, 384).rearrange("p (b n) -> p b n", b=2)
    khT = k.at(sc0 + 3076, 256).rearrange("p (b n) -> p b n", b=2)
    bmask = k.at(sc0 + 3332, 4)
    lbx = k.at(sc0 + 3336, 12).rearrange("p (l h) -> p l h", h=4)
    lbm = k.at(sc0 + 3348, 4)
    lb, oml, lbs = k.at(sc0 + 3352, 4), k.at(sc0 + 3356, 4), k.at(sc0 + 3360, 4)
    lbe = k.at(sc0 + 3364, 12).rearrange("p (l h) -> p l h", h=4)

    names = ("h_const", "h_s0", "h_lbsub", "h_lbexp", "h_lb", "h_sig", "h_f", "h_ln", "h_scan", "h_exp", "h_sub",
             "h_kexp", "h_gates", "h_vh", "h_vblk", "h_sc", "h_and", "h_kt", "h_kht", "h_u", "h_upd", "h_pv",
             "h_inter", "h_state_out", "h_sq", "h_ms", "h_rstd", "h_fin", "h_zero")
    S = {n[2:]: k.sem(n) for n in names}
    STEPS = 2 * TILES

    def halves(ap):
        return ap.rearrange("p (c h t) -> p c h t", h=2, t=SUB)

    def step(s):
        d = dirs[s % 2]
        return d, s % 2, s // 2, d.tiles[s // 2]

    def state_before(d, n, j):
        if j:
            return d.S[:, 4 * (n % 2) + j - 1, :]
        if n == 0:
            return d.S0
        if n == LAT_TILES:
            return zero
        return d.S[:, 4 * ((n - 1) % 2) + 3, :]

    with nc.Block() as block:
        @block.sync
        def _(sp):
            sp.dma_start(keep, a["keep"]).then_inc(S["const"], 16)
            sp.dma_start(masks, a["hgrn_masks"]).then_inc(S["const"], 16)
            sp.dma_start(bmask, a["bmask"]).then_inc(S["const"], 16)
            with sp.Fori(0, HEADS_A) as i:
                sp.wait_ge(S["inter"], STEPS * i)
                for d in range(2):
                    sp.dma_start(dirs[d].S0, a["state_hgrn"][0, 0, d, i]).then_inc(S["s0"], 16)
                sp.wait_ge(S["upd"], STEPS * i + STEPS)
                for d in range(2):
                    sp.dma_start(a["out_state"][d, i], dirs[d].S[:, 3, :]).then_inc(S["state_out"], 16)
            sp.wait_ge(S["state_out"], 32 * HEADS_A)

        @block.gpsimd
        def _(pool):
            nc.gpsimd.memset(zero, 0.0).then_inc(S["zero"], 1)
            nc.gpsimd.memset(ones, 1.0 / P).then_inc(S["zero"], 1)
            pool.wait_ge(S["const"], 48)
            with pool.Fori(0, HEADS_A) as i:
                pool.wait_ge(S["inter"], STEPS * i)
                nc.gpsimd.tensor_copy(vh, va[:, :, i, :]).then_inc(S["vh"], 1)
                pool.wait_ge(S["vh"], i + 1)
                for s in range(STEPS):
                    _, _, _, t = step(s)
                    pool.wait_ge(S["u"], STEPS * i + max(s - 1, 0))
                    nc.gpsimd.tensor_tensor(
                        vblk[:, s % 2], vh[:, t, :].rearrange("p (o n) -> p o n", o=1).broadcast_to([P, 4, P]),
                        bmask.rearrange("p (j o) -> p j o", o=1).broadcast_to([P, 4, P]), ALU.mult).then_inc(S["vblk"], 1)

        @block.scalar
        def _(act):
            act.wait_ge(S["lbsub"], 1)
            nc.scalar.activation(lbe, lbx, ACT.Exp).then_inc(S["lbexp"], 1)
            with act.Fori(0, HEADS_A) as i:
                act.wait_ge(S["fin"], i)
                for d, x in enumerate(dirs):
                    z = proj[:, (CFF, CFB)[d] + i, :]
                    nc.scalar.activation(x.e, z, ACT.Sigmoid).then_inc(S["sig"], 1)
                    nc.scalar.activation(x.key, z, ACT.Sigmoid, scale=-1.0).then_inc(S["sig"], 1)
                nc.scalar.activation(sig_g, proj[:, CG + i, :], ACT.Sigmoid).then_inc(S["sig"], 1)
                for d, x in enumerate(dirs):
                    act.wait_ge(S["f"], 2 * i + d + 1)
                    nc.scalar.activation(x.e, x.e, ACT.Ln).then_inc(S["ln"], 1)
                for d, x in enumerate(dirs):
                    act.wait_ge(S["scan"], 2 * i + d + 1)
                    nc.scalar.activation(x.e, x.b, ACT.Exp).then_inc(S["exp"], 1)
                    nc.scalar.activation(x.kdec, x.b, ACT.Exp, scale=-1.0).then_inc(S["exp"], 1)
                    act.wait_ge(S["sub"], 2 * i + d + 1)
                    nc.scalar.activation(x.kend, x.kend, ACT.Exp).then_inc(S["kexp"], 1)
                for s in range(STEPS):
                    act.wait_ge(S["kt"], STEPS * i + s + 1)
                    act.wait_ge(S["u"], STEPS * i + max(s - 1, 0))
                    nc.scalar.copy(khT[:, s % 2, :], k.bank(4 + s % 2)[:, 0:P]).then_inc(S["kht"], 1)
                act.wait_ge(S["inter"], STEPS * i + STEPS)
                ob, sq = dirs[0].e, dirs[1].e
                nc.scalar.copy(ob[:, 0:NS], k.bank(0))
                nc.scalar.copy(ob[:, NS:NT], k.bank(1)[:, 0:P])
                nc.scalar.activation(sq[:, 0:NS], k.bank(0), ACT.Square)
                nc.scalar.activation(sq[:, NS:NT], k.bank(1)[:, 0:P], ACT.Square).then_inc(S["sq"], 1)
                act.wait_ge(S["ms"], i + 1)
                act.wait_ge(S["sq"], i + 1)
                rs = dirs[1].qdec
                nc.scalar.activation(rs[:, 0:NS], k.bank(2), ACT.Ln, bias=k.eps).then_inc(S["rstd"], 1)
                nc.scalar.activation(rs[:, NS:NT], k.bank(3)[:, 0:P], ACT.Ln, bias=k.eps).then_inc(S["rstd"], 1)
                act.wait_ge(S["rstd"], 3 * i + 2)
                nc.scalar.activation(rs, rs, ACT.Exp, scale=-0.5).then_inc(S["rstd"], 1)

        @block.vector
        def _(dve):
            c = Chain(k, dve, "hgrn_dve")
            lg = k.cols[:, ROW_LB:ROW_HG].rearrange("p (l h) -> p l h", h=4)
            c.link(nc.vector.tensor_tensor(lbm, lg[:, 0, :], lg[:, 1, :], ALU.max))
            c.link(nc.vector.tensor_tensor(lbm, lbm, lg[:, 2, :], ALU.max))
            for r in range(3):
                last = nc.vector.tensor_tensor(lbx[:, r, :], lg[:, r, :], lbm, ALU.subtract)
            last.then_inc(S["lbsub"], 1)
            dve.wait_ge(S["lbexp"], 1)
            c.link(nc.vector.tensor_tensor(lbs, lbe[:, 0, :], lbe[:, 1, :], ALU.add))
            c.link(nc.vector.tensor_tensor(lbs, lbs, lbe[:, 2, :], ALU.add))
            c.link(nc.vector.reciprocal(lbs, lbs))
            c.link(nc.vector.tensor_tensor(lb, lbe[:, 0, :], lbs, ALU.mult))
            c.link(nc.vector.tensor_scalar(oml, lb, -1.0, 1.0, ALU.mult, ALU.add))
            dve.wait_ge(S["const"], 48)
            dve.wait_ge(S["zero"], 2)
            with dve.Fori(0, HEADS_A) as i:
                c.enter(i, 3 * STEPS + 4)
                for d, x in enumerate(dirs):
                    dve.wait_ge(S["sig"], 5 * i + 2 * d + 2)
                    nc.vector.tensor_scalar(x.e, x.e, oml[:, bass.ds(i, 1)], lb[:, bass.ds(i, 1)], ALU.mult, ALU.add).then_inc(S["f"], 1)
                    nc.vector.tensor_scalar(x.key, x.key, oml[:, bass.ds(i, 1)], None, ALU.mult)
                for d, x in enumerate(dirs):
                    dve.wait_ge(S["ln"], 2 * i + d + 1)
                    if d == 0:
                        op = nc.vector.tensor_tensor_scan(x.b, keep[:, 0:NT], x.e, 0.0, ALU.mult, ALU.add)
                    else:
                        op = nc.vector.tensor_tensor_scan(x.b[:, ::-1], keep[:, 1:NT + 1][:, ::-1], x.e[:, ::-1],
                                                          0.0, ALU.mult, ALU.add)
                    op.then_inc(S["scan"], 1)
                    dve.wait_ge(S["scan"], 2 * i + d + 1)
                    b3 = x.b.rearrange("p (c t) -> p c t", t=SUB)
                    nc.vector.tensor_tensor(x.kend.rearrange("p (c t) -> p c t", t=SUB),
                                            b3[:, :, x.end:x.end + 1].broadcast_to([P, NT // SUB, SUB]), b3,
                                            ALU.subtract).then_inc(S["sub"], 1)
                for d, x in enumerate(dirs):
                    dve.wait_ge(S["exp"], 4 * i + 2 * d + 2)
                    nc.vector.tensor_tensor(x.qdec, proj[:, CQ + i, :], x.e, ALU.mult)
                    nc.vector.tensor_tensor(x.kdec, x.kdec, x.key, ALU.mult)
                    dve.wait_ge(S["kexp"], 2 * i + d + 1)
                    c.link(nc.vector.tensor_tensor(x.kend, x.kend, x.key, ALU.mult))
                    e4, q4, qi4, ke4, kh4 = (halves(v) for v in (x.e, x.qdec, x.qi, x.kend, x.kh))
                    endA = e4[:, :, x.A, x.end:x.end + 1]
                    endB = e4[:, :, x.B, x.end:x.end + 1]
                    nc.vector.tensor_copy(qi4[:, :, x.A, :], q4[:, :, x.A, :])
                    nc.vector.tensor_tensor(qi4[:, :, x.B, :], q4[:, :, x.B, :], endA.broadcast_to([P, NB, SUB]), ALU.mult)
                    nc.vector.tensor_copy(kh4[:, :, x.B, :], ke4[:, :, x.B, :])
                    nc.vector.tensor_tensor(kh4[:, :, x.A, :], ke4[:, :, x.A, :], endB.broadcast_to([P, NB, SUB]), ALU.mult)
                    nc.vector.tensor_tensor(x.a.rearrange("p (c o) -> p c o", o=1), endA, endB,
                                            ALU.mult).then_inc(S["gates"], 1)
                dve.wait_ge(S["s0"], 32 * i + 32)
                dve.wait_ge(S["state_out"], 32 * i)
                dve.wait_ge(S["gates"], 2 * i + 2)
                for s in range(STEPS):
                    x, dn, n, t = step(s)
                    dve.wait_ge(S["sc"], STEPS * i + s + 1)
                    dve.wait_ge(S["pv"], STEPS * i + max(s - 1, 0))
                    nc.vector.tensor_tensor(scm[:, s % 2, :].bitcast(I32), k.bank(2 + s % 2)[:, 0:192].bitcast(I32),
                                            masks[:, dn, :], ALU.bitwise_and).then_inc(S["and"], 1)
                    dve.wait_ge(S["u"], STEPS * i + s + 1)
                    dve.wait_ge(S["inter"], STEPS * i + max(s - 3, 0))
                    for j, m in enumerate(x.steps):
                        op = nc.vector.scalar_tensor_tensor(
                            out=x.S[:, 4 * (n % 2) + j, :], in0=state_before(x, n, j),
                            scalar=x.a[:, 4 * t + m:4 * t + m + 1], in1=k.bank(6 + s % 2)[:, m * P:(m + 1) * P],
                            op0=ALU.mult, op1=ALU.add)
                        if j == 3:
                            op.then_inc(S["upd"], 1)
                            dve.wait_ge(S["upd"], STEPS * i + s + 1)
                        else:
                            c.link(op)
                ob, rs = dirs[0].e, dirs[1].qdec
                dve.wait_ge(S["rstd"], 3 * i + 3)
                dve.wait_ge(S["sq"], i + 1)
                dve.wait_ge(S["sig"], 5 * i + 5)
                c.link(nc.vector.scalar_tensor_tensor(out=ob, in0=ob, scalar=k.cols[:, ROW_HG:ROW_HG + 1], in1=rs,
                                                      op0=ALU.mult, op1=ALU.mult))
                c.link(nc.vector.tensor_tensor(ob, ob, sig_g, ALU.mult))
                nc.vector.tensor_tensor(k.mx[:, i, :], ob, proj[:, CG + i, :], ALU.mult).then_inc(S["fin"], 1)
                c.leave(HEADS_A)

        @block.tensor
        def _(pe):
            pe.wait_ge(S["zero"], 2)
            with pe.Fori(0, HEADS_A) as i:
                def before(s):
                    x, dn, n, t = step(s)
                    tile = slice(t * P, (t + 1) * P)
                    if s < 2:
                        pe.wait_ge(S["gates"], 2 * i + s + 1)
                    pe.wait_ge(S["and"], STEPS * i + max(s - 1, 0))
                    nc.tensor.matmul(k.bank(2 + s % 2)[:, 0:P], x.kdec[:, tile], x.qdec[:, tile], start=True, stop=True)
                    qB = halves(x.qdec)[:, 4 * t:4 * t + 4, x.B, :]
                    nc.tensor.matmul(k.bank(2 + s % 2)[:, P:192], x.kend[:, tile], qB,
                                     start=True, stop=True).then_inc(S["sc"], 1)
                    pe.wait_ge(S["kht"], STEPS * i + max(s - 1, 0))
                    nc.tensor.transpose(k.bank(4 + s % 2)[:, 0:P], x.kh[:, tile], k.ident).then_inc(S["kt"], 1)

                def after(s):
                    x, dn, n, t = step(s)
                    pe.wait_ge(S["kht"], STEPS * i + s + 1)
                    pe.wait_ge(S["vblk"], STEPS * i + s + 1)
                    pe.wait_ge(S["upd"], STEPS * i + max(s - 1, 0))
                    nc.tensor.matmul(k.bank(6 + s % 2), khT[:, s % 2, :], vblk[:, s % 2].rearrange("p j n -> p (j n)"),
                                     start=True, stop=True).then_inc(S["u"], 1)
                    pe.wait_ge(S["and"], STEPS * i + s + 1)
                    o = k.bank(0) if t < LAT_TILES else k.bank(1)[:, 0:P]
                    c0 = t * P if t < LAT_TILES else 0
                    nc.tensor.matmul(o[:, c0:c0 + P], vh[:, t, :], scm[:, s % 2, 0:P], start=(s in (0, 8)), stop=False,
                                     skip_group_check=True)
                    oB = o[:, c0:c0 + P].rearrange("p (c h t) -> p c h t", h=2, t=SUB)[:, :, x.B, :]
                    nc.tensor.matmul(oB, vh[:, t, :], scm[:, s % 2, P:192], start=False, stop=False,
                                     skip_group_check=True).then_inc(S["pv"], 1)
                    pe.wait_ge(S["upd"], STEPS * i + s + 1)
                    for j, m in enumerate(x.steps):
                        cols = slice(t * P + m * CH, t * P + (m + 1) * CH)
                        last = nc.tensor.matmul(o[:, c0 + m * CH:c0 + (m + 1) * CH], state_before(x, n, j), x.qi[:, cols],
                                                start=False, stop=(s >= STEPS - 3 and j == 3), skip_group_check=True)
                    last.then_inc(S["inter"], 1)

                pe.wait_ge(S["fin"], i)
                pe.wait_ge(S["rstd"], 3 * i)
                before(0)
                pe.wait_ge(S["vh"], i + 1)
                for s in range(STEPS):
                    if s + 1 < STEPS:
                        before(s + 1)
                    after(s)
                pe.wait_ge(S["sq"], i + 1)
                sq = dirs[1].e
                nc.tensor.matmul(k.bank(2), ones, sq[:, 0:NS], start=True, stop=True)
                nc.tensor.matmul(k.bank(3)[:, 0:P], ones, sq[:, NS:NT], start=True, stop=True).then_inc(S["ms"], 1)


def phase_project_odd(k, a):
    nc = k.nc
    proj = k.at(k.RING, 10 * NT).rearrange("p (c n) -> p c n", n=NT)
    v = k.at(6400, 1280).rearrange("p (t n) -> p t n", t=TILES)
    kout = k.at(7680, 256)
    done, lat_out, ctx_out = k.sem("oproj_done"), k.sem("oproj_lat_out"), k.sem("oproj_ctx_out")
    tok_done, tok_out, k_turned, kout_ready, stored = (
        k.sem(n) for n in ("otok_done", "otok_out", "ok_turned", "okout_ready", "okv_stored"))
    with nc.Block() as block:
        @block.sync
        def _(sp):
            for u, s in enumerate(in1_units(a)):
                if u >= WSLOTS:
                    feed(k, sp, BASE_IN1 + u, s, (done, 2 * (u - WSLOTS) + 2))
            for u, s in enumerate(w_units(a["w_out_odd"][0], 0, 4)):
                feed(k, sp, BASE_OUT1 + u, s, (done, 2 * (u + 2) + 2) if u < 3 else (tok_done, TILES))
            sp.wait_ge(tok_out, TILES)
            sp.dma_start(a["out_win_v"].rearrange("h t d -> t h d"),
                         v[:, LAT_TILES, :].rearrange("p (h d) -> p h d", h=4)).then_inc(stored, 16)
            sp.wait_ge(kout_ready, 1)
            sp.dma_start(a["out_win_k"].rearrange("h t d -> t h d"),
                         kout.rearrange("p (h d) -> p h d", h=4)).then_inc(stored, 16)
            sp.wait_ge(stored, 32)

        @block.tensor
        def _(pe):
            for u in range(N_IN1):
                n = BASE_IN1 + u
                pe.wait_ge(k.w_landed[n % WSLOTS], 16 * (n // WSLOTS + 1))
                if u < 5:
                    for e in range(2):
                        q = 2 * u + e
                        if q >= 2:
                            pe.wait_ge(lat_out, q - 1)
                            pe.wait_ge(ctx_out, q - 1)
                        last = project_feature_major(k, pe, n % WSLOTS, e, k.bank(e), k.bank(2 + e)[:, 0:P])
                        last.then_inc(done, 1)
                else:
                    for t in range(TILES):
                        if t >= 2:
                            pe.wait_ge(tok_out, t - 1)
                        for c in range(KC):
                            last = nc.tensor.matmul(k.bank(4 + t % 2)[:, 0:UNIT], k.h[:, c, t * P:(t + 1) * P],
                                                    k.wst[n % WSLOTS][:, c, :], start=(c == 0), stop=(c == KC - 1))
                        last.then_inc(tok_done, 1)
            pe.wait_ge(ctx_out, 10)
            for c in range(2):
                last = nc.tensor.transpose(k.bank(6)[:, c * P:(c + 1) * P], proj[:, 8 + c, NS:NT], k.ident)
            last.then_inc(k_turned, 1)

        @block.scalar
        def _(act):
            for q in range(10):
                act.wait_ge(done, q + 1)
                nc.scalar.copy(proj[:, q, 0:NS], k.bank(q % 2)).then_inc(lat_out, 1)

        @block.vector
        def _(dve):
            for q in range(10):
                dve.wait_ge(done, q + 1)
                nc.vector.tensor_copy(proj[:, q, NS:NT], k.bank(2 + q % 2)[:, 0:P]).then_inc(ctx_out, 1)
            for t in range(TILES):
                dve.wait_ge(tok_done, t + 1)
                nc.vector.tensor_copy(v[:, t, :], k.bank(4 + t % 2)[:, 0:UNIT]).then_inc(tok_out, 1)
            dve.wait_ge(k_turned, 1)
            nc.vector.tensor_copy(kout, k.bank(6)[:, 0:UNIT]).then_inc(kout_ready, 1)


def phase_rope(k, a, odd):
    nc = k.nc
    tag = "o" if odd else "e"
    proj = k.at(k.RING, (10 if odd else 24) * NT).rearrange("p (c n) -> p c n", n=NT)
    first, count = (0, 10) if odd else (CQB, 8)
    nk = 2 if odd else 4
    cos, sin = k.at(k.scr, 512), k.at(k.scr + 512, 512)
    straight = k.at(k.H, 1024).rearrange("p (b n) -> p b n", b=2)
    kctx = k.at(k.H + 1024, 1024).rearrange("p (c n) -> p c n", n=PAST)
    kraw = k.at(20480, 2 * nk * P).rearrange("p (c t n) -> p c t n", t=2, n=P)
    loaded, kraw_in, turned, swapped, mixed, multiplied, summed, kctx_out = (
        k.sem(f"rope_{n}_{tag}") for n in ("loaded", "kraw_in", "turned", "swapped", "mixed", "multiplied", "summed",
                                           "kctx_out"))
    with nc.Block() as block:
        @block.sync
        def _(sp):
            sp.dma_start(cos, a["cos"]).then_inc(loaded, 16)
            sp.dma_start(sin, a["sin"]).then_inc(loaded, 16)
            for c in range(nk):
                for t in range(2):
                    if odd:
                        src = a["cache_win_k"][0, 0, 2 * c:2 * c + 2, t * P:(t + 1) * P, :].rearrange("h t d -> t h d")
                        dst = kraw[:, c, t, :].rearrange("p (h d) -> p h d", h=2)
                    else:
                        src, dst = a["cache_diff_k"][0, 0, c, t * P:(t + 1) * P, :], kraw[:, c, t, :]
                    sp.dma_start(dst, src).then_inc(kraw_in, 16)

        @block.tensor
        def _(pe):
            with pe.Fori(0, count // 2) as i:
                for b in range(2):
                    pe.wait_ge(multiplied, 2 * i + 0)
                    nc.tensor.matmul(k.bank(b), k.perm, proj[:, first + i * 2 + b, 0:NS],
                                     start=True, stop=True).then_inc(swapped, 1)
            pe.wait_ge(kraw_in, 32 * nk)
            for c in range(nk):
                for t in range(2):
                    last = nc.tensor.transpose(k.bank(4 + c // 2)[:, (c % 2) * PAST + t * P:(c % 2) * PAST + (t + 1) * P],
                                               kraw[:, c, t, :], k.ident)
            last.then_inc(turned, 1)

        @block.gpsimd
        def _(pool):
            pool.wait_ge(loaded, 32)
            with pool.Fori(0, count // 2) as i:
                for b in range(2):
                    pool.wait_ge(summed, 2 * i)
                    nc.gpsimd.tensor_tensor(straight[:, b, :], proj[:, first + i * 2 + b, 0:NS], cos,
                                            ALU.mult).then_inc(mixed, 1)

        @block.vector
        def _(dve):
            dve.wait_ge(loaded, 32)
            with dve.Fori(0, count // 2) as i:
                for b in range(2):
                    x = proj[:, first + i * 2 + b, 0:NS]
                    dve.wait_ge(swapped, 2 * i + b + 1)
                    dve.wait_ge(mixed, 2 * i + b + 1)
                    nc.vector.tensor_tensor(x, k.bank(b), sin, ALU.mult).then_inc(multiplied, 1)
                    dve.wait_ge(multiplied, 2 * i + b + 1)
                    nc.vector.tensor_tensor(x, x, straight[:, b, :], ALU.add).then_inc(summed, 1)
            dve.wait_ge(turned, 1)
            for c in range(nk):
                nc.vector.tensor_copy(kctx[:, c, :], k.bank(4 + c // 2)[:, (c % 2) * PAST:(c % 2 + 1) * PAST])


def phase_attention(k, a, odd):
    nc = k.nc
    tag = "o" if odd else "e"
    ITER = 8 if odd else HEADS_B
    proj = k.at(k.RING, (10 if odd else 24) * NT).rearrange("p (c n) -> p c n", n=NT)
    kctx = k.at(k.H + 1024, 1024).rearrange("p (c n) -> p c n", n=PAST)
    qr = k.at(k.H + 2048, 2 * NT).rearrange("p (b n) -> p b n", b=2)
    free = 10240 if odd else 0
    kr = k.at(free, 2 * NT).rearrange("p (b n) -> p b n", b=2)
    kcr = k.at(free + 2 * NT, 2 * PAST).rearrange("p (b n) -> p b n", b=2)
    ob = k.at(k.H + 3328, NT).rearrange("p (t n) -> p t n", t=TILES)
    small = k.H + 3968
    negm = k.at(small, 10)
    rsum = k.at(small + 10, 10)
    rinv = k.at(small + 20, 10)
    top = k.at(small + 30, 10)
    esink = k.at(small + 40, 10)
    ssq = k.at(small + 50, 5)
    rstd = k.at(small + 55, 5)
    neglam = k.at(small + 60, 1)
    dots = k.at(small + 61, 2)
    gdiff = k.at(small + 63, 1)
    lamx = k.at(small + 64, 256).rearrange("p (j n) -> p j n", j=4)
    sink = k.at(small + 320, 16)
    t2 = k.at(small + 336, P)
    junk = k.at(small + 464, P)
    tick = k.at(small + 592, 1)
    sinkc = k.at(small + 594, 4).rearrange("p (b n) -> p b n", b=2)
    prob = k.at(k.scr + 1024, 1536).rearrange("p (b n) -> p b n", b=2)
    probT = k.at(k.scr + 2560, 1536).rearrange("p (b n) -> p b n", b=2)
    if odd:
        vlat = k.at(6400, 1280).rearrange("p (t h n) -> p t h n", t=TILES, h=4)
        vctx = k.at(8192, 512).rearrange("p (t h n) -> p t h n", t=2, h=4)
        mask = k.at(8704, 768)
    else:
        vlat = k.at(17920, 2560).rearrange("p (t h n) -> p t h n", t=TILES, h=4)
        vctx = k.at(20480, 1024).rearrange("p (t h n) -> p t h n", t=2, h=4)
    S = {n: k.sem(f"at_{n}_{tag}") for n in ("v_in", "dots", "lam", "lam_ready", "q_in", "qk", "max", "small", "exp", "esink",
                                             "pt", "outd", "outa", "pv", "comb", "fold", "ssq", "rstd", "norm", "turned", "stored")}
    UN = 2 * TILES
    QIN = 4 if odd else 3

    def unit(u):
        t, m = divmod(u, 2)
        if t == LAT_TILES:
            return (t, m, 256, 384) if odd else (t, m, 0, P)
        if odd:
            return t, m, (128 if t else 256), (768 if t < LAT_TILES - 1 else 640)
        return t, m, 0, 768

    def key_tiles(t):
        if t == LAT_TILES:
            return [("own", LAT_TILES)]
        if not odd:
            return [("ctx", 0), ("ctx", 1)] + [("own", j) for j in range(LAT_TILES)]
        return ([("own", t - 1)] if t else []) + [("ctx", 0), ("ctx", 1), ("own", t)] + (
            [("own", t + 1)] if t < LAT_TILES - 1 else [])

    def split(u):
        t, m, lo, hi = unit(u)
        n = (hi - lo) // P
        return n, max(n // 2, 1)

    def outa(i, u):
        return i * (UN - 2) + min(u, UN - 2)

    with nc.Block() as block:
        @block.sync
        def _(sp):
            for t in range(2):
                src = a["cache_win_v" if odd else "cache_diff_v"][0, 0, :, t * P:(t + 1) * P, :].rearrange("h t d -> t h d")
                sp.dma_start(vctx[:, t], src).then_inc(S["v_in"], 16)
            if odd:
                sp.dma_start(sink, bcast_rows(a["win_sink"], 0, [[1, 16]])).then_inc(S["v_in"], 16)
                sp.dma_start(mask, a["wmask"]).then_inc(S["v_in"], 16)
            else:
                sp.dma_start(lamx, bcast_rows(a["diff_lambda"], 0, [[DH, 4], [1, DH]])).then_inc(S["v_in"], 16)

        @block.gpsimd
        def _(pool):
            if odd:
                pool.wait_ge(S["v_in"], 64)
            with pool.Fori(0, ITER // 2) as i:
                for b in range(2):
                    pool.wait_ge(S["qk"], 2 * UN * i)
                    chunk = (0 if odd else CQB) + i * 2 + b
                    kchunk = i // 2 if odd else i * 2 + b
                    nc.gpsimd.tensor_copy(qr[:, b, :], proj[:, chunk, :]).then_inc(S["q_in"], 1)
                    nc.gpsimd.tensor_copy(kr[:, b, :], proj[:, (8 if odd else CKB) + kchunk, :]).then_inc(S["q_in"], 1)
                    nc.gpsimd.tensor_copy(kcr[:, b, :], kctx[:, kchunk, :]).then_inc(S["q_in"], 1)
                    if odd:
                        pool.wait_ge(S["exp"], 2 * UN * i)
                        nc.gpsimd.tensor_copy(sinkc[:, b, :], sink[:, bass.ds(4 * i + 2 * b, 2)]).then_inc(S["q_in"], 1)

        @block.tensor
        def _(pe):
            pe.wait_ge(S["v_in"], 64 if odd else 48)
            with pe.Fori(0, ITER // 2) as i2:
                for b in range(2):
                    i = i2 * 2 + b
                    N = i * UN
                    if odd:
                        kchunk = i2 // 2
                    else:
                        kchunk = i

                    def qk(u):
                        t, m, lo, hi = unit(u)
                        rows = slice(DH * m, DH * m + DH)
                        q = qr[rows, b, t * P:(t + 1) * P]
                        dst = k.pt[m]
                        pe.wait_ge(S["max" if odd else "exp"], N + max(u - 1, 0))
                        keys = kr[rows, b]

                        def put(col, cols, rhs):
                            return nc.tensor.matmul(dst[:, col:col + cols], q, rhs, start=True, stop=True)
                        if t == LAT_TILES:
                            last = put(lo, P, keys[:, NS:NT])
                        elif odd:
                            if t:
                                put(128, P, keys[:, (t - 1) * P:t * P])
                            put(256, PAST, kcr[rows, b, :])
                            last = put(512, hi - 512, keys[:, t * P:t * P + hi - 512])
                        else:
                            put(0, PAST, kcr[rows, b, :])
                            put(256, 256, keys[:, 0:256])
                            last = put(512, 256, keys[:, 256:512])
                        last.then_inc(S["qk"], 1)

                    def turn(u):
                        t, m, lo, hi = unit(u)
                        pe.wait_ge(S["exp"], N + u + 1)
                        pe.wait_ge(S["outd"], N + u)
                        pe.wait_ge(S["outa"], outa(i, u))
                        n, h = split(u)
                        for j in range(n):
                            dst = k.bank(4)[:, j * P:(j + 1) * P] if j < h else k.bank(5)[:, (j - h) * P:(j - h + 1) * P]
                            last = nc.tensor.transpose(dst, prob[:, u % 2, j * P:(j + 1) * P], k.ident)
                        last.then_inc(S["pt"], 1)

                    def pv(u):
                        t, m, lo, hi = unit(u)
                        pe.wait_ge(S["outd"], N + u + 1)
                        pe.wait_ge(S["outa"], outa(i, u + 1))
                        pe.wait_ge(S["comb"], N + (u if m == 0 and not odd else max(u - 1, 0)))
                        tiles = key_tiles(t)
                        for j, (kind, vt) in enumerate(tiles):
                            if odd:
                                v = (vctx if kind == "ctx" else vlat)[:, vt, kchunk * 2 + m, :]
                                o = k.bank(6 + m)[:, 0:DH]
                            else:
                                v = (vctx if kind == "ctx" else vlat)[:, vt, kchunk, :]
                                o = k.bank(6 + m)[:, 0:P]
                            last = nc.tensor.matmul(o, probT[:, u % 2, j * P:(j + 1) * P], v, start=(j == 0),
                                                    stop=(j == len(tiles) - 1))
                        last.then_inc(S["pv"], 1)

                    pe.wait_ge(S["q_in"], QIN * i + QIN)
                    qk(0)
                    for u in range(UN):
                        if u + 1 < UN:
                            qk(u + 1)
                        turn(u)
                        if u:
                            pv(u - 1)
                    pv(UN - 1)
                    if odd:
                        pe.wait_ge(S["comb"], N + UN)
                    else:
                        pe.wait_ge(S["norm"], i + 1)
                    for t in range(TILES):
                        last = nc.tensor.transpose(k.pt[2][:, t * P:(t + 1) * P], ob[:, t, :], k.ident)
                    last.then_inc(S["turned"], 1)
                    pe.wait_ge(S["stored"], i + 1)

        @block.scalar
        def _(act):
            if not odd:
                act.wait_ge(S["dots"], 2)
                nc.scalar.activation(dots, dots, ACT.Exp).then_inc(S["lam"], 1)
            else:
                act.wait_ge(S["v_in"], 64)
            with act.Fori(0, ITER // 2) as i2:
                for b in range(2):
                    i = i2 * 2 + b
                    N = i * UN

                    def evacuate(u):
                        n, h = split(u)
                        if n > h:
                            act.wait_ge(S["pt"], N + u + 1)
                            act.wait_ge(S["pv"], N + max(u - 1, 0))
                            nc.scalar.copy(probT[:, u % 2, h * P:n * P], k.bank(5)[:, 0:(n - h) * P]).then_inc(S["outa"], 1)

                    if odd:
                        act.wait_ge(S["q_in"], QIN * i + QIN)
                    for u in range(UN):
                        t, m, lo, hi = unit(u)
                        act.wait_ge(S["max"], N + u + 1)
                        act.wait_ge(S["small"], N + u + 1)
                        act.wait_ge(S["pt"], N + max(u - 1, 0))
                        if odd:
                            nc.scalar.activation(esink[:, u:u + 1], sinkc[:, b, m:m + 1], ACT.Exp,
                                                 bias=negm[:, u:u + 1]).then_inc(S["esink"], 1)
                            nc.scalar.activation(prob[:, u % 2, 0:hi - lo], prob[:, u % 2, 0:hi - lo], ACT.Exp,
                                                 bias=negm[:, u:u + 1], accum_out=rsum[:, u:u + 1]).then_inc(S["exp"], 1)
                        else:
                            nc.scalar.activation(prob[:, u % 2, 0:hi - lo], k.pt[m][:, lo:hi], ACT.Exp, scale=SCALE,
                                                 bias=negm[:, u:u + 1], accum_out=rsum[:, u:u + 1]).then_inc(S["exp"], 1)
                        if u:
                            evacuate(u - 1)
                    evacuate(UN - 1)
                    if not odd:
                        act.wait_ge(S["ssq"], i + 1)
                        nc.scalar.activation(rstd, ssq, ACT.Ln, scale=1.0 / P, bias=k.eps).then_inc(S["rstd"], 1)
                        act.wait_ge(S["rstd"], 2 * i + 1)
                        nc.scalar.activation(rstd, rstd, ACT.Exp, scale=-0.5).then_inc(S["rstd"], 1)
                    act.wait_ge(S["turned"], i + 1)
                    dst = k.mx[:, (0 if odd else 4) + i, :]
                    if odd:
                        nc.scalar.copy(dst, k.pt[2][:, 0:NT]).then_inc(S["stored"], 1)
                    else:
                        nc.scalar.activation(dst, k.pt[2][:, 0:NT], ACT.Identity, scale=gdiff).then_inc(S["stored"], 1)

        @block.vector
        def _(dve):
            dve.wait_ge(S["v_in"], 64 if odd else 48)
            c = Chain(k, dve, f"at_dve_{tag}")
            if not odd:
                for j in range(2):
                    nc.vector.tensor_tensor_reduce(junk[:, DH * j:DH * (j + 1)], lamx[:, 2 * j, :], lamx[:, 2 * j + 1, :], 1.0, 0.0,
                                                   ALU.mult, ALU.add, dots[:, j:j + 1]).then_inc(S["dots"], 1)
                dve.wait_ge(S["lam"], 1)
                c.link(nc.vector.tensor_tensor(neglam, dots[:, 1:2], dots[:, 0:1], ALU.subtract))
                c.link(nc.vector.tensor_scalar(neglam, neglam, -LAM_INIT, None, ALU.add))
                c.link(nc.vector.tensor_scalar(gdiff, k.cols[:, ROW_DG:ROW_DG + 1], 1.0 - LAM_INIT, None, ALU.mult))
            with dve.Fori(0, ITER // 2) as i2:
                c.enter(i2, 4 * UN if odd else 4 * TILES - 2)
                for b in range(2):
                    i = i2 * 2 + b
                    N = i * UN

                    def evacuate(u):
                        n, h = split(u)
                        dve.wait_ge(S["pt"], N + u + 1)
                        dve.wait_ge(S["pv"], N + max(u - 1, 0))
                        nc.vector.tensor_copy(probT[:, u % 2, 0:h * P], k.bank(4)[:, 0:h * P]).then_inc(S["outd"], 1)

                    def combine(u):
                        t, m, lo, hi = unit(u)
                        dve.wait_ge(S["pv"], N + u + 1)
                        if odd:
                            dve.wait_ge(S["esink"], N + u + 1)
                            c.link(nc.vector.tensor_tensor(rsum[:, u:u + 1], rsum[:, u:u + 1], esink[:, u:u + 1], ALU.add))
                            c.link(nc.vector.reciprocal(rinv[:, u:u + 1], rsum[:, u:u + 1]))
                            nc.vector.tensor_scalar(ob[:, t, m * DH:(m + 1) * DH], k.bank(6 + m)[:, 0:DH],
                                                    rinv[:, u:u + 1], None, ALU.mult).then_inc(S["comb"], 1)
                        elif m == 1:
                            c.link(nc.vector.reciprocal(rinv[:, u - 1:u + 1], rsum[:, u - 1:u + 1]))
                            nc.vector.tensor_scalar(t2, k.bank(7)[:, 0:P], rinv[:, u:u + 1], neglam, ALU.mult,
                                                    ALU.mult).then_inc(S["comb"], 1)
                            dve.wait_ge(S["comb"], N + u)
                            nc.vector.scalar_tensor_tensor(out=ob[:, t, :], in0=k.bank(6)[:, 0:P],
                                                           scalar=rinv[:, u - 1:u], in1=t2, op0=ALU.mult,
                                                           op1=ALU.add).then_inc(S["comb"], 1)
                            dve.wait_ge(S["comb"], N + u + 1)
                            op = nc.vector.tensor_tensor_reduce(junk, ob[:, t, :], ob[:, t, :], 1.0, 0.0, ALU.mult,
                                                                ALU.add, ssq[:, t:t + 1])
                            if t == LAT_TILES:
                                op.then_inc(S["ssq"], 1)
                                dve.wait_ge(S["ssq"], i + 1)
                            else:
                                c.link(op)

                    if odd:
                        dve.wait_ge(S["q_in"], QIN * i + QIN)
                    for u in range(UN):
                        t, m, lo, hi = unit(u)
                        dve.wait_ge(S["qk"], N + u + 1)
                        if odd:
                            dve.wait_ge(S["pt"], N + max(u - 1, 0))
                            nc.vector.tensor_copy(tick, mask[:, 0:1])
                            nc.vector.tensor_tensor_reduce(prob[:, u % 2, 0:hi - lo], k.pt[m][:, lo:hi], mask[:, lo:hi],
                                                           SCALE, -3e38, ALU.add, ALU.max, top[:, u:u + 1]).then_inc(S["max"], 1)
                            dve.wait_ge(S["max"], N + u + 1)
                            nc.vector.tensor_scalar(negm[:, u:u + 1], top[:, u:u + 1],
                                                    sinkc[:, b, m:m + 1], -1.0, ALU.max,
                                                    ALU.mult).then_inc(S["small"], 1)
                        else:
                            nc.vector.reduce_max(top[:, u:u + 1], k.pt[m][:, lo:hi], AX).then_inc(S["max"], 1)
                            dve.wait_ge(S["max"], N + u + 1)
                            nc.vector.tensor_scalar(negm[:, u:u + 1], top[:, u:u + 1], -SCALE, None,
                                                    ALU.mult).then_inc(S["small"], 1)
                        if u:
                            evacuate(u - 1)
                        if u >= 2:
                            combine(u - 2)
                    evacuate(UN - 1)
                    combine(UN - 2)
                    combine(UN - 1)
                    if not odd:
                        dve.wait_ge(S["rstd"], 2 * i + 2)
                        nc.vector.tensor_tensor(ob, ob, rstd.rearrange("p (t o) -> p t o", o=1).broadcast_to([P, TILES, P]),
                                                ALU.mult).then_inc(S["norm"], 1)
                c.leave(ITER // 2)



def norm_steps(k, tag):
    return {n: k.sem(f"ln_{n}_{tag}") for n in ("rows_in", "done", "read", "stats", "lnvar", "rstd", "shift", "normed",
                                                "scaled", "ready", "out")}


def phase_residual_norm(k, a, l, which):
    nc = k.nc
    tag = f"{l}{which}"
    S = norm_steps(k, tag)
    gate_rows = k.at(k.H, 2048).rearrange("p (g n) -> p g n", g=2)
    ln_g, ln_b = k.at(k.H + 2048, D), k.at(k.H + 3072, D)
    tmp = k.at(k.scr, 2048).rearrange("p (b n) -> p b n", b=2)
    st = k.at(k.scr + 2048, 12 * TILES).rearrange("p (t n) -> p t n", t=TILES)
    mv = k.at(k.scr + 2110, 2 * TILES).rearrange("p (t n) -> p t n", t=TILES)
    rstd = k.at(k.scr + 2120, TILES)
    shift = k.at(k.scr + 2125, TILES)
    part = GA1 if which == 0 else GA2
    base = BASE_OUT0 if l == 0 else BASE_OUT1
    last_norm = l == DEPTH - 1 and which == 1
    with nc.Block() as block:
        @block.sync
        def _(sp):
            for g in range(2):
                off = l * 96 * P + (2 * part + g) * P
                sp.dma_start(gate_rows[:, g, :].rearrange("p (c n) -> p c n", n=P),
                             bcast_rows(k.dram["mod_rows"], off, [[2 * P, KC], [1, P]])).then_inc(S["rows_in"], 16)
            off = (2 * l + which) * D
            sp.dma_start(ln_g, bcast_rows(a["ln_g"], off, [[1, D]])).then_inc(S["rows_in"], 16)
            sp.dma_start(ln_b, bcast_rows(a["ln_b"], off, [[1, D]])).then_inc(S["rows_in"], 16)
            if which == 0:
                for s in range(6):
                    if l:
                        sp.wait_ge(k.r_free, 6 * E * l)
                    sp.dma_start(k.ring[s], expert_half(a, l, 0, s)).then_inc(k.r_landed[s], 16)
            elif l == 0:
                for u in range(WSLOTS):
                    feed(k, sp, BASE_IN1 + u, in1_units(a)[u])
            for t in range(TILES):
                sp.wait_ge(S["ready"], t + 1)
                if last_norm:
                    dst = a["y_sample"][t * P:(t + 1) * P, :] if t < LAT_TILES else a["y_prompt"]
                else:
                    dst = k.dram["y_rows"][t * P:(t + 1) * P, :]
                sp.dma_start(dst, k.y[:, t, :]).then_inc(S["out"], 16)
            sp.wait_ge(S["out"], 16 * TILES)

        @block.tensor
        def _(pe):
            if which == 1:
                return
            for s in range(4):
                n = base + s
                pe.wait_ge(k.w_landed[n % WSLOTS], 16 * (n // WSLOTS + 1))
                for t in range(TILES):
                    g = s * TILES + t
                    if g >= 8:
                        pe.wait_ge(S["read"], g - 7)
                    for c in range(KC):
                        last = nc.tensor.matmul(k.bank(g % 8)[:, 0:UNIT], k.mx[:, c, t * P:(t + 1) * P],
                                                k.wst[n % WSLOTS][:, c, :], start=(c == 0), stop=(c == KC - 1))
                    last.then_inc(S["done"], 1)

        @block.scalar
        def _(act):
            for t in range(TILES):
                act.wait_ge(S["stats"], t + 1)
                nc.scalar.activation(rstd[:, t:t + 1], mv[:, t, 1:2], ACT.Ln, bias=k.eps).then_inc(S["lnvar"], 1)
                act.wait_ge(S["lnvar"], t + 1)
                nc.scalar.activation(rstd[:, t:t + 1], rstd[:, t:t + 1], ACT.Exp, scale=-0.5).then_inc(S["rstd"], 1)
                act.wait_ge(S["shift"], t + 1)
                act.wait_ge(S["rstd"], t + 1)
                nc.scalar.activation(k.y[:, t, :], k.y[:, t, :], ACT.Identity, scale=rstd[:, t:t + 1],
                                     bias=shift[:, t:t + 1]).then_inc(S["normed"], 1)

        @block.gpsimd
        def _(pool):
            for t in range(TILES):
                pool.wait_ge(S["scaled"], t + 1)
                nc.gpsimd.tensor_tensor(k.y[:, t, :], k.y[:, t, :], ln_b, ALU.add).then_inc(S["ready"], 1)

        @block.vector
        def _(dve):
            c = Chain(k, dve, f"ln_dve_{tag}")
            dve.wait_ge(S["rows_in"], 64)

            def statistics(t):
                nc.vector.bn_stats(st[:, t, 0:6], k.y[:, t, 0:512])
                c.link(nc.vector.bn_stats(st[:, t, 6:12], k.y[:, t, 512:1024]))
                nc.vector.bn_aggr(mv[:, t, :], st[:, t, :]).then_inc(S["stats"], 1)

            def finish(t):
                dve.wait_ge(S["rstd"], t + 1)
                dve.wait_ge(S["stats"], t + 1)
                nc.vector.tensor_scalar(shift[:, t:t + 1], mv[:, t, 0:1], rstd[:, t:t + 1], -1.0, ALU.mult,
                                        ALU.mult).then_inc(S["shift"], 1)

            def scale(t):
                dve.wait_ge(S["normed"], t + 1)
                nc.vector.tensor_tensor(k.y[:, t, :], k.y[:, t, :], ln_g, ALU.mult).then_inc(S["scaled"], 1)

            if which == 0:
                for s in range(4):
                    for t in range(TILES):
                        g = s * TILES + t
                        cols = slice(s * UNIT, (s + 1) * UNIT)
                        dve.wait_ge(S["done"], g + 1)
                        x = tmp[:, g % 2, 0:UNIT]
                        nc.vector.tensor_tensor(x, k.bank(g % 8)[:, 0:UNIT], gate_rows[:, t // LAT_TILES, cols],
                                                ALU.mult).then_inc(S["read"], 1)
                        dve.wait_ge(S["read"], g + 1)
                        c.link(nc.vector.scalar_tensor_tensor(out=k.y[:, t, cols], in0=k.y[:, t, cols], scalar=ALPHA,
                                                              in1=x, op0=ALU.mult, op1=ALU.add))
            for t in range(TILES):
                if which == 1:
                    c.link(nc.vector.tensor_tensor(tmp[:, t % 2, :], k.moe[:, t, :], gate_rows[:, t // LAT_TILES, :], ALU.mult))
                    c.link(nc.vector.scalar_tensor_tensor(out=k.y[:, t, :], in0=k.y[:, t, :], scalar=ALPHA,
                                                          in1=tmp[:, t % 2, :], op0=ALU.mult, op1=ALU.add))
                statistics(t)
                if t:
                    finish(t - 1)
                if t >= 2:
                    scale(t - 2)
            finish(TILES - 1)
            scale(TILES - 2)
            scale(TILES - 1)


def expert_half(a, l, e, s):
    name, half = [("w_exp_gate", 0), ("w_exp_up", 0), ("w_exp_gate", 1), ("w_exp_up", 1), ("w_exp_down", 0),
                  ("w_exp_down", 1)][s]
    return a[name][l].rearrange("e (c p) (h n) -> e h p c n", p=P, h=2)[e, half]


def moe_views(k):
    w, s = k.WST, k.scr
    v = {}
    v["xs"] = k.at(w, 2048).rearrange("p (b n) -> p b n", b=2)
    v["outT"] = k.at(w + 2048, 1024).rearrange("p (c n) -> p c n", c=KC)
    v["outTc"] = k.at(w + 3072, 2048).rearrange("p (c n) -> p c n", c=KC)
    v["rows"] = k.at(w + 5120, 1024)
    v["hot"] = k.at(w + 6144, 512)
    v["scale"] = k.at(w + 6656, 640).rearrange("p (c n) -> p c n", c=KC)
    v["shift"] = k.at(w + 7296, 640).rearrange("p (c n) -> p c n", c=KC)
    v["iota"] = k.at(s, 512)
    v["idx_pair"] = k.at(s + 512, 8)
    v["gate_pair"] = k.at(s + 520, 8)
    v["idx_ctx"] = k.at(s + 528, 2)
    v["gate_ctx"] = k.at(s + 530, 2)
    v["idx80"] = k.at(s + 532, 16)
    v["icol"] = k.at(s + 548, 2)
    v["tick"] = k.at(s + 550, 1)
    v["xT"] = k.at(k.H, 1280).rearrange("p (b c n) -> p b c n", b=2, c=KC)
    v["hid"] = k.at(k.H + 1280, 640).rearrange("p (c n) -> p c n", c=KC)
    v["sg"] = k.at(k.H + 1920, 640).rearrange("p (h n) -> p h n", h=2)
    return v


def phase_router(k, a, l):
    nc = k.nc
    v = moe_views(k)
    s0 = k.scr + 560
    wr = k.at(s0, 128).rearrange("p (c n) -> p c n", c=KC)
    top = k.at(s0 + 128, TILES)
    tot = k.at(s0 + 133, TILES)
    aff = k.at(s0 + 140, 80).rearrange("p (t n) -> p t n", t=TILES)
    affT = k.at(s0 + 220, NT)[0:E]
    vals = k.at(s0 + 860, SLOTS)[0:E]
    idx = k.at(s0 + 940, SLOTS).bitcast(U32)[0:E]
    idf = k.at(s0 + 1020, SLOTS)[0:E]
    S = {n: k.sem(f"ro_{n}_{l}") for n in ("w_in", "logits", "sub", "exp", "aff", "turned", "picked", "kept", "laid", "ctxi",
                                           "slots")}
    lg = k.bank(4)[:, 0:80].rearrange("p (t n) -> p t n", t=TILES)
    with nc.Block() as block:
        @block.sync
        def _(sp):
            sp.dma_start(wr, a["w_router"][l].rearrange("(c p) n -> p c n", p=P)).then_inc(S["w_in"], 16)
            sp.dma_start(v["iota"], a["iota"]).then_inc(S["w_in"], 16)
            sp.wait_ge(S["picked"], 1)
            dv, di = k.dram["gates"], k.dram["index"]
            ns = E * CAP_S
            for dst, src in ((dv, vals), (di, idf)):
                sp.dma_start(dst[0:ns].rearrange("(e s) -> e s", s=CAP_S), src[:, 0:CAP_S]).then_inc(S["kept"], 16)
                sp.dma_start(dst[ns:].rearrange("(e s) -> e s", s=CAP_P), src[:, CAP_S:SLOTS]).then_inc(S["kept"], 16)
            sp.wait_ge(S["kept"], 64)
            with nc.allow_non_contiguous_dma(reason="slot tables of a few hundred words"):
                sp.dma_start(v["idx80"][0:CAP_S], di[0:ns].rearrange("(e s) -> s e", s=CAP_S)).then_inc(S["laid"], 16)
                sp.dma_start(v["idx80"][CAP_S:SLOTS], di[ns:].rearrange("(e s) -> s e", s=CAP_P)).then_inc(S["laid"], 16)
                for dst, src in (("idx_pair", di), ("gate_pair", dv)):
                    sp.dma_start(v[dst], src[0:ns].rearrange("(e s) -> s e", s=P)).then_inc(S["laid"], 16)
                for dst, src in (("idx_ctx", di), ("gate_ctx", dv)):
                    sp.dma_start(v[dst], src[ns:].rearrange("(e s) -> s e", s=P)).then_inc(S["laid"], 16)
            sp.wait_ge(S["laid"], 96)

        @block.tensor
        def _(pe):
            pe.wait_ge(S["w_in"], 32)
            for t in range(TILES):
                for c in range(KC):
                    last = nc.tensor.matmul(lg[:, t, :], k.h[:, c, t * P:(t + 1) * P], wr[:, c, :], start=(c == 0),
                                            stop=(c == KC - 1))
            last.then_inc(S["logits"], 1)
            pe.wait_ge(S["aff"], 1)
            for t in range(TILES):
                last = nc.tensor.transpose(k.pt[0][0:E, t * P:(t + 1) * P], aff[:, t, :], k.ident)
            last.then_inc(S["turned"], 1)

        @block.scalar
        def _(act):
            act.wait_ge(S["sub"], 1)
            nc.scalar.activation(aff, aff, ACT.Exp).then_inc(S["exp"], 1)

        @block.gpsimd
        def _(pool):
            nc.gpsimd.memset(k.mx, 0.0)

        @block.vector
        def _(dve):
            c = Chain(k, dve, f"ro_dve_{l}")
            for name, part in (("scale", SC2), ("shift", SH2)):
                for g, (lo, hi) in enumerate(((0, CAP_S), (CAP_S, SLOTS))):
                    nc.vector.tensor_copy(v[name][:, :, lo:hi],
                                          k.mod[l][:, part:part + KC, g:g + 1].broadcast_to([P, KC, hi - lo]))
            dve.wait_ge(S["logits"], 1)
            c.link(nc.vector.reduce_max(top, lg, AX))
            nc.vector.tensor_tensor(aff, lg, top.rearrange("p (t o) -> p t o", o=1).broadcast_to([P, TILES, E]),
                                    ALU.subtract).then_inc(S["sub"], 1)
            dve.wait_ge(S["exp"], 1)
            c.link(nc.vector.reduce_sum(tot, aff, AX))
            c.link(nc.vector.reciprocal(tot, tot))
            nc.vector.tensor_tensor(aff, aff, tot.rearrange("p (t o) -> p t o", o=1).broadcast_to([P, TILES, E]),
                                    ALU.mult).then_inc(S["aff"], 1)
            dve.wait_ge(S["turned"], 1)
            c.link(nc.vector.tensor_copy(affT, k.pt[0][0:E, 0:NT]))
            for lo, hi, first, rounds in ((0, NS, 0, CAP_S // 8), (NS, NT, CAP_S, CAP_P // 8)):
                row = affT[:, lo:hi]
                for r in range(rounds):
                    sl = slice(first + 8 * r, first + 8 * r + 8)
                    c.link(nc.vector.max(vals[:, sl], row))
                    c.link(nc.vector.max_index(idx[:, sl], vals[:, sl], row))
                    if r < rounds - 1:
                        c.link(nc.vector.match_replace(row, vals[:, sl], row, -1.0))
            nc.vector.tensor_copy(idf[:, 0:CAP_S], idx[:, 0:CAP_S])
            nc.vector.tensor_scalar(idf[:, CAP_S:SLOTS], idx[:, CAP_S:SLOTS], float(NS), None,
                                    ALU.add).then_inc(S["picked"], 1)


def phase_experts(k, a, l):
    nc = k.nc
    v = moe_views(k)
    S = {n: k.sem(f"ex_{n}_{l}") for n in ("icol", "g0", "g1", "x0", "x1", "xmul", "xev", "silu0", "silu1", "hid0", "hid1",
                                           "outs0", "outs1", "outc0", "outc1", "turned", "rows", "hot", "sum", "acc")}
    GATHERED, XTURNED = (S["g0"], S["g1"]), (S["x0"], S["x1"])
    SILU, HID, OUTS, OUTC = ((S[n + "0"], S[n + "1"]) for n in ("silu", "hid", "outs", "outc"))
    rbase = 6 * E * l
    PAIRS = E // 2

    def side(x):
        return x.rearrange("p (c n) -> p c n", n=SLOTS)

    with nc.Block() as block:
        @block.sync
        def _(sp):
            with sp.Fori(1, E) as e:
                for s in range(6):
                    sp.wait_ge(k.r_free, e * 6 + (rbase + s - 5))
                    sp.dma_start(k.ring[s], expert_half(a, l, e, s)).then_inc(k.r_landed[s], 16)

        @block.gpsimd
        def _(pool):
            with pool.Fori(0, PAIRS) as i:
                for b in range(2):
                    pool.wait_ge(GATHERED[b], 16 * i)
                    nc.gpsimd.tensor_copy(v["icol"][0:SLOTS, b:b + 1].bitcast(U32),
                                          v["idx80"][0:SLOTS, bass.ds(2 * i + b, 1)]).then_inc(S["icol"], 1)
                    pool.wait_ge(XTURNED[b], i)
                    pool.wait_ge(S["icol"], 2 * i + b + 1)
                    nc.gpsimd.tensor_tensor(v["tick"], v["iota"][:, 0:1], v["iota"][:, 0:1],
                                            ALU.add)
                    nc.gpsimd.indirect_dma_start(
                        v["xs"][0:SLOTS, b, :], None, k.dram["y_rows"],
                        bass.IndirectOffsetOnAxis(ap=v["icol"][0:SLOTS, b:b + 1].bitcast(U32), axis=0)).then_inc(GATHERED[b], 16)

        @block.tensor
        def _(pe):
            with pe.Fori(0, PAIRS) as i:
                for b in range(2):
                    e = 2 * i + b
                    pe.wait_ge(GATHERED[b], 16 * i + 16)
                    pe.wait_ge(S["xev"], e)
                    if b == 0:
                        pe.wait_ge(S["rows"], 2 * i)
                    for c in range(KC):
                        last = nc.tensor.transpose(k.pt[0][:, c // 4 * 512 + (c % 4) * SLOTS:c // 4 * 512 + (c % 4 + 1) * SLOTS],
                                                   v["xs"][0:SLOTS, b, c * P:(c + 1) * P], k.ident[0:SLOTS, 0:SLOTS])
                    last.then_inc(XTURNED[b], 1)
                    pe.wait_ge(S["xev"], e + 1)
                    if b == 0:
                        pe.wait_ge(S["acc"], 8 * i)
                    for hf in range(2):
                        pe.wait_ge(HID[hf], e)
                        for m in range(2):
                            s = 2 * hf + m
                            pe.wait_ge(k.r_landed[s], e * 16 + 16 * (E * l + 1))
                            for f in range(4):
                                for c in range(KC):
                                    last = nc.tensor.matmul(k.bank(2 + 2 * hf + m)[:, f * SLOTS:(f + 1) * SLOTS],
                                                            k.ring[s][:, c, f * P:(f + 1) * P], v["xT"][:, b, c, :],
                                                            start=(c == 0), stop=(c == KC - 1))
                            last.then_inc(k.r_free, 1)
                    for hd in range(2):
                        pe.wait_ge(k.r_landed[4 + hd], e * 16 + 16 * (E * l + 1))
                        pe.wait_ge(HID[0], e + 1)
                        pe.wait_ge(HID[1], e + 1)
                        pe.wait_ge(OUTS[hd], e)
                        pe.wait_ge(OUTC[hd], e)
                        for c in range(4):
                            for f in range(KC):
                                last = nc.tensor.matmul(k.bank(6 + hd)[:, c * SLOTS:(c + 1) * SLOTS],
                                                        k.ring[4 + hd][:, f, c * P:(c + 1) * P], v["hid"][:, f, :],
                                                        start=(f == 0), stop=(f == KC - 1))
                        last.then_inc(k.r_free, 1)
                for hd in range(2):
                    pe.wait_ge(OUTS[hd], 2 * i + 2)
                pe.wait_ge(S["xev"], 2 * i + 2)
                for c in range(KC):
                    last = nc.tensor.transpose(k.pt[0][:, c * P:(c + 1) * P], v["outT"][:, c, :], k.ident)
                last.then_inc(S["turned"], 1)
                pe.wait_ge(S["rows"], 2 * i + 2)
                pe.wait_ge(S["hot"], i + 1)
                pe.wait_ge(HID[1], 2 * i + 2)
                for j in range(8):
                    t, hf = divmod(j, 2)
                    if j >= 4:
                        pe.wait_ge(S["acc"], 8 * i + j - 3)
                    nc.tensor.matmul(k.bank(2 + j % 4), v["hot"][:, t * P:(t + 1) * P], v["rows"][:, hf * 512:(hf + 1) * 512],
                                     start=True, stop=True).then_inc(S["sum"], 1)
            for hd in range(2):
                pe.wait_ge(OUTC[hd], E)
            pe.wait_ge(S["acc"], 8 * PAIRS)
            for q in range(2):
                pe.wait_ge(S["rows"], 2 * PAIRS + 2 * q)
                for c in range(KC):
                    last = nc.tensor.transpose(k.pt[0][:, c * P:(c + 1) * P], v["outTc"][:, c, q * P:(q + 1) * P], k.ident)
                last.then_inc(S["turned"], 1)
                pe.wait_ge(S["rows"], 2 * PAIRS + 2 * q + 2)
                pe.wait_ge(S["hot"], PAIRS + q + 1)
                for hf in range(2):
                    nc.tensor.matmul(k.bank(2 + hf), v["hot"][:, 0:P], v["rows"][:, hf * 512:(hf + 1) * 512],
                                     start=(q == 0), stop=(q == 1)).then_inc(S["sum"], 1)

        @block.scalar
        def _(act):
            with act.Fori(0, PAIRS) as i:
                for b in range(2):
                    e = 2 * i + b
                    for hf in range(2):
                        act.wait_ge(k.r_free, 6 * e + (rbase + 2 * hf + 1))
                        act.wait_ge(HID[hf], e)
                        nc.scalar.activation(v["sg"][:, hf, 0:320], k.bank(2 + 2 * hf)[:, 0:320], ACT.Silu).then_inc(SILU[hf], 1)
                    for hd in range(2):
                        act.wait_ge(k.r_free, 6 * e + (rbase + 5 + hd))
                        nc.scalar.copy(v["outTc"][:, 4 * hd:4 * hd + 4, bass.ds(CAP_P * e, CAP_P)],
                                       side(k.bank(6 + hd)[:, 0:320])[:, :, CAP_S:SLOTS]).then_inc(OUTC[hd], 1)
                        if b == 0:
                            act.wait_ge(S["turned"], i)
                        nc.scalar.copy(v["outT"][:, 4 * hd:4 * hd + 4, b * CAP_S:(b + 1) * CAP_S],
                                       side(k.bank(6 + hd)[:, 0:320])[:, :, 0:CAP_S]).then_inc(OUTS[hd], 1)
                act.wait_ge(S["turned"], i + 1)
                act.wait_ge(S["sum"], 8 * i)
                for hf in range(2):
                    nc.scalar.activation(v["rows"][:, hf * 512:(hf + 1) * 512], k.bank(hf), ACT.Copy,
                                         scale=v["gate_pair"][:, bass.ds(i, 1)]).then_inc(S["rows"], 1)
            for q in range(2):
                act.wait_ge(S["turned"], PAIRS + q + 1)
                act.wait_ge(S["sum"], 8 * PAIRS + 2 * q)
                for hf in range(2):
                    nc.scalar.activation(v["rows"][:, hf * 512:(hf + 1) * 512], k.bank(hf), ACT.Copy,
                                         scale=v["gate_ctx"][:, q:q + 1]).then_inc(S["rows"], 1)

        @block.vector
        def _(dve):
            with dve.Fori(0, PAIRS) as i:
                for b in range(2):
                    e = 2 * i + b
                    dve.wait_ge(XTURNED[b], i + 1)
                    for hf in range(2):
                        chunks = slice(4 * hf, 4 * hf + 4)
                        nc.vector.tensor_tensor(v["xT"][:, b, chunks, :], side(k.bank(hf)[:, 0:320]), v["scale"][:, chunks, :],
                                                ALU.mult).then_inc(S["xmul"], 1)
                    dve.wait_ge(S["xmul"], 2 * e + 2)
                    nc.vector.tensor_tensor(v["xT"][:, b], v["xT"][:, b], v["shift"], ALU.add).then_inc(S["xev"], 1)
                    for hf in range(2):
                        dve.wait_ge(SILU[hf], e + 1)
                        dve.wait_ge(k.r_free, 6 * e + (rbase + 2 * hf + 2))
                        nc.vector.tensor_tensor(v["hid"][:, 4 * hf:4 * hf + 4, :].rearrange("p c n -> p (c n)"),
                                                v["sg"][:, hf, 0:320], k.bank(3 + 2 * hf)[:, 0:320],
                                                ALU.mult).then_inc(HID[hf], 1)
                    if b == 1:
                        dve.wait_ge(S["sum"], 8 * i)
                        nc.vector.tensor_scalar(v["hot"], v["iota"], v["idx_pair"][:, bass.ds(i, 1)], None,
                                                ALU.is_equal).then_inc(S["hot"], 1)
                for j in range(8):
                    t, hf = divmod(j, 2)
                    dve.wait_ge(S["sum"], 8 * i + j + 1)
                    acc = k.moe[:, t, hf * 512:(hf + 1) * 512]
                    nc.vector.tensor_tensor(acc, acc, k.bank(2 + j % 4), ALU.add).then_inc(S["acc"], 1)
            c = Chain(k, dve, f"ex_dve_{l}")
            for q in range(2):
                dve.wait_ge(S["sum"], 8 * PAIRS + 2 * q)
                c.link(nc.vector.tensor_scalar(v["idx_ctx"][:, q:q + 1], v["idx_ctx"][:, q:q + 1], -float(NS), None, ALU.add))
                nc.vector.tensor_scalar(v["hot"][:, 0:P], v["iota"][:, 0:P], v["idx_ctx"][:, q:q + 1], None,
                                        ALU.is_equal).then_inc(S["hot"], 1)
            dve.wait_ge(S["sum"], 8 * PAIRS + 4)
            for hf in range(2):
                nc.vector.tensor_copy(k.moe[:, LAT_TILES, hf * 512:(hf + 1) * 512], k.bank(2 + hf))


def build(nc, a, last=None):
    with ExitStack() as stack:
        dram = {
            "mod_rows": nc.dram_tensor("mod_rows", (DEPTH, 96, P), F32, kind="Internal").ap(),
            "y_rows": nc.dram_tensor("y_rows", (NT, D), F32, kind="Internal").ap(),
            "gates": nc.dram_tensor("slot_gates", (E * SLOTS,), F32, kind="Internal").ap(),
            "index": nc.dram_tensor("slot_index", (E * SLOTS,), F32, kind="Internal").ap(),
        }
        k = Ctx(nc, stack, dram)
        k.moe = k.mx.rearrange("p c n -> p (c n)").rearrange("p (t n) -> p t n", t=TILES)
        phases = [
            ("mod", lambda: phase_modulation(k, a)),
            ("h0", lambda: phase_modulate(k, 0, SH1, SC1, "00")),
            ("proj0", lambda: phase_project_even(k, a)),
            ("hgrn", lambda: phase_hgrn(k, a)),
            ("rope0", lambda: phase_rope(k, a, False)),
            ("att0", lambda: phase_attention(k, a, False)),
            ("ln00", lambda: phase_residual_norm(k, a, 0, 0)),
            ("h0b", lambda: phase_modulate(k, 0, SH2, SC2, "01")),
            ("router0", lambda: phase_router(k, a, 0)),
            ("moe0", lambda: phase_experts(k, a, 0)),
            ("ln01", lambda: phase_residual_norm(k, a, 0, 1)),
            ("clear", k.clear),
            ("h1", lambda: phase_modulate(k, 1, SH1, SC1, "10")),
            ("proj1", lambda: phase_project_odd(k, a)),
            ("rope1", lambda: phase_rope(k, a, True)),
            ("att1", lambda: phase_attention(k, a, True)),
            ("ln10", lambda: phase_residual_norm(k, a, 1, 0)),
            ("h1b", lambda: phase_modulate(k, 1, SH2, SC2, "11")),
            ("router1", lambda: phase_router(k, a, 1)),
            ("moe1", lambda: phase_experts(k, a, 1)),
            ("ln11", lambda: phase_residual_norm(k, a, 1, 1)),
        ]
        for name, phase in phases:
            phase()
            if last and name == last[0]:
                last[1](k)
                break
        return k


_OUTS = {
    "y_prompt": (1, 128, 1024), "y_sample": (1, 512, 1024), "out_state": (1, 1, 2, 4, 128, 128),
    "out_diff_k": (1, 1, 4, 128, 128), "out_diff_v": (1, 1, 4, 128, 128),
    "out_win_k": (1, 1, 4, 128, 64), "out_win_v": (1, 1, 4, 128, 64),
}


def constants():
    t = np.arange(NS)
    quarter = DH // 4
    inv = (10000.0 ** (-np.arange(quarter, dtype=np.float32) / quarter)).astype(np.float32)
    angle = np.zeros((P, NS), np.float32)
    perm = np.zeros((P, P), np.float32)
    for d in range(P):
        half, j = divmod(d % DH, DH // 2)
        pos = (t // 64 if half == 0 else t % 64).astype(np.float32)
        angle[d] = pos * inv[j % quarter]
        if j < quarter:
            perm[d + quarter, d] = -1.0
        else:
            perm[d - quarter, d] = 1.0
    r = np.arange(P)
    masks = np.zeros((P, 2, 192), np.int32)
    for d in range(2):
        same = (r[:, None] // SUB) == (r[None, :] // SUB)
        order = (r[:, None] <= r[None, :]) if d == 0 else (r[:, None] >= r[None, :])
        masks[:, d, 0:P] = np.where(same & order, -1, 0)
        cols = r.reshape(4, 2, SUB)[:, 1 - d, :].reshape(-1)
        pair = (r[:, None] // CH) == (cols[None, :] // CH)
        first = (r[:, None] // SUB) % 2 == d
        masks[:, d, P:192] = np.where(pair & first, -1, 0)
    keep = np.ones((P, NT + 1), np.float32)
    keep[:, ::SUB] = 0.0
    wmask = np.zeros((P, 768), np.float32)
    wmask[:, 128:256] = np.where(r[:, None] <= r[None, :], 0.0, NEG)
    wmask[:, 640:768] = np.where(r[None, :] <= r[:, None], 0.0, NEG)
    return {
        "ident": np.eye(P, dtype=np.float32), "perm": perm, "cos": np.cos(angle), "sin": np.sin(angle),
        "hgrn_masks": masks, "keep": keep, "wmask": wmask,
        "bmask": (r[:, None] // CH == np.arange(4)[None, :]).astype(np.float32),
        "iota": np.broadcast_to(np.arange(NS, dtype=np.float32), (P, NS)).copy(),
    }


PAIRED = [h for m in range(8) for h in ((m, 4 + m) if m < 4 else (4 + m, 8 + m))]


def kernel(**inputs):
    import concourse.bacc as _bacc
    from concourse.bass_utils import run_bass_kernel_spmd as _run

    nc = _bacc.Bacc("TRN2", target_bir_lowering=False, num_devices=1)
    arrays = {n: np.ascontiguousarray(x) for n, x in inputs.items()}
    w = arrays["w_in_odd"]
    q = w[:, :, :1024].reshape(1, D, 16, DH)[:, :, PAIRED, :].reshape(1, D, 1024)
    arrays["w_in_odd"] = np.concatenate([q, w[:, :, 1024:]], axis=2)
    arrays["w_out_odd"] = arrays["w_out_odd"].reshape(1, 16, DH, D)[:, PAIRED].reshape(1, D, D)
    arrays["win_sink"] = np.ascontiguousarray(arrays["win_sink"][:, PAIRED])
    arrays.update(constants())
    arrays = {f"in_{n}": x for n, x in arrays.items()}
    a = {n[3:]: nc.dram_tensor(n, x.shape, mybir.dt.from_np(x.dtype), kind="ExternalInput").ap() for n, x in arrays.items()}
    for n, shape in _OUTS.items():
        a[n] = nc.dram_tensor(f"res_{n}", shape, F32, kind="ExternalOutput").ap()
    for n in ("y_prompt", "y_sample"):
        a[n] = a[n][0]
    for n in ("out_state", "out_diff_k", "out_diff_v", "out_win_k", "out_win_v"):
        a[n] = a[n][0, 0]
    build(nc, a)
    r = _run(nc, [arrays], core_ids=[0])
    return tuple(r.results[0][f"res_{n}"] for n in _OUTS)
```

```python
from contextlib import ExitStack

import numpy as np

import concourse.bass as bass
import concourse.mybir as mybir

F32 = mybir.dt.float32
I32 = mybir.dt.int32
U32 = mybir.dt.uint32
ALU = mybir.AluOpType
ACT = mybir.ActivationFunctionType
AX = mybir.AxisListType.X

P = 128
D = 1024
KC = D // P
NS, NP_ = 512, 128
NT = NS + NP_
TILES = NT // P
LAT_TILES = NS // P
PAST = 256
DEPTH = 2
HEADS_A = 4
HEADS_B = 4
E = 16
CAP_S, CAP_P = 2 * NS // E, 2 * NP_ // E
SLOTS = CAP_S + CAP_P
FF = 1024
ALPHA = float((2 * DEPTH) ** 0.25)
LN_EPS = 1e-5
LAM_INIT = 0.2
DH = 64
SCALE = DH ** -0.5
NEG = -1e30
UNIT = 256
WSLOTS = 4
SUB = 16
CH = 2 * SUB
GATES = 2 * HEADS_A

ROW_BMOD, ROW_C, ROW_CCTX, ROW_LB, ROW_HG, ROW_DG, N_ROWS = 0, 96, 104, 112, 124, 125, 126
SH1, SC1, GA1, SH2, SC2, GA2 = (8 * j for j in range(6))


LEAD = 1


class Ctx:

    def __init__(self, nc, stack, dram):
        self.nc, self.stack, self.dram = nc, stack, dram
        self.phase_sems = []
        self.big = stack.enter_context(nc.sbuf_tensor("memory", [P, 53200], F32))
        self.pt = [stack.enter_context(nc.psum_tensor(f"psum{i}", [P, 1024], F32)) for i in range(4)]
        self.RING, self.WST, self.Y, self.H, self.MX, self.MISC = 0, 24576, 32768, 37888, 43008, 48128
        self.ring = [self.at(self.RING + 4096 * s, 4096).rearrange("p (c n) -> p c n", c=KC) for s in range(6)]
        self.wst = [self.at(self.WST + 2048 * s, 2048).rearrange("p (c n) -> p c n", c=KC) for s in range(WSLOTS)]
        self.y = self.at(self.Y, 5120).rearrange("p (t n) -> p t n", t=TILES)
        self.h = self.at(self.H, 5120).rearrange("p (c n) -> p c n", c=KC)
        self.mx = self.at(self.MX, 5120).rearrange("p (c n) -> p c n", c=KC)
        self.ident = self.at(self.MISC, 128)
        self.perm = self.at(self.MISC + 128, 128)
        self.cols = self.at(self.MISC + 256, 126)
        self.mod = [self.at(self.MISC + 384 + 96 * l, 96).rearrange("p (c g) -> p c g", g=2) for l in range(DEPTH)]
        self.silu_c = self.at(self.MISC + 576, 16).rearrange("p (c g) -> p c g", g=2)
        self.scr = self.MISC + 592
        self.w_landed = [self.sem(f"w_landed{s}") for s in range(WSLOTS)]
        self.w_free = self.sem("w_free")
        self.w_seen = 0
        self.r_landed = [self.sem(f"ring_landed{s}") for s in range(6)]
        self.eps = LN_EPS
        self.r_free = self.sem("ring_free")
        self.phase_sems = []

    def at(self, start, size):
        return self.big[:, start:start + size]

    def sem(self, name):
        self.phase_sems.append(self.nc.alloc_semaphore(name))
        return self.phase_sems[-1]

    def clear(self):
        self.nc.all_engine_barrier()
        self.nc.clear_and_free_semaphores(self.phase_sems)
        self.phase_sems = []
        self.nc.all_engine_barrier()

    def bank(self, i):
        return self.pt[i // 2][:, (i % 2) * 512:(i % 2) * 512 + 512]


class Chain:

    def __init__(self, k, engine, name):
        self.sem, self.engine, self.n, self.base = k.sem(name), engine, 0, 0

    def enter(self, i, per):
        self.saved, self.per, self.n0 = self.n, per, self.n
        self.base, self.n = i * per + self.n, 0

    def leave(self, times):
        assert self.n == self.per, (self.n, self.per)
        self.n, self.base = self.saved + times * self.per, 0

    def link(self, instruction):
        instruction.then_inc(self.sem, 1)
        self.n += 1
        self.engine.wait_ge(self.sem, self.base + self.n)


def bcast_rows(ap, offset, dims):
    return bass.AP(tensor=ap.tensor, offset=offset, ap=[[0, P]] + dims)


def w_units(weight, first, count):
    v = weight.rearrange("(c p) (u n) -> u p c n", p=P, n=UNIT)
    return [v[u] for u in range(first, first + count)]


def feed(k, sp, number, source, reader=None):
    if reader:
        sp.wait_ge(*reader)
    sp.dma_start(k.wst[number % WSLOTS], source).then_inc(k.w_landed[number % WSLOTS], 16)


MOD_UNITS = 6 * D // UNIT
N_IN0, N_OUT, N_IN1 = 16, 4, 6
BASE_IN0 = MOD_UNITS
BASE_OUT0 = BASE_IN0 + N_IN0
BASE_IN1 = BASE_OUT0 + N_OUT
BASE_OUT1 = BASE_IN1 + N_IN1


def phase_modulation(k, a):
    nc = k.nc
    rows = k.at(k.scr, 128)
    mrows, bias = k.at(k.RING, 6 * D)[0:2], k.at(k.RING + 6 * D, 6 * D)[0:2]
    sc = k.silu_c
    consts_in, rows_in, x_in = k.sem("consts_in"), k.sem("rows_in"), k.sem("x_in")
    rows_turned, cols_ready, sc_ready = k.sem("rows_turned"), k.sem("cols_ready"), k.sem("sc_ready")
    LEAD = WSLOTS
    bias_in, row_ready, mod_turned, rows_out = (k.sem(n) for n in ("bias_in", "row_ready", "mod_turned", "mod_rows_out"))
    with nc.Block() as block:
        @block.sync
        def _(sp):
            sp.sem_inc(row_ready, LEAD)
            sp.dma_start(k.ident, a["ident"]).then_inc(consts_in, 16)
            sp.dma_start(k.perm, a["perm"]).then_inc(consts_in, 16)
            sp.dma_start(rows[ROW_BMOD:ROW_C], a["b_mod"].rearrange("l (r n) -> (l r) n", n=P)).then_inc(rows_in, 16)
            sp.dma_start(rows[ROW_C:ROW_CCTX], a["c"].rearrange("b (r n) -> (b r) n", n=P)).then_inc(rows_in, 16)
            sp.dma_start(rows[ROW_CCTX:ROW_LB], a["c_ctx"].rearrange("(r n) -> r n", n=P)).then_inc(rows_in, 16)
            sp.dma_start(rows[ROW_LB:ROW_HG],
                         a["hgrn_lb_logits"].rearrange("l (r n) -> (l r) n", n=P)).then_inc(rows_in, 16)
            sp.dma_start(rows[ROW_HG:ROW_DG], a["hgrn_norm_g"]).then_inc(rows_in, 16)
            sp.dma_start(rows[ROW_DG:N_ROWS], a["diff_norm_g"]).then_inc(rows_in, 16)
            for g in range(2):
                sp.dma_start(bias[g:g + 1], a["b_mod"][0:1]).then_inc(bias_in, 16)
            w = a["w_mod"][0].rearrange("(c p) (u n) -> u p c n", p=P, n=UNIT)
            for s in range(WSLOTS):
                feed(k, sp, s, w[s])
            with sp.Fori(1, MOD_UNITS // WSLOTS) as i:
                for s in range(WSLOTS):
                    sp.wait_ge(k.w_free, (i - 1) * WSLOTS + (s + 1))
                    sp.dma_start(k.wst[s], w[i * WSLOTS + s]).then_inc(k.w_landed[s], 16)
            for t in range(LAT_TILES):
                sp.dma_start(k.y[:, t, :], a["x_sample"][0, t * P:(t + 1) * P, :]).then_inc(x_in, 16)
            sp.dma_start(k.y[:, LAT_TILES, :], a["x_prompt"][0]).then_inc(x_in, 16)
            for s, unit in enumerate(in0_units(a)[:WSLOTS]):
                feed(k, sp, BASE_IN0 + s, unit, (k.w_free, MOD_UNITS - WSLOTS + s + 1))
            sp.wait_ge(row_ready, MOD_UNITS + LEAD)
            sp.dma_start(k.dram["mod_rows"][0], mrows).then_inc(rows_out, 16)
            sp.wait_ge(rows_out, 16)
            sp.wait_ge(x_in, 16 * TILES)

        @block.tensor
        def _(pe):
            pe.wait_ge(consts_in, 32)
            pe.wait_ge(rows_in, 96)
            nc.tensor.transpose(k.bank(1)[:, 0:N_ROWS], rows[0:N_ROWS, :], k.ident[0:N_ROWS, 0:N_ROWS]).then_inc(rows_turned, 1)
            pe.wait_ge(sc_ready, 1)
            with pe.Fori(0, MOD_UNITS // WSLOTS) as i:
                for s in range(WSLOTS):
                    pe.wait_ge(k.w_landed[s], i * 16 + 16)
                    pe.wait_ge(row_ready, i * WSLOTS + (s - WSLOTS + 1 + LEAD))
                    for c in range(KC):
                        last = nc.tensor.matmul(k.bank(2 + s)[0:2, 0:UNIT], sc[:, c, :], k.wst[s][:, c, :],
                                                start=(c == 0), stop=(c == KC - 1))
                    last.then_inc(k.w_free, 1)
            pe.wait_ge(row_ready, MOD_UNITS + LEAD)
            for r in range(48):
                last = nc.tensor.transpose(k.bank(0)[:, 2 * r:2 * r + 2], mrows[:, r * P:(r + 1) * P], k.ident[0:2, 0:2])
            last.then_inc(mod_turned, 1)

        @block.scalar
        def _(act):
            act.wait_ge(cols_ready, 1)
            nc.scalar.activation(sc, k.cols[:, ROW_C:ROW_LB].rearrange("p (g c) -> p c g", g=2),
                                 ACT.Silu).then_inc(sc_ready, 1)

        @block.vector
        def _(dve):
            chain = Chain(k, dve, "mod_dve")
            dve.wait_ge(rows_turned, 1)
            nc.vector.tensor_copy(k.cols, k.bank(1)[:, 0:N_ROWS]).then_inc(cols_ready, 1)
            dve.wait_ge(bias_in, 32)
            row_units, bias_units = (x.rearrange("p (u n) -> p u n", n=UNIT) for x in (mrows, bias))
            with dve.Fori(0, MOD_UNITS // WSLOTS) as i:
                for s in range(WSLOTS):
                    dve.wait_ge(k.w_free, i * WSLOTS + (s + 1))
                    nc.vector.tensor_tensor(row_units[:, i * WSLOTS + s, :], k.bank(2 + s)[0:2, 0:UNIT],
                                            bias_units[:, i * WSLOTS + s, :], ALU.add).then_inc(row_ready, 1)
            dve.wait_ge(mod_turned, 1)
            chain.link(nc.vector.tensor_copy(k.mod[0], k.bank(0)[:, 0:96].rearrange("p (c g) -> p c g", g=2)))
            for part in (SC1, SC2):
                nc.vector.tensor_scalar(k.mod[0][:, part:part + KC, :], k.mod[0][:, part:part + KC, :], 1.0, None, ALU.add)


def phase_modulate(k, l, shift, scale, tag):
    nc = k.nc
    turned, lat_out, ctx_out = k.sem(f"turned_{tag}"), k.sem(f"lat_out_{tag}"), k.sem(f"ctx_out_{tag}")
    with nc.Block() as block:
        @block.tensor
        def _(pe):
            for c in range(KC):
                if c >= 2:
                    pe.wait_ge(lat_out, c - 1)
                    pe.wait_ge(ctx_out, c - 1)
                for t in range(LAT_TILES):
                    nc.tensor.transpose(k.bank(c % 2)[:, t * P:(t + 1) * P], k.y[:, t, c * P:(c + 1) * P], k.ident)
                nc.tensor.transpose(k.bank(2 + c % 2)[:, 0:P], k.y[:, LAT_TILES, c * P:(c + 1) * P],
                                    k.ident).then_inc(turned, 1)

        @block.scalar
        def _(act):
            for c in range(KC):
                act.wait_ge(turned, c + 1)
                nc.scalar.activation(k.h[:, c, 0:NS], k.bank(c % 2), ACT.Identity,
                                     scale=k.mod[l][:, scale + c, 0:1], bias=k.mod[l][:, shift + c, 0:1]).then_inc(lat_out, 1)

        @block.vector
        def _(dve):
            for c in range(KC):
                dve.wait_ge(turned, c + 1)
                nc.vector.tensor_scalar(k.h[:, c, NS:NT], k.bank(2 + c % 2)[:, 0:P], k.mod[l][:, scale + c, 1:2],
                                        k.mod[l][:, shift + c, 1:2], ALU.mult, ALU.add).then_inc(ctx_out, 1)


IN0_ORDER = [0, 1, 2, 3, 4, 5, 8, 9, 10, 11, 12, 13, 6, 7, 14, 15]
CQ, CFF, CFB, CG, CQB, CKB = 0, 4, 8, 12, 16, 20


def in0_units(a):
    v = a["w_in_even"][0].rearrange("(c p) (u n) -> u p c n", p=P, n=UNIT)
    return [v[u] for u in IN0_ORDER]


def in1_units(a):
    return w_units(a["w_in_odd"][0], 0, N_IN1)


def project_feature_major(k, pe, w_slot, e, bank_lat, bank_ctx):
    nc = k.nc
    for c in range(KC):
        w = k.wst[w_slot][:, c, e * P:(e + 1) * P]
        nc.tensor.matmul(bank_lat, w, k.h[:, c, 0:NS], start=(c == 0), stop=(c == KC - 1))
        last = nc.tensor.matmul(bank_ctx, w, k.h[:, c, NS:NT], start=(c == 0), stop=(c == KC - 1))
    return last


def phase_project_even(k, a):
    nc = k.nc
    proj = k.at(k.RING, 24 * NT).rearrange("p (c n) -> p c n", n=NT)
    va = k.at(15360, 2560).rearrange("p (t n) -> p t n", t=TILES)
    vb = k.at(17920, 2560).rearrange("p (t n) -> p t n", t=TILES)
    kout = k.at(20480, 512)
    done, lat_out, ctx_out = k.sem("proj_done"), k.sem("proj_lat_out"), k.sem("proj_ctx_out")
    tok_done, tok_out, k_turned, kout_ready, stored = (
        k.sem(n) for n in ("ptok_done", "ptok_out", "k_turned", "kout_ready", "kv_stored"))
    b16 = BASE_IN0 // WSLOTS
    with nc.Block() as block:
        @block.sync
        def _(sp):
            for sem in (lat_out, ctx_out):
                sp.sem_inc(sem, LEAD)
            src = in0_units(a)
            for u in range(WSLOTS, N_IN0):
                feed(k, sp, BASE_IN0 + u, src[u], (done, 2 * (u - WSLOTS) + 2))
            sp.wait_ge(tok_out, 4 * TILES)
            sp.dma_start(a["out_diff_v"].rearrange("h t d -> t h d"),
                         vb[:, LAT_TILES, :].rearrange("p (h d) -> p h d", h=HEADS_B)).then_inc(stored, 16)
            sp.wait_ge(kout_ready, 1)
            sp.dma_start(a["out_diff_k"].rearrange("h t d -> t h d"),
                         kout.rearrange("p (h d) -> p h d", h=HEADS_B)).then_inc(stored, 16)
            sp.wait_ge(stored, 32)

        @block.tensor
        def _(pe):
            with pe.Fori(0, 3) as i:
                for s in range(WSLOTS):
                    pe.wait_ge(k.w_landed[s], i * 16 + 16 * (b16 + 1))
                    for e in range(2):
                        q = 2 * s + e
                        pe.wait_ge(lat_out, i * 8 + max(q - 1, 0) + LEAD)
                        pe.wait_ge(ctx_out, i * 8 + max(q - 1, 0) + LEAD)
                        last = project_feature_major(k, pe, s, e, k.bank(e), k.bank(2 + e)[:, 0:P])
                        last.then_inc(done, 1)
            for s in range(WSLOTS):
                pe.wait_ge(k.w_landed[s], 16 * (b16 + 4))
                for t in range(TILES):
                    g = s * TILES + t
                    if g >= 2:
                        pe.wait_ge(tok_out, g - 1)
                    for c in range(KC):
                        last = nc.tensor.matmul(k.bank(4 + g % 2)[:, 0:UNIT], k.h[:, c, t * P:(t + 1) * P],
                                                k.wst[s][:, c, :], start=(c == 0), stop=(c == KC - 1))
                    last.then_inc(tok_done, 1)
            pe.wait_ge(ctx_out, 24 + LEAD)
            for hd in range(HEADS_B):
                last = nc.tensor.transpose(k.bank(6)[:, hd * P:(hd + 1) * P], proj[:, CKB + hd, NS:NT], k.ident)
            last.then_inc(k_turned, 1)

        @block.scalar
        def _(act):
            with act.Fori(0, 3) as i:
                for q in range(8):
                    act.wait_ge(done, i * 8 + q + 1)
                    nc.scalar.copy(proj[:, i * 8 + q, 0:NS], k.bank(q % 2)).then_inc(lat_out, 1)

        @block.vector
        def _(dve):
            with dve.Fori(0, 3) as i:
                for q in range(8):
                    dve.wait_ge(done, i * 8 + q + 1)
                    nc.vector.tensor_copy(proj[:, i * 8 + q, NS:NT], k.bank(2 + q % 2)[:, 0:P]).then_inc(ctx_out, 1)
            for s in range(WSLOTS):
                for t in range(TILES):
                    g = s * TILES + t
                    dve.wait_ge(tok_done, g + 1)
                    dst = va if s < 2 else vb
                    nc.vector.tensor_copy(dst[:, t, (s % 2) * UNIT:(s % 2 + 1) * UNIT],
                                          k.bank(4 + g % 2)[:, 0:UNIT]).then_inc(tok_out, 1)
            dve.wait_ge(k_turned, 1)
            nc.vector.tensor_copy(kout, k.bank(6)).then_inc(kout_ready, 1)


def phase_hgrn(k, a):
    nc = k.nc
    MOD_HEAD = MOD_UNITS // HEADS_A
    MSLOTS = 3
    LEAD = MSLOTS
    halves_at = {-1: [0, 1, 2, 3], 0: [4], 1: [5], 2: [6], 3: [7], 4: [8], 5: [9], 6: [10], 7: [11]}
    stage = k.at(k.WST + 2048 * MSLOTS, MOD_HEAD * UNIT).rearrange("p (u n) -> p u n", n=UNIT)[0:2]
    proj = k.at(k.RING, 24 * NT).rearrange("p (c n) -> p c n", n=NT)
    va = k.at(15360, 2560).rearrange("p (t h n) -> p t h n", t=TILES, h=HEADS_A)
    NB = NT // CH

    class Dir:
        pass
    dirs = []
    for d, base in enumerate((k.H, 20480)):
        x = Dir()
        x.e, x.key, x.b, x.kdec, x.kend, x.qdec = (k.at(base + NT * j, NT) for j in range(6))
        x.qi, x.kh = x.key, x.b
        x.a = k.at(base + 6 * NT, NB)
        x.A, x.B = (0, 1) if d == 0 else (1, 0)
        x.end = SUB - 1 if d == 0 else 0
        x.tiles = [0, 1, 2, 3, 4] if d == 0 else [3, 2, 1, 0, 4]
        x.steps = [0, 1, 2, 3] if d == 0 else [3, 2, 1, 0]
        x.S = k.at(k.MX + 2560 + 1024 * d, 1024).rearrange("p (s n) -> p s n", s=8)
        x.S0 = k.at(k.MX + 2560 + 2048 + P * d, P)
        dirs.append(x)
    zero = k.at(k.MX + 2560 + 2304, P)
    ones = k.at(k.MX + 2560 + 2432, P)
    sig_g = k.at(k.H + 3860, NT)
    sc0 = k.scr
    keep = k.at(sc0, 641)
    masks = k.at(sc0 + 644, 384).bitcast(I32).rearrange("p (d n) -> p d n", d=2)
    vh = k.at(sc0 + 1028, NT).rearrange("p (t n) -> p t n", t=TILES)
    vblk = k.at(sc0 + 1668, 1024).rearrange("p (b j n) -> p b j n", b=2, j=4)
    scm = k.at(sc0 + 2692, 384).rearrange("p (b n) -> p b n", b=2)
    khT = k.at(sc0 + 3076, 256).rearrange("p (b n) -> p b n", b=2)
    bmask = k.at(sc0 + 3332, 4)
    lbx = k.at(sc0 + 3336, 12).rearrange("p (l h) -> p l h", h=4)
    lbm = k.at(sc0 + 3348, 4)
    lb, oml, lbs = k.at(sc0 + 3352, 4), k.at(sc0 + 3356, 4), k.at(sc0 + 3360, 4)
    lbe = k.at(sc0 + 3364, 12).rearrange("p (l h) -> p l h", h=4)

    names = ("h_const", "h_s0", "h_lbsub", "h_lbexp", "h_lb", "h_sig", "h_f", "h_ln", "h_scan", "h_exp", "h_sub",
             "h_kexp", "h_gates", "h_vh", "h_vblk", "h_sc", "h_and", "h_kt", "h_kht", "h_u", "h_upd", "h_pv",
             "h_inter", "h_state_out", "h_sq", "h_ms", "h_rstd", "h_fin", "h_zero", "h_m_landed0", "h_m_landed1", "h_m_landed2", "h_m_done", "h_m_row",
             "h_m_stored")
    S = {n[2:]: k.sem(n) for n in names}
    STEPS = 2 * TILES

    def halves(ap):
        return ap.rearrange("p (c h t) -> p c h t", h=2, t=SUB)

    def step(s):
        d = dirs[s % 2]
        return d, s % 2, s // 2, d.tiles[s // 2]

    def state_before(d, n, j):
        if j:
            return d.S[:, 4 * (n % 2) + j - 1, :]
        if n == 0:
            return d.S0
        if n == LAT_TILES:
            return zero
        return d.S[:, 4 * ((n - 1) % 2) + 3, :]

    with nc.Block() as block:
        @block.sync
        def _(sp):
            for name in ("m_done", "m_row", "m_stored", "inter", "u", "fin", "state_out", "pv", "and", "kht", "upd", "rstd"):
                sp.sem_inc(S[name], LEAD)
            sp.dma_start(keep, a["keep"]).then_inc(S["const"], 16)
            sp.dma_start(masks, a["hgrn_masks"]).then_inc(S["const"], 16)
            sp.dma_start(bmask, a["bmask"]).then_inc(S["const"], 16)
            wm = a["w_mod"][1].rearrange("(c p) (u n) -> u p c n", p=P, n=UNIT)
            raw = k.dram["mod_raw"].rearrange("g (h u n) -> h g u n", h=HEADS_A, n=UNIT)
            with sp.Fori(0, HEADS_A) as i:
                sp.wait_ge(S["inter"], STEPS * i + LEAD)
                for d in range(2):
                    sp.dma_start(dirs[d].S0, a["state_hgrn"][0, 0, d, i]).then_inc(S["s0"], 16)
                for x in range(MOD_HEAD):
                    sp.wait_ge(S["m_done"], i * MOD_HEAD + (x - MSLOTS + 1 + LEAD))
                    sp.dma_start(k.wst[x % MSLOTS], wm[i * MOD_HEAD + x]).then_inc(S[f"m_landed{x % MSLOTS}"], 16)
                sp.wait_ge(S["m_row"], i * MOD_HEAD + (MOD_HEAD + LEAD))
                sp.dma_start(raw[i], stage).then_inc(S["m_stored"], 16)
                sp.wait_ge(S["upd"], STEPS * i + STEPS + LEAD)
                for d in range(2):
                    sp.dma_start(a["out_state"][d, i], dirs[d].S[:, 3, :]).then_inc(S["state_out"], 16)
            sp.wait_ge(S["state_out"], 32 * HEADS_A + LEAD)
            sp.wait_ge(S["m_stored"], 16 * HEADS_A + LEAD)

        @block.gpsimd
        def _(pool):
            nc.gpsimd.memset(zero, 0.0).then_inc(S["zero"], 1)
            nc.gpsimd.memset(ones, 1.0 / P).then_inc(S["zero"], 1)
            pool.wait_ge(S["const"], 48)
            with pool.Fori(0, HEADS_A) as i:
                pool.wait_ge(S["inter"], STEPS * i + LEAD)
                nc.gpsimd.tensor_copy(vh, va[:, :, i, :]).then_inc(S["vh"], 1)
                pool.wait_ge(S["vh"], i + 1)
                for s in range(STEPS):
                    _, _, _, t = step(s)
                    pool.wait_ge(S["u"], STEPS * i + max(s - 1, 0) + LEAD)
                    nc.gpsimd.tensor_tensor(
                        vblk[:, s % 2], vh[:, t, :].rearrange("p (o n) -> p o n", o=1).broadcast_to([P, 4, P]),
                        bmask.rearrange("p (j o) -> p j o", o=1).broadcast_to([P, 4, P]), ALU.mult).then_inc(S["vblk"], 1)

        @block.scalar
        def _(act):
            act.wait_ge(S["lbsub"], 1)
            nc.scalar.activation(lbe, lbx, ACT.Exp).then_inc(S["lbexp"], 1)
            with act.Fori(0, HEADS_A) as i:
                act.wait_ge(S["fin"], i + LEAD)
                for d, x in enumerate(dirs):
                    z = proj[:, (CFF, CFB)[d] + i, :]
                    nc.scalar.activation(x.e, z, ACT.Sigmoid).then_inc(S["sig"], 1)
                    nc.scalar.activation(x.key, z, ACT.Sigmoid, scale=-1.0).then_inc(S["sig"], 1)
                nc.scalar.activation(sig_g, proj[:, CG + i, :], ACT.Sigmoid).then_inc(S["sig"], 1)
                for d, x in enumerate(dirs):
                    act.wait_ge(S["f"], 2 * i + d + 1)
                    nc.scalar.activation(x.e, x.e, ACT.Ln).then_inc(S["ln"], 1)
                for d, x in enumerate(dirs):
                    act.wait_ge(S["scan"], 2 * i + d + 1)
                    nc.scalar.activation(x.e, x.b, ACT.Exp).then_inc(S["exp"], 1)
                    nc.scalar.activation(x.kdec, x.b, ACT.Exp, scale=-1.0).then_inc(S["exp"], 1)
                    act.wait_ge(S["sub"], 2 * i + d + 1)
                    nc.scalar.activation(x.kend, x.kend, ACT.Exp).then_inc(S["kexp"], 1)
                for s in range(STEPS):
                    act.wait_ge(S["kt"], STEPS * i + s + 1)
                    act.wait_ge(S["u"], STEPS * i + max(s - 1, 0) + LEAD)
                    nc.scalar.copy(khT[:, s % 2, :], k.bank(4)[:, 0:P]).then_inc(S["kht"], 1)
                act.wait_ge(S["inter"], STEPS * i + STEPS + LEAD)
                ob, sq = dirs[0].e, dirs[1].e
                nc.scalar.copy(ob[:, 0:NS], k.bank(0))
                nc.scalar.copy(ob[:, NS:NT], k.bank(1)[:, 0:P])
                nc.scalar.activation(sq[:, 0:NS], k.bank(0), ACT.Square)
                nc.scalar.activation(sq[:, NS:NT], k.bank(1)[:, 0:P], ACT.Square).then_inc(S["sq"], 1)
                act.wait_ge(S["ms"], i + 1)
                act.wait_ge(S["sq"], i + 1)
                rs = dirs[1].qdec
                nc.scalar.activation(rs[:, 0:NS], k.bank(2), ACT.Ln, bias=k.eps).then_inc(S["rstd"], 1)
                nc.scalar.activation(rs[:, NS:NT], k.bank(3)[:, 0:P], ACT.Ln, bias=k.eps).then_inc(S["rstd"], 1)
                act.wait_ge(S["rstd"], 3 * i + 2 + LEAD)
                nc.scalar.activation(rs, rs, ACT.Exp, scale=-0.5).then_inc(S["rstd"], 1)

        @block.vector
        def _(dve):
            c = Chain(k, dve, "hgrn_dve")
            lg = k.cols[:, ROW_LB:ROW_HG].rearrange("p (l h) -> p l h", h=4)
            c.link(nc.vector.tensor_tensor(lbm, lg[:, 0, :], lg[:, 1, :], ALU.max))
            c.link(nc.vector.tensor_tensor(lbm, lbm, lg[:, 2, :], ALU.max))
            for r in range(3):
                last = nc.vector.tensor_tensor(lbx[:, r, :], lg[:, r, :], lbm, ALU.subtract)
            last.then_inc(S["lbsub"], 1)
            dve.wait_ge(S["lbexp"], 1)
            c.link(nc.vector.tensor_tensor(lbs, lbe[:, 0, :], lbe[:, 1, :], ALU.add))
            c.link(nc.vector.tensor_tensor(lbs, lbs, lbe[:, 2, :], ALU.add))
            c.link(nc.vector.reciprocal(lbs, lbs))
            c.link(nc.vector.tensor_tensor(lb, lbe[:, 0, :], lbs, ALU.mult))
            c.link(nc.vector.tensor_scalar(oml, lb, -1.0, 1.0, ALU.mult, ALU.add))
            dve.wait_ge(S["const"], 48)
            dve.wait_ge(S["zero"], 2)
            with dve.Fori(0, HEADS_A) as i:
                c.enter(i, 3 * STEPS + 4)
                dve.wait_ge(S["m_stored"], 16 * i + LEAD)

                def modulation_row(x):
                    dve.wait_ge(S["m_done"], i * MOD_HEAD + (x + 1 + LEAD))
                    nc.vector.tensor_copy(stage[:, x, :], k.bank(5)[0:2, 0:UNIT]).then_inc(S["m_row"], 1)

                for half in halves_at[-1]:
                    if half % 2:
                        modulation_row(half // 2)
                for d, x in enumerate(dirs):
                    dve.wait_ge(S["sig"], 5 * i + 2 * d + 2)
                    nc.vector.tensor_scalar(x.e, x.e, oml[:, bass.ds(i, 1)], lb[:, bass.ds(i, 1)], ALU.mult, ALU.add).then_inc(S["f"], 1)
                    nc.vector.tensor_scalar(x.key, x.key, oml[:, bass.ds(i, 1)], None, ALU.mult)
                for d, x in enumerate(dirs):
                    dve.wait_ge(S["ln"], 2 * i + d + 1)
                    if d == 0:
                        op = nc.vector.tensor_tensor_scan(x.b, keep[:, 0:NT], x.e, 0.0, ALU.mult, ALU.add)
                    else:
                        op = nc.vector.tensor_tensor_scan(x.b[:, ::-1], keep[:, 1:NT + 1][:, ::-1], x.e[:, ::-1],
                                                          0.0, ALU.mult, ALU.add)
                    op.then_inc(S["scan"], 1)
                    dve.wait_ge(S["scan"], 2 * i + d + 1)
                    b3 = x.b.rearrange("p (c t) -> p c t", t=SUB)
                    nc.vector.tensor_tensor(x.kend.rearrange("p (c t) -> p c t", t=SUB),
                                            b3[:, :, x.end:x.end + 1].broadcast_to([P, NT // SUB, SUB]), b3,
                                            ALU.subtract).then_inc(S["sub"], 1)
                for d, x in enumerate(dirs):
                    dve.wait_ge(S["exp"], 4 * i + 2 * d + 2)
                    nc.vector.tensor_tensor(x.qdec, proj[:, CQ + i, :], x.e, ALU.mult)
                    nc.vector.tensor_tensor(x.kdec, x.kdec, x.key, ALU.mult)
                    dve.wait_ge(S["kexp"], 2 * i + d + 1)
                    c.link(nc.vector.tensor_tensor(x.kend, x.kend, x.key, ALU.mult))
                    e4, q4, qi4, ke4, kh4 = (halves(v) for v in (x.e, x.qdec, x.qi, x.kend, x.kh))
                    endA = e4[:, :, x.A, x.end:x.end + 1]
                    endB = e4[:, :, x.B, x.end:x.end + 1]
                    nc.vector.tensor_copy(qi4[:, :, x.A, :], q4[:, :, x.A, :])
                    nc.vector.tensor_tensor(qi4[:, :, x.B, :], q4[:, :, x.B, :], endA.broadcast_to([P, NB, SUB]), ALU.mult)
                    nc.vector.tensor_copy(kh4[:, :, x.B, :], ke4[:, :, x.B, :])
                    nc.vector.tensor_tensor(kh4[:, :, x.A, :], ke4[:, :, x.A, :], endB.broadcast_to([P, NB, SUB]), ALU.mult)
                    nc.vector.tensor_tensor(x.a.rearrange("p (c o) -> p c o", o=1), endA, endB,
                                            ALU.mult).then_inc(S["gates"], 1)
                dve.wait_ge(S["s0"], 32 * i + 32)
                dve.wait_ge(S["state_out"], 32 * i + LEAD)
                dve.wait_ge(S["gates"], 2 * i + 2)
                for s in range(STEPS):
                    x, dn, n, t = step(s)
                    dve.wait_ge(S["sc"], STEPS * i + s + 1)
                    dve.wait_ge(S["pv"], STEPS * i + max(s - 1, 0) + LEAD)
                    nc.vector.tensor_tensor(scm[:, s % 2, :].bitcast(I32), k.bank(2 + s % 2)[:, 0:192].bitcast(I32),
                                            masks[:, dn, :], ALU.bitwise_and).then_inc(S["and"], 1)
                    dve.wait_ge(S["u"], STEPS * i + s + 1 + LEAD)
                    dve.wait_ge(S["inter"], STEPS * i + max(s - 3, 0) + LEAD)
                    for j, m in enumerate(x.steps):
                        op = nc.vector.scalar_tensor_tensor(
                            out=x.S[:, 4 * (n % 2) + j, :], in0=state_before(x, n, j),
                            scalar=x.a[:, 4 * t + m:4 * t + m + 1], in1=k.bank(6 + s % 2)[:, m * P:(m + 1) * P],
                            op0=ALU.mult, op1=ALU.add)
                        if j == 3:
                            op.then_inc(S["upd"], 1)
                            dve.wait_ge(S["upd"], STEPS * i + s + 1 + LEAD)
                        else:
                            c.link(op)
                    for half in (halves_at.get(s - 1, []) if s else []):
                        if half % 2:
                            modulation_row(half // 2)
                ob, rs = dirs[0].e, dirs[1].qdec
                dve.wait_ge(S["rstd"], 3 * i + 3 + LEAD)
                dve.wait_ge(S["sq"], i + 1)
                dve.wait_ge(S["sig"], 5 * i + 5)
                c.link(nc.vector.scalar_tensor_tensor(out=ob, in0=ob, scalar=k.cols[:, ROW_HG:ROW_HG + 1], in1=rs,
                                                      op0=ALU.mult, op1=ALU.mult))
                c.link(nc.vector.tensor_tensor(ob, ob, sig_g, ALU.mult))
                nc.vector.tensor_tensor(k.mx[:, i, :], ob, proj[:, CG + i, :], ALU.mult).then_inc(S["fin"], 1)
                c.leave(HEADS_A)

        @block.tensor
        def _(pe):
            pe.wait_ge(S["zero"], 2)
            with pe.Fori(0, HEADS_A) as i:
                def before(s):
                    x, dn, n, t = step(s)
                    tile = slice(t * P, (t + 1) * P)
                    if s < 2:
                        pe.wait_ge(S["gates"], 2 * i + s + 1)
                    pe.wait_ge(S["and"], STEPS * i + max(s - 1, 0) + LEAD)
                    nc.tensor.matmul(k.bank(2 + s % 2)[:, 0:P], x.kdec[:, tile], x.qdec[:, tile], start=True, stop=True)
                    qB = halves(x.qdec)[:, 4 * t:4 * t + 4, x.B, :]
                    nc.tensor.matmul(k.bank(2 + s % 2)[:, P:192], x.kend[:, tile], qB,
                                     start=True, stop=True).then_inc(S["sc"], 1)
                    pe.wait_ge(S["kht"], STEPS * i + s + LEAD)
                    nc.tensor.transpose(k.bank(4)[:, 0:P], x.kh[:, tile], k.ident).then_inc(S["kt"], 1)

                def after(s):
                    x, dn, n, t = step(s)
                    pe.wait_ge(S["kht"], STEPS * i + s + 1 + LEAD)
                    pe.wait_ge(S["vblk"], STEPS * i + s + 1)
                    pe.wait_ge(S["upd"], STEPS * i + max(s - 1, 0) + LEAD)
                    nc.tensor.matmul(k.bank(6 + s % 2), khT[:, s % 2, :], vblk[:, s % 2].rearrange("p j n -> p (j n)"),
                                     start=True, stop=True).then_inc(S["u"], 1)
                    pe.wait_ge(S["and"], STEPS * i + s + 1 + LEAD)
                    o = k.bank(0) if t < LAT_TILES else k.bank(1)[:, 0:P]
                    c0 = t * P if t < LAT_TILES else 0
                    nc.tensor.matmul(o[:, c0:c0 + P], vh[:, t, :], scm[:, s % 2, 0:P], start=(s in (0, 8)), stop=False,
                                     skip_group_check=True)
                    oB = o[:, c0:c0 + P].rearrange("p (c h t) -> p c h t", h=2, t=SUB)[:, :, x.B, :]
                    nc.tensor.matmul(oB, vh[:, t, :], scm[:, s % 2, P:192], start=False, stop=False,
                                     skip_group_check=True).then_inc(S["pv"], 1)
                    pe.wait_ge(S["upd"], STEPS * i + s + 1 + LEAD)
                    for j, m in enumerate(x.steps):
                        cols = slice(t * P + m * CH, t * P + (m + 1) * CH)
                        last = nc.tensor.matmul(o[:, c0 + m * CH:c0 + (m + 1) * CH], state_before(x, n, j), x.qi[:, cols],
                                                start=False, stop=(s >= STEPS - 3 and j == 3), skip_group_check=True)
                    last.then_inc(S["inter"], 1)

                def modulation(half):
                    x, part = divmod(half, 2)
                    if part == 0:
                        pe.wait_ge(S[f"m_landed{x % MSLOTS}"], i * 32 + 16 * (x // MSLOTS + 1))
                        pe.wait_ge(S["m_row"], i * MOD_HEAD + (x + LEAD))
                    for c in range(4 * part, 4 * part + 4):
                        last = nc.tensor.matmul(k.bank(5)[0:2, 0:UNIT], k.silu_c[:, c, :], k.wst[x % MSLOTS][:, c, :],
                                                start=(c == 0), stop=(c == KC - 1))
                    if part:
                        last.then_inc(S["m_done"], 1)

                for half in halves_at[-1]:
                    modulation(half)
                pe.wait_ge(S["fin"], i + LEAD)
                pe.wait_ge(S["rstd"], 3 * i + LEAD)
                before(0)
                pe.wait_ge(S["vh"], i + 1)
                for s in range(STEPS):
                    if s + 1 < STEPS:
                        before(s + 1)
                    after(s)
                    for half in halves_at.get(s, []):
                        modulation(half)
                pe.wait_ge(S["sq"], i + 1)
                sq = dirs[1].e
                nc.tensor.matmul(k.bank(2), ones, sq[:, 0:NS], start=True, stop=True)
                nc.tensor.matmul(k.bank(3)[:, 0:P], ones, sq[:, NS:NT], start=True, stop=True).then_inc(S["ms"], 1)


def phase_project_odd(k, a):
    nc = k.nc
    proj = k.at(k.RING, 10 * NT).rearrange("p (c n) -> p c n", n=NT)
    v = k.at(6400, 1280).rearrange("p (t n) -> p t n", t=TILES)
    kout = k.at(7680, 256)
    done, lat_out, ctx_out = k.sem("oproj_done"), k.sem("oproj_lat_out"), k.sem("oproj_ctx_out")
    tok_done, tok_out, k_turned, kout_ready, stored = (
        k.sem(n) for n in ("otok_done", "otok_out", "ok_turned", "okout_ready", "okv_stored"))
    with nc.Block() as block:
        @block.sync
        def _(sp):
            for u, s in enumerate(in1_units(a)):
                if u >= WSLOTS:
                    feed(k, sp, BASE_IN1 + u, s, (done, 2 * (u - WSLOTS) + 2))
            for u, s in enumerate(w_units(a["w_out_odd"][0], 0, 4)):
                feed(k, sp, BASE_OUT1 + u, s, (done, 2 * (u + 2) + 2) if u < 3 else (tok_done, TILES))
            sp.wait_ge(tok_out, TILES)
            sp.dma_start(a["out_win_v"].rearrange("h t d -> t h d"),
                         v[:, LAT_TILES, :].rearrange("p (h d) -> p h d", h=4)).then_inc(stored, 16)
            sp.wait_ge(kout_ready, 1)
            sp.dma_start(a["out_win_k"].rearrange("h t d -> t h d"),
                         kout.rearrange("p (h d) -> p h d", h=4)).then_inc(stored, 16)
            sp.wait_ge(stored, 32)

        @block.tensor
        def _(pe):
            for u in range(N_IN1):
                n = BASE_IN1 + u
                pe.wait_ge(k.w_landed[n % WSLOTS], 16 * (n // WSLOTS + 1))
                if u < 5:
                    for e in range(2):
                        q = 2 * u + e
                        if q >= 2:
                            pe.wait_ge(lat_out, q - 1)
                            pe.wait_ge(ctx_out, q - 1)
                        last = project_feature_major(k, pe, n % WSLOTS, e, k.bank(e), k.bank(2 + e)[:, 0:P])
                        last.then_inc(done, 1)
                else:
                    for t in range(TILES):
                        if t >= 2:
                            pe.wait_ge(tok_out, t - 1)
                        for c in range(KC):
                            last = nc.tensor.matmul(k.bank(4 + t % 2)[:, 0:UNIT], k.h[:, c, t * P:(t + 1) * P],
                                                    k.wst[n % WSLOTS][:, c, :], start=(c == 0), stop=(c == KC - 1))
                        last.then_inc(tok_done, 1)
            pe.wait_ge(ctx_out, 10)
            for c in range(2):
                last = nc.tensor.transpose(k.bank(6)[:, c * P:(c + 1) * P], proj[:, 8 + c, NS:NT], k.ident)
            last.then_inc(k_turned, 1)

        @block.scalar
        def _(act):
            for q in range(10):
                act.wait_ge(done, q + 1)
                nc.scalar.copy(proj[:, q, 0:NS], k.bank(q % 2)).then_inc(lat_out, 1)

        @block.vector
        def _(dve):
            for q in range(10):
                dve.wait_ge(done, q + 1)
                nc.vector.tensor_copy(proj[:, q, NS:NT], k.bank(2 + q % 2)[:, 0:P]).then_inc(ctx_out, 1)
            for t in range(TILES):
                dve.wait_ge(tok_done, t + 1)
                nc.vector.tensor_copy(v[:, t, :], k.bank(4 + t % 2)[:, 0:UNIT]).then_inc(tok_out, 1)
            dve.wait_ge(k_turned, 1)
            nc.vector.tensor_copy(kout, k.bank(6)[:, 0:UNIT]).then_inc(kout_ready, 1)


def phase_rope(k, a, odd):
    nc = k.nc
    tag = "o" if odd else "e"
    proj = k.at(k.RING, (10 if odd else 24) * NT).rearrange("p (c n) -> p c n", n=NT)
    first, count = (0, 10) if odd else (CQB, 8)
    nk = 2 if odd else 4
    cos, sin = k.at(k.scr, 512), k.at(k.scr + 512, 512)
    straight = k.at(k.H, 1024).rearrange("p (b n) -> p b n", b=2)
    kctx = k.at(k.H + 1024, 1024).rearrange("p (c n) -> p c n", n=PAST)
    kraw = k.at(20480, 2 * nk * P).rearrange("p (c t n) -> p c t n", t=2, n=P)
    loaded, kraw_in, turned, swapped, mixed, multiplied, summed, kctx_out = (
        k.sem(f"rope_{n}_{tag}") for n in ("loaded", "kraw_in", "turned", "swapped", "mixed", "multiplied", "summed",
                                           "kctx_out"))
    raw, cols96, rows96 = k.at(k.H + 2048, P)[0:96], k.at(k.H + 2176, 96), k.at(k.H + 2272, P)[0:96]
    raw_in, raw_turned, biased, rows_turned, rows_ready, rows_out = (
        k.sem(f"rope_{n}_{tag}") for n in ("raw_in", "raw_turned", "biased", "mrows_turned", "mrows_ready", "mrows_out"))
    with nc.Block() as block:
        @block.sync
        def _(sp):
            for sem in (multiplied, summed):
                sp.sem_inc(sem, LEAD)
            sp.dma_start(cos, a["cos"]).then_inc(loaded, 16)
            sp.dma_start(sin, a["sin"]).then_inc(loaded, 16)
            for c in range(nk):
                for t in range(2):
                    if odd:
                        src = a["cache_win_k"][0, 0, 2 * c:2 * c + 2, t * P:(t + 1) * P, :].rearrange("h t d -> t h d")
                        dst = kraw[:, c, t, :].rearrange("p (h d) -> p h d", h=2)
                    else:
                        src, dst = a["cache_diff_k"][0, 0, c, t * P:(t + 1) * P, :], kraw[:, c, t, :]
                    sp.dma_start(dst, src).then_inc(kraw_in, 16)
            if not odd:
                sp.dma_start(raw, k.dram["mod_raw"].rearrange("g (c n) -> (g c) n", n=P)).then_inc(raw_in, 16)
                sp.wait_ge(rows_ready, 1)
                sp.dma_start(k.dram["mod_rows"][1].rearrange("g (c n) -> (g c) n", n=P), rows96).then_inc(rows_out, 16)
                sp.wait_ge(rows_out, 16)

        @block.tensor
        def _(pe):
            with pe.Fori(0, count // 2) as i:
                for b in range(2):
                    pe.wait_ge(multiplied, 2 * i + 0 + LEAD)
                    nc.tensor.matmul(k.bank(b), k.perm, proj[:, first + i * 2 + b, 0:NS],
                                     start=True, stop=True).then_inc(swapped, 1)
            pe.wait_ge(kraw_in, 32 * nk)
            for c in range(nk):
                for t in range(2):
                    last = nc.tensor.transpose(k.bank(4 + c // 2)[:, (c % 2) * PAST + t * P:(c % 2) * PAST + (t + 1) * P],
                                               kraw[:, c, t, :], k.ident)
            last.then_inc(turned, 1)
            if not odd:
                pe.wait_ge(raw_in, 16)
                nc.tensor.transpose(k.bank(6)[:, 0:96], raw, k.ident[0:96, 0:96]).then_inc(raw_turned, 1)
                pe.wait_ge(biased, 1)
                nc.tensor.transpose(k.bank(7)[0:96, 0:P], cols96, k.ident).then_inc(rows_turned, 1)

        @block.gpsimd
        def _(pool):
            pool.wait_ge(loaded, 32)
            with pool.Fori(0, count // 2) as i:
                for b in range(2):
                    pool.wait_ge(summed, 2 * i + LEAD)
                    nc.gpsimd.tensor_tensor(straight[:, b, :], proj[:, first + i * 2 + b, 0:NS], cos,
                                            ALU.mult).then_inc(mixed, 1)

        @block.vector
        def _(dve):
            dve.wait_ge(loaded, 32)
            with dve.Fori(0, count // 2) as i:
                for b in range(2):
                    x = proj[:, first + i * 2 + b, 0:NS]
                    dve.wait_ge(swapped, 2 * i + b + 1)
                    dve.wait_ge(mixed, 2 * i + b + 1)
                    nc.vector.tensor_tensor(x, k.bank(b), sin, ALU.mult).then_inc(multiplied, 1)
                    dve.wait_ge(multiplied, 2 * i + b + 1 + LEAD)
                    nc.vector.tensor_tensor(x, x, straight[:, b, :], ALU.add).then_inc(summed, 1)
            dve.wait_ge(turned, 1)
            for c in range(nk):
                nc.vector.tensor_copy(kctx[:, c, :], k.bank(4 + c // 2)[:, (c % 2) * PAST:(c % 2 + 1) * PAST])
            if not odd:
                gc, cg = "p (g c) -> p g c", "p (g c) -> p c g"
                dve.wait_ge(raw_turned, 1)
                nc.vector.tensor_tensor(cols96.rearrange(gc, g=2), k.bank(6)[:, 0:96].rearrange(gc, g=2),
                                        k.cols[:, 48:96].rearrange("p (o c) -> p o c", o=1).broadcast_to([P, 2, 48]),
                                        ALU.add).then_inc(biased, 1)
                dve.wait_ge(biased, 1)
                nc.vector.tensor_copy(k.mod[1], cols96.rearrange(cg, g=2)).then_inc(biased, 1)
                dve.wait_ge(biased, 2)
                for part in (SC1, SC2):
                    nc.vector.tensor_scalar(k.mod[1][:, part:part + KC, :], k.mod[1][:, part:part + KC, :], 1.0, None,
                                            ALU.add)
                dve.wait_ge(rows_turned, 1)
                nc.vector.tensor_copy(rows96, k.bank(7)[0:96, 0:P]).then_inc(rows_ready, 1)


def phase_attention(k, a, odd):
    nc = k.nc
    tag = "o" if odd else "e"
    ITER = 8 if odd else HEADS_B
    proj = k.at(k.RING, (10 if odd else 24) * NT).rearrange("p (c n) -> p c n", n=NT)
    kctx = k.at(k.H + 1024, 1024).rearrange("p (c n) -> p c n", n=PAST)
    qr = k.at(k.H + 2048, 2 * NT).rearrange("p (b n) -> p b n", b=2)
    free = 10240 if odd else 0
    kr = k.at(free, 2 * NT).rearrange("p (b n) -> p b n", b=2)
    kcr = k.at(free + 2 * NT, 2 * PAST).rearrange("p (b n) -> p b n", b=2)
    ob = k.at(k.H + 3328, NT).rearrange("p (t n) -> p t n", t=TILES)
    small = k.H + 3968
    negm = k.at(small, 10)
    rsum = k.at(small + 10, 10)
    rinv = k.at(small + 20, 10)
    top = k.at(small + 30, 10)
    esink = k.at(small + 40, 10)
    ssq = k.at(small + 50, 5)
    rstd = k.at(small + 55, 5)
    neglam = k.at(small + 60, 1)
    dots = k.at(small + 61, 2)
    gdiff = k.at(small + 63, 1)
    lamx = k.at(small + 64, 256).rearrange("p (j n) -> p j n", j=4)
    sink = k.at(small + 320, 16)
    t2 = k.at(small + 336, P)
    junk = k.at(small + 464, P)
    tick = k.at(small + 592, 1)
    sinkc = k.at(small + 594, 4).rearrange("p (b n) -> p b n", b=2)
    prob = k.at(k.scr + 1024, 1536).rearrange("p (b n) -> p b n", b=2)
    probT = k.at(k.scr + 2560, 1536).rearrange("p (b n) -> p b n", b=2)
    if odd:
        vlat = k.at(6400, 1280).rearrange("p (t h n) -> p t h n", t=TILES, h=4)
        vctx = k.at(8192, 512).rearrange("p (t h n) -> p t h n", t=2, h=4)
        mask = k.at(8704, 768)
    else:
        vlat = k.at(17920, 2560).rearrange("p (t h n) -> p t h n", t=TILES, h=4)
        vctx = k.at(20480, 1024).rearrange("p (t h n) -> p t h n", t=2, h=4)
    S = {n: k.sem(f"at_{n}_{tag}") for n in ("v_in", "dots", "lam", "lam_ready", "q_in", "qk", "max", "small", "exp", "esink",
                                             "pt", "outd", "outa", "pv", "comb", "fold", "ssq", "rstd", "norm", "turned", "stored")}
    UN = 2 * TILES
    QIN = 4 if odd else 3

    def unit(u):
        t, m = divmod(u, 2)
        if t == LAT_TILES:
            return (t, m, 256, 384) if odd else (t, m, 0, P)
        if odd:
            return t, m, (128 if t else 256), (768 if t < LAT_TILES - 1 else 640)
        return t, m, 0, 768

    def key_tiles(t):
        if t == LAT_TILES:
            return [("own", LAT_TILES)]
        if not odd:
            return [("ctx", 0), ("ctx", 1)] + [("own", j) for j in range(LAT_TILES)]
        return ([("own", t - 1)] if t else []) + [("ctx", 0), ("ctx", 1), ("own", t)] + (
            [("own", t + 1)] if t < LAT_TILES - 1 else [])

    def split(u):
        t, m, lo, hi = unit(u)
        n = (hi - lo) // P
        return n, max(n // 2, 1)

    def outa(i, u):
        return i * (UN - 2) + min(u, UN - 2)

    with nc.Block() as block:
        @block.sync
        def _(sp):
            for name in ("qk", "exp", "max", "outd", "outa", "pv", "comb", "pt"):
                sp.sem_inc(S[name], LEAD)
            for t in range(2):
                src = a["cache_win_v" if odd else "cache_diff_v"][0, 0, :, t * P:(t + 1) * P, :].rearrange("h t d -> t h d")
                sp.dma_start(vctx[:, t], src).then_inc(S["v_in"], 16)
            if not odd:
                for u, s in enumerate(w_units(a["w_out_even"][0], 0, 4)):
                    feed(k, sp, BASE_OUT0 + u, s)
            if odd:
                sp.dma_start(sink, bcast_rows(a["win_sink"], 0, [[1, 16]])).then_inc(S["v_in"], 16)
                sp.dma_start(mask, a["wmask"]).then_inc(S["v_in"], 16)
            else:
                sp.dma_start(lamx, bcast_rows(a["diff_lambda"], 0, [[DH, 4], [1, DH]])).then_inc(S["v_in"], 16)

        @block.gpsimd
        def _(pool):
            if odd:
                pool.wait_ge(S["v_in"], 64)
            with pool.Fori(0, ITER // 2) as i:
                for b in range(2):
                    pool.wait_ge(S["qk"], 2 * UN * i + LEAD)
                    chunk = (0 if odd else CQB) + i * 2 + b
                    kchunk = i // 2 if odd else i * 2 + b
                    nc.gpsimd.tensor_copy(qr[:, b, :], proj[:, chunk, :]).then_inc(S["q_in"], 1)
                    nc.gpsimd.tensor_copy(kr[:, b, :], proj[:, (8 if odd else CKB) + kchunk, :]).then_inc(S["q_in"], 1)
                    nc.gpsimd.tensor_copy(kcr[:, b, :], kctx[:, kchunk, :]).then_inc(S["q_in"], 1)
                    if odd:
                        pool.wait_ge(S["exp"], 2 * UN * i + LEAD)
                        nc.gpsimd.tensor_copy(sinkc[:, b, :], sink[:, bass.ds(4 * i + 2 * b, 2)]).then_inc(S["q_in"], 1)

        @block.tensor
        def _(pe):
            pe.wait_ge(S["v_in"], 64 if odd else 48)
            with pe.Fori(0, ITER // 2) as i2:
                for b in range(2):
                    i = i2 * 2 + b
                    N = i * UN
                    if odd:
                        kchunk = i2 // 2
                    else:
                        kchunk = i

                    def qk(u):
                        t, m, lo, hi = unit(u)
                        rows = slice(DH * m, DH * m + DH)
                        q = qr[rows, b, t * P:(t + 1) * P]
                        dst = k.pt[m]
                        pe.wait_ge(S["max" if odd else "exp"], N + max(u - 1, 0) + LEAD)
                        keys = kr[rows, b]

                        def put(col, cols, rhs):
                            return nc.tensor.matmul(dst[:, col:col + cols], q, rhs, start=True, stop=True)
                        if t == LAT_TILES:
                            last = put(lo, P, keys[:, NS:NT])
                        elif odd:
                            if t:
                                put(128, P, keys[:, (t - 1) * P:t * P])
                            put(256, PAST, kcr[rows, b, :])
                            last = put(512, hi - 512, keys[:, t * P:t * P + hi - 512])
                        else:
                            put(0, PAST, kcr[rows, b, :])
                            put(256, 256, keys[:, 0:256])
                            last = put(512, 256, keys[:, 256:512])
                        last.then_inc(S["qk"], 1)

                    def turn(u):
                        t, m, lo, hi = unit(u)
                        pe.wait_ge(S["exp"], N + u + 1 + LEAD)
                        pe.wait_ge(S["outd"], N + u + LEAD)
                        pe.wait_ge(S["outa"], outa(i, u) + LEAD)
                        n, h = split(u)
                        for j in range(n):
                            dst = k.bank(4)[:, j * P:(j + 1) * P] if j < h else k.bank(5)[:, (j - h) * P:(j - h + 1) * P]
                            last = nc.tensor.transpose(dst, prob[:, u % 2, j * P:(j + 1) * P], k.ident)
                        last.then_inc(S["pt"], 1)

                    def pv(u):
                        t, m, lo, hi = unit(u)
                        pe.wait_ge(S["outd"], N + u + 1 + LEAD)
                        pe.wait_ge(S["outa"], outa(i, u + 1) + LEAD)
                        pe.wait_ge(S["comb"], N + (u if m == 0 and not odd else max(u - 1, 0)) + LEAD)
                        tiles = key_tiles(t)
                        for j, (kind, vt) in enumerate(tiles):
                            if odd:
                                v = (vctx if kind == "ctx" else vlat)[:, vt, kchunk * 2 + m, :]
                                o = k.bank(6 + m)[:, 0:DH]
                            else:
                                v = (vctx if kind == "ctx" else vlat)[:, vt, kchunk, :]
                                o = k.bank(6 + m)[:, 0:P]
                            last = nc.tensor.matmul(o, probT[:, u % 2, j * P:(j + 1) * P], v, start=(j == 0),
                                                    stop=(j == len(tiles) - 1))
                        last.then_inc(S["pv"], 1)

                    pe.wait_ge(S["q_in"], QIN * i + QIN)
                    qk(0)
                    for u in range(UN):
                        if u + 1 < UN:
                            qk(u + 1)
                        turn(u)
                        if u:
                            pv(u - 1)
                    pv(UN - 1)
                    if odd:
                        pe.wait_ge(S["comb"], N + UN + LEAD)
                    else:
                        pe.wait_ge(S["norm"], i + 1)
                    for t in range(TILES):
                        last = nc.tensor.transpose(k.pt[2][:, t * P:(t + 1) * P], ob[:, t, :], k.ident)
                    last.then_inc(S["turned"], 1)
                    pe.wait_ge(S["stored"], i + 1)

        @block.scalar
        def _(act):
            if not odd:
                act.wait_ge(S["dots"], 2)
                nc.scalar.activation(dots, dots, ACT.Exp).then_inc(S["lam"], 1)
            else:
                act.wait_ge(S["v_in"], 64)
            with act.Fori(0, ITER // 2) as i2:
                for b in range(2):
                    i = i2 * 2 + b
                    N = i * UN

                    def evacuate(u):
                        n, h = split(u)
                        if n > h:
                            act.wait_ge(S["pt"], N + u + 1 + LEAD)
                            act.wait_ge(S["pv"], N + max(u - 1, 0) + LEAD)
                            nc.scalar.copy(probT[:, u % 2, h * P:n * P], k.bank(5)[:, 0:(n - h) * P]).then_inc(S["outa"], 1)

                    if odd:
                        act.wait_ge(S["q_in"], QIN * i + QIN)
                    for u in range(UN):
                        t, m, lo, hi = unit(u)
                        act.wait_ge(S["max"], N + u + 1 + LEAD)
                        act.wait_ge(S["small"], N + u + 1)
                        act.wait_ge(S["pt"], N + max(u - 1, 0) + LEAD)
                        if odd:
                            nc.scalar.activation(esink[:, u:u + 1], sinkc[:, b, m:m + 1], ACT.Exp,
                                                 bias=negm[:, u:u + 1]).then_inc(S["esink"], 1)
                            nc.scalar.activation(prob[:, u % 2, 0:hi - lo], prob[:, u % 2, 0:hi - lo], ACT.Exp,
                                                 bias=negm[:, u:u + 1], accum_out=rsum[:, u:u + 1]).then_inc(S["exp"], 1)
                        else:
                            nc.scalar.activation(prob[:, u % 2, 0:hi - lo], k.pt[m][:, lo:hi], ACT.Exp, scale=SCALE,
                                                 bias=negm[:, u:u + 1], accum_out=rsum[:, u:u + 1]).then_inc(S["exp"], 1)
                        if u:
                            evacuate(u - 1)
                    evacuate(UN - 1)
                    if not odd:
                        act.wait_ge(S["ssq"], i + 1)
                        nc.scalar.activation(rstd, ssq, ACT.Ln, scale=1.0 / P, bias=k.eps).then_inc(S["rstd"], 1)
                        act.wait_ge(S["rstd"], 2 * i + 1)
                        nc.scalar.activation(rstd, rstd, ACT.Exp, scale=-0.5).then_inc(S["rstd"], 1)
                    act.wait_ge(S["turned"], i + 1)
                    dst = k.mx[:, (0 if odd else 4) + i, :]
                    if odd:
                        nc.scalar.copy(dst, k.pt[2][:, 0:NT]).then_inc(S["stored"], 1)
                    else:
                        nc.scalar.activation(dst, k.pt[2][:, 0:NT], ACT.Identity, scale=gdiff).then_inc(S["stored"], 1)

        @block.vector
        def _(dve):
            dve.wait_ge(S["v_in"], 64 if odd else 48)
            c = Chain(k, dve, f"at_dve_{tag}")
            if not odd:
                for j in range(2):
                    nc.vector.tensor_tensor_reduce(junk[:, DH * j:DH * (j + 1)], lamx[:, 2 * j, :], lamx[:, 2 * j + 1, :], 1.0, 0.0,
                                                   ALU.mult, ALU.add, dots[:, j:j + 1]).then_inc(S["dots"], 1)
                dve.wait_ge(S["lam"], 1)
                c.link(nc.vector.tensor_tensor(neglam, dots[:, 1:2], dots[:, 0:1], ALU.subtract))
                c.link(nc.vector.tensor_scalar(neglam, neglam, -LAM_INIT, None, ALU.add))
                c.link(nc.vector.tensor_scalar(gdiff, k.cols[:, ROW_DG:ROW_DG + 1], 1.0 - LAM_INIT, None, ALU.mult))
            with dve.Fori(0, ITER // 2) as i2:
                c.enter(i2, 4 * UN if odd else 4 * TILES - 2)
                for b in range(2):
                    i = i2 * 2 + b
                    N = i * UN

                    def evacuate(u):
                        n, h = split(u)
                        dve.wait_ge(S["pt"], N + u + 1 + LEAD)
                        dve.wait_ge(S["pv"], N + max(u - 1, 0) + LEAD)
                        nc.vector.tensor_copy(probT[:, u % 2, 0:h * P], k.bank(4)[:, 0:h * P]).then_inc(S["outd"], 1)

                    def combine(u):
                        t, m, lo, hi = unit(u)
                        dve.wait_ge(S["pv"], N + u + 1 + LEAD)
                        if odd:
                            dve.wait_ge(S["esink"], N + u + 1)
                            c.link(nc.vector.tensor_tensor(rsum[:, u:u + 1], rsum[:, u:u + 1], esink[:, u:u + 1], ALU.add))
                            c.link(nc.vector.reciprocal(rinv[:, u:u + 1], rsum[:, u:u + 1]))
                            nc.vector.tensor_scalar(ob[:, t, m * DH:(m + 1) * DH], k.bank(6 + m)[:, 0:DH],
                                                    rinv[:, u:u + 1], None, ALU.mult).then_inc(S["comb"], 1)
                        elif m == 1:
                            c.link(nc.vector.reciprocal(rinv[:, u - 1:u + 1], rsum[:, u - 1:u + 1]))
                            nc.vector.tensor_scalar(t2, k.bank(7)[:, 0:P], rinv[:, u:u + 1], neglam, ALU.mult,
                                                    ALU.mult).then_inc(S["comb"], 1)
                            dve.wait_ge(S["comb"], N + u + LEAD)
                            nc.vector.scalar_tensor_tensor(out=ob[:, t, :], in0=k.bank(6)[:, 0:P],
                                                           scalar=rinv[:, u - 1:u], in1=t2, op0=ALU.mult,
                                                           op1=ALU.add).then_inc(S["comb"], 1)
                            dve.wait_ge(S["comb"], N + u + 1 + LEAD)
                            op = nc.vector.tensor_tensor_reduce(junk, ob[:, t, :], ob[:, t, :], 1.0, 0.0, ALU.mult,
                                                                ALU.add, ssq[:, t:t + 1])
                            if t == LAT_TILES:
                                op.then_inc(S["ssq"], 1)
                                dve.wait_ge(S["ssq"], i + 1)
                            else:
                                c.link(op)

                    if odd:
                        dve.wait_ge(S["q_in"], QIN * i + QIN)
                    for u in range(UN):
                        t, m, lo, hi = unit(u)
                        dve.wait_ge(S["qk"], N + u + 1 + LEAD)
                        if odd:
                            dve.wait_ge(S["pt"], N + max(u - 1, 0) + LEAD)
                            nc.vector.tensor_copy(tick, mask[:, 0:1])
                            nc.vector.tensor_tensor_reduce(prob[:, u % 2, 0:hi - lo], k.pt[m][:, lo:hi], mask[:, lo:hi],
                                                           SCALE, -3e38, ALU.add, ALU.max, top[:, u:u + 1]).then_inc(S["max"], 1)
                            dve.wait_ge(S["max"], N + u + 1 + LEAD)
                            nc.vector.tensor_scalar(negm[:, u:u + 1], top[:, u:u + 1],
                                                    sinkc[:, b, m:m + 1], -1.0, ALU.max,
                                                    ALU.mult).then_inc(S["small"], 1)
                        else:
                            nc.vector.reduce_max(top[:, u:u + 1], k.pt[m][:, lo:hi], AX).then_inc(S["max"], 1)
                            dve.wait_ge(S["max"], N + u + 1 + LEAD)
                            nc.vector.tensor_scalar(negm[:, u:u + 1], top[:, u:u + 1], -SCALE, None,
                                                    ALU.mult).then_inc(S["small"], 1)
                        if u:
                            evacuate(u - 1)
                        if u >= 2:
                            combine(u - 2)
                    evacuate(UN - 1)
                    combine(UN - 2)
                    combine(UN - 1)
                    if not odd:
                        dve.wait_ge(S["rstd"], 2 * i + 2)
                        nc.vector.tensor_tensor(ob, ob, rstd.rearrange("p (t o) -> p t o", o=1).broadcast_to([P, TILES, P]),
                                                ALU.mult).then_inc(S["norm"], 1)
                c.leave(ITER // 2)



def norm_steps(k, tag):
    return {n: k.sem(f"ln_{n}_{tag}") for n in ("rows_in", "done", "read", "stats", "lnvar", "rstd", "shift", "normed",
                                                "scaled", "ready", "out")}


def phase_residual_norm(k, a, l, which):
    nc = k.nc
    tag = f"{l}{which}"
    S = norm_steps(k, tag)
    gate_rows = k.at(k.H, 2048).rearrange("p (g n) -> p g n", g=2)
    ln_g, ln_b = k.at(k.H + 2048, D), k.at(k.H + 3072, D)
    tmp = k.at(k.scr, 2048).rearrange("p (b n) -> p b n", b=2)
    st = k.at(k.scr + 2048, 12 * TILES).rearrange("p (t n) -> p t n", t=TILES)
    mv = k.at(k.scr + 2110, 2 * TILES).rearrange("p (t n) -> p t n", t=TILES)
    rstd = k.at(k.scr + 2120, TILES)
    shift = k.at(k.scr + 2125, TILES)
    part = GA1 if which == 0 else GA2
    base = BASE_OUT0 if l == 0 else BASE_OUT1
    last_norm = l == DEPTH - 1 and which == 1
    with nc.Block() as block:
        @block.sync
        def _(sp):
            for g in range(2):
                off = (2 * l + g) * 6 * D + part * P
                sp.dma_start(gate_rows[:, g, :], bcast_rows(k.dram["mod_rows"], off, [[1, D]])).then_inc(S["rows_in"], 16)
            off = (2 * l + which) * D
            sp.dma_start(ln_g, bcast_rows(a["ln_g"], off, [[1, D]])).then_inc(S["rows_in"], 16)
            sp.dma_start(ln_b, bcast_rows(a["ln_b"], off, [[1, D]])).then_inc(S["rows_in"], 16)
            if which == 0:
                for s in range(6):
                    if l:
                        sp.wait_ge(k.r_free, 6 * E * l)
                    sp.dma_start(k.ring[s], expert_half(a, l, 0, s)).then_inc(k.r_landed[s], 16)
            elif l == 0:
                for u in range(WSLOTS):
                    feed(k, sp, BASE_IN1 + u, in1_units(a)[u])
            for t in range(TILES):
                sp.wait_ge(S["ready"], t + 1)
                if last_norm:
                    dst = a["y_sample"][t * P:(t + 1) * P, :] if t < LAT_TILES else a["y_prompt"]
                else:
                    dst = k.dram["y_rows"][t * P:(t + 1) * P, :]
                sp.dma_start(dst, k.y[:, t, :]).then_inc(S["out"], 16)
            sp.wait_ge(S["out"], 16 * TILES)

        @block.tensor
        def _(pe):
            if which == 1:
                return
            for s in range(4):
                n = base + s
                pe.wait_ge(k.w_landed[n % WSLOTS], 16 * (n // WSLOTS + 1))
                for t in range(TILES):
                    g = s * TILES + t
                    if g >= 8:
                        pe.wait_ge(S["read"], g - 7)
                    for c in range(KC):
                        last = nc.tensor.matmul(k.bank(g % 8)[:, 0:UNIT], k.mx[:, c, t * P:(t + 1) * P],
                                                k.wst[n % WSLOTS][:, c, :], start=(c == 0), stop=(c == KC - 1))
                    last.then_inc(S["done"], 1)

        @block.scalar
        def _(act):
            for t in range(TILES):
                act.wait_ge(S["stats"], t + 1)
                nc.scalar.activation(rstd[:, t:t + 1], mv[:, t, 1:2], ACT.Ln, bias=k.eps).then_inc(S["lnvar"], 1)
                act.wait_ge(S["lnvar"], t + 1)
                nc.scalar.activation(rstd[:, t:t + 1], rstd[:, t:t + 1], ACT.Exp, scale=-0.5).then_inc(S["rstd"], 1)
                act.wait_ge(S["shift"], t + 1)
                act.wait_ge(S["rstd"], t + 1)
                nc.scalar.activation(k.y[:, t, :], k.y[:, t, :], ACT.Identity, scale=rstd[:, t:t + 1],
                                     bias=shift[:, t:t + 1]).then_inc(S["normed"], 1)

        @block.gpsimd
        def _(pool):
            for t in range(TILES):
                pool.wait_ge(S["scaled"], t + 1)
                nc.gpsimd.tensor_tensor(k.y[:, t, :], k.y[:, t, :], ln_b, ALU.add).then_inc(S["ready"], 1)

        @block.vector
        def _(dve):
            c = Chain(k, dve, f"ln_dve_{tag}")
            dve.wait_ge(S["rows_in"], 64)

            def statistics(t):
                nc.vector.bn_stats(st[:, t, 0:6], k.y[:, t, 0:512])
                c.link(nc.vector.bn_stats(st[:, t, 6:12], k.y[:, t, 512:1024]))
                nc.vector.bn_aggr(mv[:, t, :], st[:, t, :]).then_inc(S["stats"], 1)

            def finish(t):
                dve.wait_ge(S["rstd"], t + 1)
                dve.wait_ge(S["stats"], t + 1)
                nc.vector.tensor_scalar(shift[:, t:t + 1], mv[:, t, 0:1], rstd[:, t:t + 1], -1.0, ALU.mult,
                                        ALU.mult).then_inc(S["shift"], 1)

            def scale(t):
                dve.wait_ge(S["normed"], t + 1)
                nc.vector.tensor_tensor(k.y[:, t, :], k.y[:, t, :], ln_g, ALU.mult).then_inc(S["scaled"], 1)

            if which == 0:
                for s in range(4):
                    for t in range(TILES):
                        g = s * TILES + t
                        cols = slice(s * UNIT, (s + 1) * UNIT)
                        dve.wait_ge(S["done"], g + 1)
                        x = tmp[:, g % 2, 0:UNIT]
                        nc.vector.tensor_tensor(x, k.bank(g % 8)[:, 0:UNIT], gate_rows[:, t // LAT_TILES, cols],
                                                ALU.mult).then_inc(S["read"], 1)
                        dve.wait_ge(S["read"], g + 1)
                        c.link(nc.vector.scalar_tensor_tensor(out=k.y[:, t, cols], in0=k.y[:, t, cols], scalar=ALPHA,
                                                              in1=x, op0=ALU.mult, op1=ALU.add))
            for t in range(TILES):
                if which == 1:
                    c.link(nc.vector.tensor_tensor(tmp[:, t % 2, :], k.moe[:, t, :], gate_rows[:, t // LAT_TILES, :], ALU.mult))
                    c.link(nc.vector.scalar_tensor_tensor(out=k.y[:, t, :], in0=k.y[:, t, :], scalar=ALPHA,
                                                          in1=tmp[:, t % 2, :], op0=ALU.mult, op1=ALU.add))
                statistics(t)
                if t:
                    finish(t - 1)
                if t >= 2:
                    scale(t - 2)
            finish(TILES - 1)
            scale(TILES - 2)
            scale(TILES - 1)


def expert_half(a, l, e, s):
    name, half = [("w_exp_gate", 0), ("w_exp_up", 0), ("w_exp_gate", 1), ("w_exp_up", 1), ("w_exp_down", 0),
                  ("w_exp_down", 1)][s]
    return a[name][l].rearrange("e (c p) (h n) -> e h p c n", p=P, h=2)[e, half]


def moe_views(k):
    w, s = k.WST, k.scr
    v = {}
    v["xs"] = k.at(w, 2048).rearrange("p (b n) -> p b n", b=2)
    v["rows"] = k.at(w + 2048, 2048).rearrange("p (b n) -> p b n", b=2)
    v["rowsc"] = k.at(w + 4096, D)
    v["hot"] = k.at(w + 5120, 1024).rearrange("p (b n) -> p b n", b=2)
    v["hotc"] = k.at(w + 6144, P)
    v["scale"] = k.at(w + 6272, 640).rearrange("p (c n) -> p c n", c=KC)
    v["shift"] = k.at(w + 6912, 640).rearrange("p (c n) -> p c n", c=KC)
    v["iota"] = k.at(s, NT)
    v["idx_pair"] = k.at(s + 640, E // 2)
    v["idx_ctx"] = k.at(s + 648, E // 4)
    v["idx80"] = k.at(s + 652, E + 1)
    v["gate80"] = k.at(s + 669, E + 1)
    v["icol"] = k.at(s + 686, 2)
    v["gcol"] = k.at(s + 688, 2)
    v["tick"] = k.at(s + 690, 1)
    v["xT"] = k.at(k.H, 1280).rearrange("p (b c n) -> p b c n", b=2, c=KC)
    v["hidT"] = k.at(k.H + 1280, 640).rearrange("p (c n) -> p c n", c=KC)
    v["hid"] = k.at(k.H + 1920, FF)
    v["sg"] = k.at(k.H + 2944, FF)
    return v


def phase_router(k, a, l):
    nc = k.nc
    v = moe_views(k)
    s0 = k.scr + 700
    wr = k.at(s0, 128).rearrange("p (c n) -> p c n", c=KC)
    top = k.at(s0 + 128, TILES)
    tot = k.at(s0 + 133, TILES)
    aff = k.at(s0 + 140, 80).rearrange("p (t n) -> p t n", t=TILES)
    affT = k.at(s0 + 220, NT)[0:E]
    vals = k.at(s0 + 860, SLOTS)[0:E]
    idx = k.at(s0 + 940, SLOTS).bitcast(U32)[0:E]
    idf = k.at(s0 + 1020, SLOTS)[0:E]
    S = {n: k.sem(f"ro_{n}_{l}") for n in ("w_in", "logits", "sub", "exp", "aff", "turned", "picked", "kept", "laid", "cleared")}
    lg = k.bank(4)[:, 0:80].rearrange("p (t n) -> p t n", t=TILES)
    with nc.Block() as block:
        @block.sync
        def _(sp):
            sp.dma_start(wr, a["w_router"][l].rearrange("(c p) n -> p c n", p=P)).then_inc(S["w_in"], 16)
            sp.dma_start(v["iota"], a["iota"]).then_inc(S["w_in"], 16)
            sp.wait_ge(S["picked"], 1)
            dv, di = k.dram["gates"], k.dram["index"]
            ns = E * CAP_S
            for dst, src in ((dv, vals), (di, idf)):
                sp.dma_start(dst[0:ns].rearrange("(e s) -> e s", s=CAP_S), src[:, 0:CAP_S]).then_inc(S["kept"], 16)
                sp.dma_start(dst[ns:].rearrange("(e s) -> e s", s=CAP_P), src[:, CAP_S:SLOTS]).then_inc(S["kept"], 16)
            sp.wait_ge(S["kept"], 64)
            sp.wait_ge(S["cleared"], 1)
            with nc.allow_non_contiguous_dma(reason="slot tables of a few hundred words"):
                for dst, src in (("idx80", di), ("gate80", dv)):
                    sp.dma_start(v[dst][0:CAP_S, 0:E], src[0:ns].rearrange("(e s) -> s e", s=CAP_S)).then_inc(S["laid"], 16)
                    sp.dma_start(v[dst][CAP_S:SLOTS, 0:E],
                                 src[ns:].rearrange("(e s) -> s e", s=CAP_P)).then_inc(S["laid"], 16)
                sp.dma_start(v["idx_pair"], di[0:ns].rearrange("(e s) -> s e", s=P)).then_inc(S["laid"], 16)
                for j in range(4):
                    sp.dma_start(v["idx_ctx"][32 * j:32 * j + CAP_P],
                                 di[ns:].rearrange("(g j s) -> j s g", j=4, s=CAP_P)[j]).then_inc(S["laid"], 16)
            sp.wait_ge(S["laid"], 144)

        @block.tensor
        def _(pe):
            pe.wait_ge(S["w_in"], 32)
            for t in range(TILES):
                for c in range(KC):
                    last = nc.tensor.matmul(lg[:, t, :], k.h[:, c, t * P:(t + 1) * P], wr[:, c, :], start=(c == 0),
                                            stop=(c == KC - 1))
            last.then_inc(S["logits"], 1)
            pe.wait_ge(S["aff"], 1)
            for t in range(TILES):
                last = nc.tensor.transpose(k.pt[0][0:E, t * P:(t + 1) * P], aff[:, t, :], k.ident)
            last.then_inc(S["turned"], 1)

        @block.scalar
        def _(act):
            act.wait_ge(S["sub"], 1)
            nc.scalar.activation(aff, aff, ACT.Exp).then_inc(S["exp"], 1)

        @block.gpsimd
        def _(pool):
            nc.gpsimd.memset(v["idx_ctx"], -1.0)
            nc.gpsimd.memset(v["gate80"][:, E:E + 1], 0.0)
            nc.gpsimd.memset(v["idx80"][:, E:E + 1], 0.0).then_inc(S["cleared"], 1)
            nc.gpsimd.memset(k.mx, 0.0)
            nc.gpsimd.memset(v["rows"][:, 1], 0.0)
            nc.gpsimd.memset(v["rowsc"], 0.0)
            nc.gpsimd.memset(v["hot"][:, 1], 0.0)
            nc.gpsimd.memset(v["hotc"], 0.0)

        @block.vector
        def _(dve):
            c = Chain(k, dve, f"ro_dve_{l}")
            for name, part in (("scale", SC2), ("shift", SH2)):
                for g, (lo, hi) in enumerate(((0, CAP_S), (CAP_S, SLOTS))):
                    nc.vector.tensor_copy(v[name][:, :, lo:hi],
                                          k.mod[l][:, part:part + KC, g:g + 1].broadcast_to([P, KC, hi - lo]))
            dve.wait_ge(S["logits"], 1)
            c.link(nc.vector.reduce_max(top, lg, AX))
            nc.vector.tensor_tensor(aff, lg, top.rearrange("p (t o) -> p t o", o=1).broadcast_to([P, TILES, E]),
                                    ALU.subtract).then_inc(S["sub"], 1)
            dve.wait_ge(S["exp"], 1)
            c.link(nc.vector.reduce_sum(tot, aff, AX))
            c.link(nc.vector.reciprocal(tot, tot))
            nc.vector.tensor_tensor(aff, aff, tot.rearrange("p (t o) -> p t o", o=1).broadcast_to([P, TILES, E]),
                                    ALU.mult).then_inc(S["aff"], 1)
            dve.wait_ge(S["turned"], 1)
            c.link(nc.vector.tensor_copy(affT, k.pt[0][0:E, 0:NT]))
            for lo, hi, first, rounds in ((0, NS, 0, CAP_S // 8), (NS, NT, CAP_S, CAP_P // 8)):
                row = affT[:, lo:hi]
                for r in range(rounds):
                    sl = slice(first + 8 * r, first + 8 * r + 8)
                    c.link(nc.vector.max(vals[:, sl], row))
                    c.link(nc.vector.max_index(idx[:, sl], vals[:, sl], row))
                    if r < rounds - 1:
                        c.link(nc.vector.match_replace(row, vals[:, sl], row, -1.0))
            nc.vector.tensor_copy(idf[:, 0:CAP_S], idx[:, 0:CAP_S])
            nc.vector.tensor_scalar(idf[:, CAP_S:SLOTS], idx[:, CAP_S:SLOTS], float(NS), None,
                                    ALU.add).then_inc(S["picked"], 1)


def phase_experts(k, a, l):
    nc = k.nc
    v = moe_views(k)
    S = {n: k.sem(f"ex_{n}_{l}") for n in ("icol", "gathered0", "gathered1", "xturned", "xmul", "xready", "silu",
                                           "hid", "hturned", "hready", "rows", "hot", "sum", "acc")}
    GATHERED = (S["gathered0"], S["gathered1"])
    LEAD = 3
    rbase = 6 * E * l
    ROUNDS = E // 4
    SUMS = 4 * 4 + 2
    G, U, O = (2, 4), (3, 5), (6, 7)
    sg, hid = v["sg"][0:SLOTS], v["hid"][0:SLOTS]

    def side(x):
        return x.rearrange("p (c n) -> p c n", n=SLOTS)

    def sums(q):
        pair = 1 if q < 2 else 0
        out = [("pair", pair, t, hf) for t in ((0, 1) if q % 2 == 0 else (2, 3)) for hf in range(2)]
        return out + ([("ctx", 0, LAT_TILES, hf) for hf in range(2)] if q == 0 else [])

    def sums_before(q):
        return sum(len(sums(x)) for x in range(q))

    with nc.Block() as block:
        @block.sync
        def _(sp):
            for s in S.values():
                if s not in GATHERED:
                    sp.sem_inc(s, LEAD)
            with sp.Fori(1, E) as e:
                for s in range(6):
                    sp.wait_ge(k.r_free, e * 6 + (rbase + s - 5))
                    sp.dma_start(k.ring[s], expert_half(a, l, e, s)).then_inc(k.r_landed[s], 16)

        @block.gpsimd
        def _(pool):
            def gather(i, q, b):
                e = 4 * i + q
                pool.wait_ge(S["xturned"], e + (LEAD - 1))
                pool.wait_ge(S["rows"], 2 * e + (LEAD - 2))
                nc.gpsimd.tensor_copy(v["gcol"][0:SLOTS, b:b + 1], v["gate80"][0:SLOTS, bass.ds(e, 1)])
                nc.gpsimd.tensor_copy(v["icol"][0:SLOTS, b:b + 1].bitcast(U32),
                                      v["idx80"][0:SLOTS, bass.ds(e, 1)]).then_inc(S["icol"], 1)
                pool.wait_ge(S["icol"], e + (LEAD + 1))
                nc.gpsimd.tensor_tensor(v["tick"], v["iota"][:, 0:1], v["iota"][:, 0:1],
                                        ALU.add)
                nc.gpsimd.indirect_dma_start(
                    v["xs"][0:SLOTS, b, :], None, k.dram["y_rows"],
                    bass.IndirectOffsetOnAxis(ap=v["icol"][0:SLOTS, b:b + 1].bitcast(U32), axis=0)).then_inc(GATHERED[b], 16)

            with pool.Fori(0, ROUNDS) as i:
                for q in range(4):
                    gather(i, q, q % 2)
            pool.wait_ge(S["xturned"], E + LEAD - 1)
            nc.gpsimd.tensor_copy(v["icol"][0:SLOTS, 0:1].bitcast(U32), v["idx80"][0:SLOTS, E:E + 1]).then_inc(S["icol"], 1)
            pool.wait_ge(S["icol"], E + LEAD + 1)
            nc.gpsimd.indirect_dma_start(
                v["xs"][0:SLOTS, 0, :], None, k.dram["y_rows"],
                bass.IndirectOffsetOnAxis(ap=v["icol"][0:SLOTS, 0:1].bitcast(U32), axis=0)).then_inc(GATHERED[0], 16)
            pool.wait_ge(GATHERED[0], 16 * (E // 2 + 1))

        @block.tensor
        def _(pe):
            def turn_rows(b):
                for c in range(KC):
                    last = nc.tensor.transpose(k.bank(c // 4)[:, (c % 4) * SLOTS:(c % 4 + 1) * SLOTS],
                                               v["xs"][0:SLOTS, b, c * P:(c + 1) * P], k.ident[0:SLOTS, 0:SLOTS])
                last.then_inc(S["xturned"], 1)

            def turn_hidden(hf):
                for f in range(4):
                    col = hf * 512 + f * P
                    last = nc.tensor.transpose(k.bank(hf)[:, f * SLOTS:(f + 1) * SLOTS], hid[:, col:col + P],
                                               k.ident[0:SLOTS, 0:SLOTS])
                last.then_inc(S["hturned"], 1)

            def add_rows(what, b, t, hf, bank):
                if what == "pair":
                    lhs, rows = v["hot"][:, b, t * P:(t + 1) * P], v["rows"][:, b, hf * 512:(hf + 1) * 512]
                else:
                    lhs, rows = v["hotc"], v["rowsc"][:, hf * 512:(hf + 1) * 512]
                nc.tensor.matmul(k.bank(bank), lhs, rows, start=True, stop=True).then_inc(S["sum"], 1)

            pe.wait_ge(GATHERED[0], 16)
            turn_rows(0)
            with pe.Fori(0, ROUNDS) as i:
                for q in range(4):
                    b = q % 2
                    e = 4 * i + q
                    pe.wait_ge(S["xready"], e + (LEAD + 1))
                    for hf in range(2):
                        if hf == 0:
                            pe.wait_ge(S["acc"], SUMS * i + (sums_before(q) + LEAD))
                        for m in range(2):
                            s = 2 * hf + m
                            pe.wait_ge(k.r_landed[s], e * 16 + 16 * (E * l + 1))
                            for c in range(KC):
                                last = nc.tensor.matmul(k.bank((G, U)[m][hf])[0:SLOTS, :], v["xT"][:, b, c, :],
                                                        k.ring[s][:, c, :], start=(c == 0), stop=(c == KC - 1))
                            last.then_inc(k.r_free, 1)
                    pe.wait_ge(S["hid"], 2 * e + (LEAD + 1))
                    turn_hidden(0)
                    pe.wait_ge(S["rows"], 2 * e + LEAD)
                    pe.wait_ge(S["hot"], 3 * i + ((0, 0, 1, 1)[q] + LEAD))
                    for n, (what, pair, t, hf) in enumerate(sums(q)):
                        if n >= 2:
                            pe.wait_ge(S["acc"], SUMS * i + (sums_before(q) + n - 1 + LEAD))
                        add_rows(what, pair, t, hf, 2 + n % 2)
                    pe.wait_ge(S["hid"], 2 * e + (LEAD + 2))
                    turn_hidden(1)
                    for part in range(2):
                        pe.wait_ge(S["hready"], 2 * e + (LEAD + 1 + part))
                        if part == 1:
                            pe.wait_ge(GATHERED[1 - b], i * 32 + 16 * ((q + 1) // 2 + 1))
                            turn_rows(1 - b)
                        for hd in range(2):
                            if part == 0:
                                pe.wait_ge(k.r_landed[4 + hd], e * 16 + 16 * (E * l + 1))
                            for f in range(4 * part, 4 * part + 4):
                                last = nc.tensor.matmul(k.bank(O[hd])[0:SLOTS, :], v["hidT"][:, f, :],
                                                        k.ring[4 + hd][:, f, :], start=(f == 0), stop=(f == KC - 1))
                            if part == 1:
                                last.then_inc(k.r_free, 1)
            pe.wait_ge(S["rows"], 2 * E + LEAD)
            pe.wait_ge(S["hot"], 3 * ROUNDS + LEAD)
            for n, (what, pair, t, hf) in enumerate(sums(0) + sums(1)):
                pe.wait_ge(S["acc"], SUMS * ROUNDS + max(n - 3, 0) + LEAD)
                add_rows(what, pair, t, hf, 2 + n % 4)

        @block.scalar
        def _(act):
            with act.Fori(0, ROUNDS) as i:
                for q in range(4):
                    e = 4 * i + q
                    for hf in range(2):
                        act.wait_ge(k.r_free, 6 * e + (rbase + 2 * hf + 1))
                        act.wait_ge(S["hid"], 2 * e + (hf - 1 + LEAD))
                        nc.scalar.activation(sg[:, hf * 512:(hf + 1) * 512], k.bank(G[hf])[0:SLOTS, :],
                                             ACT.Silu).then_inc(S["silu"], 1)
                    for hf in range(2):
                        act.wait_ge(S["hturned"], 2 * e + (hf + 1 + LEAD))
                        nc.scalar.copy(v["hidT"][:, 4 * hf:4 * hf + 4, :], side(k.bank(hf)[:, 0:320])).then_inc(S["hready"], 1)
                    gate = v["gcol"][:, q % 2:q % 2 + 1]
                    lo = CAP_S * (q % 2)
                    for hd in range(2):
                        act.wait_ge(k.r_free, 6 * e + (rbase + 5 + hd))
                        if hd == 0:
                            act.wait_ge(S["icol"], e + (LEAD + 1))
                        cols = slice(hd * 512, (hd + 1) * 512)
                        nc.scalar.activation(v["rows"][lo:lo + CAP_S, q // 2, cols], k.bank(O[hd])[0:CAP_S, :], ACT.Copy,
                                             scale=gate[0:CAP_S])
                        nc.scalar.activation(v["rowsc"][32 * q:32 * q + CAP_P, cols], k.bank(O[hd])[CAP_S:SLOTS, :],
                                             ACT.Copy, scale=gate[CAP_S:SLOTS]).then_inc(S["rows"], 1)

        @block.vector
        def _(dve):
            def modulate_rows(e_ready, e_mul, b):
                dve.wait_ge(S["xturned"], e_ready)
                for hf in range(2):
                    chunks = slice(4 * hf, 4 * hf + 4)
                    nc.vector.tensor_tensor(v["xT"][:, b, chunks, :], side(k.bank(hf)[:, 0:320]), v["scale"][:, chunks, :],
                                            ALU.mult).then_inc(S["xmul"], 1)
                dve.wait_ge(S["xmul"], e_mul)
                nc.vector.tensor_tensor(v["xT"][:, b], v["xT"][:, b], v["shift"], ALU.add).then_inc(S["xready"], 1)

            def add_sum(t, hf, bank):
                acc = k.moe[:, t, hf * 512:(hf + 1) * 512]
                nc.vector.tensor_tensor(acc, acc, k.bank(bank), ALU.add).then_inc(S["acc"], 1)

            modulate_rows(LEAD + 1, LEAD + 2, 0)
            with dve.Fori(0, ROUNDS) as i:
                for q in range(4):
                    e = 4 * i + q
                    for hf in range(2):
                        dve.wait_ge(S["silu"], 2 * e + (hf + 1 + LEAD))
                        dve.wait_ge(k.r_free, 6 * e + (rbase + 2 * hf + 2))
                        dve.wait_ge(S["hturned"], 2 * e + (hf - 1 + LEAD))
                        nc.vector.tensor_tensor(hid[:, hf * 512:(hf + 1) * 512], sg[:, hf * 512:(hf + 1) * 512],
                                                k.bank(U[hf])[0:SLOTS, :], ALU.mult).then_inc(S["hid"], 1)
                    for n, (_, _, t, hf) in enumerate(sums(q)):
                        dve.wait_ge(S["sum"], SUMS * i + (sums_before(q) + n + 1 + LEAD))
                        add_sum(t, hf, 2 + n % 2)
                    if q % 2:
                        nc.vector.tensor_scalar(v["hot"][:, q // 2, :], v["iota"][:, 0:NS],
                                                v["idx_pair"][:, bass.ds(2 * i + q // 2, 1)], None,
                                                ALU.is_equal).then_inc(S["hot"], 1)
                    if q == 3:
                        nc.vector.tensor_scalar(v["hotc"], v["iota"][:, NS:NT], v["idx_ctx"][:, bass.ds(i, 1)], None,
                                                ALU.is_equal).then_inc(S["hot"], 1)
                    modulate_rows(e + (LEAD + 2), 2 * e + (LEAD + 4), 1 - q % 2)
            for n, (_, _, t, hf) in enumerate(sums(0) + sums(1)):
                dve.wait_ge(S["sum"], SUMS * ROUNDS + n + 1 + LEAD)
                add_sum(t, hf, 2 + n % 4)


def build(nc, a, last=None):
    with ExitStack() as stack:
        dram = {
            "mod_rows": nc.dram_tensor("mod_rows", (DEPTH, 2, 6 * D), F32, kind="Internal").ap(),
            "mod_raw": nc.dram_tensor("mod_raw", (2, 6 * D), F32, kind="Internal").ap(),
            "y_rows": nc.dram_tensor("y_rows", (NT, D), F32, kind="Internal").ap(),
            "gates": nc.dram_tensor("slot_gates", (E * SLOTS,), F32, kind="Internal").ap(),
            "index": nc.dram_tensor("slot_index", (E * SLOTS,), F32, kind="Internal").ap(),
        }
        k = Ctx(nc, stack, dram)
        k.moe = k.mx.rearrange("p c n -> p (c n)").rearrange("p (t n) -> p t n", t=TILES)
        phases = [
            ("mod", lambda: phase_modulation(k, a)),
            ("h0", lambda: phase_modulate(k, 0, SH1, SC1, "00")),
            ("proj0", lambda: phase_project_even(k, a)),
            ("hgrn", lambda: phase_hgrn(k, a)),
            ("clear0", k.clear),
            ("rope0", lambda: phase_rope(k, a, False)),
            ("att0", lambda: phase_attention(k, a, False)),
            ("ln00", lambda: phase_residual_norm(k, a, 0, 0)),
            ("h0b", lambda: phase_modulate(k, 0, SH2, SC2, "01")),
            ("router0", lambda: phase_router(k, a, 0)),
            ("moe0", lambda: phase_experts(k, a, 0)),
            ("ln01", lambda: phase_residual_norm(k, a, 0, 1)),
            ("clear", k.clear),
            ("h1", lambda: phase_modulate(k, 1, SH1, SC1, "10")),
            ("proj1", lambda: phase_project_odd(k, a)),
            ("rope1", lambda: phase_rope(k, a, True)),
            ("att1", lambda: phase_attention(k, a, True)),
            ("ln10", lambda: phase_residual_norm(k, a, 1, 0)),
            ("h1b", lambda: phase_modulate(k, 1, SH2, SC2, "11")),
            ("router1", lambda: phase_router(k, a, 1)),
            ("moe1", lambda: phase_experts(k, a, 1)),
            ("ln11", lambda: phase_residual_norm(k, a, 1, 1)),
        ]
        for name, phase in phases:
            phase()
            if last and name == last[0]:
                last[1](k)
                break
        return k


_OUTS = {
    "y_prompt": (1, 128, 1024), "y_sample": (1, 512, 1024), "out_state": (1, 1, 2, 4, 128, 128),
    "out_diff_k": (1, 1, 4, 128, 128), "out_diff_v": (1, 1, 4, 128, 128),
    "out_win_k": (1, 1, 4, 128, 64), "out_win_v": (1, 1, 4, 128, 64),
}


def constants():
    t = np.arange(NS)
    quarter = DH // 4
    inv = (10000.0 ** (-np.arange(quarter, dtype=np.float32) / quarter)).astype(np.float32)
    angle = np.zeros((P, NS), np.float32)
    perm = np.zeros((P, P), np.float32)
    for d in range(P):
        half, j = divmod(d % DH, DH // 2)
        pos = (t // 64 if half == 0 else t % 64).astype(np.float32)
        angle[d] = pos * inv[j % quarter]
        if j < quarter:
            perm[d + quarter, d] = -1.0
        else:
            perm[d - quarter, d] = 1.0
    r = np.arange(P)
    masks = np.zeros((P, 2, 192), np.int32)
    for d in range(2):
        same = (r[:, None] // SUB) == (r[None, :] // SUB)
        order = (r[:, None] <= r[None, :]) if d == 0 else (r[:, None] >= r[None, :])
        masks[:, d, 0:P] = np.where(same & order, -1, 0)
        cols = r.reshape(4, 2, SUB)[:, 1 - d, :].reshape(-1)
        pair = (r[:, None] // CH) == (cols[None, :] // CH)
        first = (r[:, None] // SUB) % 2 == d
        masks[:, d, P:192] = np.where(pair & first, -1, 0)
    keep = np.ones((P, NT + 1), np.float32)
    keep[:, ::SUB] = 0.0
    wmask = np.zeros((P, 768), np.float32)
    wmask[:, 128:256] = np.where(r[:, None] <= r[None, :], 0.0, NEG)
    wmask[:, 640:768] = np.where(r[None, :] <= r[:, None], 0.0, NEG)
    return {
        "ident": np.eye(P, dtype=np.float32), "perm": perm, "cos": np.cos(angle), "sin": np.sin(angle),
        "hgrn_masks": masks, "keep": keep, "wmask": wmask,
        "bmask": (r[:, None] // CH == np.arange(4)[None, :]).astype(np.float32),
        "iota": np.broadcast_to(np.arange(NT, dtype=np.float32), (P, NT)).copy(),
    }


PAIRED = [h for m in range(8) for h in ((m, 4 + m) if m < 4 else (4 + m, 8 + m))]


def kernel(**inputs):
    import concourse.bacc as _bacc
    from concourse.bass_utils import run_bass_kernel_spmd as _run

    nc = _bacc.Bacc("TRN2", target_bir_lowering=False, num_devices=1)
    arrays = {n: np.ascontiguousarray(x) for n, x in inputs.items()}
    w = arrays["w_in_odd"]
    q = w[:, :, :1024].reshape(1, D, 16, DH)[:, :, PAIRED, :].reshape(1, D, 1024)
    arrays["w_in_odd"] = np.concatenate([q, w[:, :, 1024:]], axis=2)
    arrays["w_out_odd"] = arrays["w_out_odd"].reshape(1, 16, DH, D)[:, PAIRED].reshape(1, D, D)
    arrays["win_sink"] = np.ascontiguousarray(arrays["win_sink"][:, PAIRED])
    arrays.update(constants())
    arrays = {f"in_{n}": x for n, x in arrays.items()}
    a = {n[3:]: nc.dram_tensor(n, x.shape, mybir.dt.from_np(x.dtype), kind="ExternalInput").ap() for n, x in arrays.items()}
    for n, shape in _OUTS.items():
        a[n] = nc.dram_tensor(f"res_{n}", shape, F32, kind="ExternalOutput").ap()
    for n in ("y_prompt", "y_sample"):
        a[n] = a[n][0]
    for n in ("out_state", "out_diff_k", "out_diff_v", "out_win_k", "out_win_v"):
        a[n] = a[n][0, 0]
    build(nc, a)
    r = _run(nc, [arrays], core_ids=[0])
    return tuple(r.results[0][f"res_{n}"] for n in _OUTS)
```

```python
from contextlib import ExitStack

import numpy as np

import concourse.bass as bass
import concourse.mybir as mybir

F32 = mybir.dt.float32
F32R = mybir.dt.float32r
I32 = mybir.dt.int32
U32 = mybir.dt.uint32
ALU = mybir.AluOpType
ACT = mybir.ActivationFunctionType
AX = mybir.AxisListType.X

P = 128
D = 1024
KC = D // P
NS, NP_ = 512, 128
NT = NS + NP_
TILES = NT // P
LAT_TILES = NS // P
PAST = 256
DEPTH = 2
HEADS_A = 4
HEADS_B = 4
E = 16
CAP_S, CAP_P = 2 * NS // E, 2 * NP_ // E
SLOTS = CAP_S + CAP_P
FF = 1024
ALPHA = float((2 * DEPTH) ** 0.25)
LN_EPS = 1e-5
LAM_INIT = 0.2
DH = 64
SCALE = DH ** -0.5
NEG = -1e30
UNIT = 256
WSLOTS = 4
SUB = 16
CH = 2 * SUB
GATES = 2 * HEADS_A

AREA = 24576 + 2 * 5120

ROW_BMOD, ROW_C, ROW_CCTX, ROW_LB, ROW_HG, ROW_DG, N_ROWS = 0, 96, 104, 112, 124, 125, 126
SH1, SC1, GA1, SH2, SC2, GA2 = (8 * j for j in range(6))


LEAD = 1


class Ctx:

    def __init__(self, nc, stack, dram):
        self.nc, self.stack, self.dram = nc, stack, dram
        self.phase_sems = []
        self.big = stack.enter_context(nc.sbuf_tensor("memory", [P, 53200 - AREA], F32))
        self.area_stack, self.areas = ExitStack(), 0
        self.pt = [stack.enter_context(nc.psum_tensor(f"psum{i}", [P, 1024], F32)) for i in range(4)]
        self.RING, self.H, self.Y, self.WST, self.MX, self.MISC = 0, 24576, 29696, AREA, 43008, 48128
        self.wst = [self.at(self.WST + 2048 * s, 2048).rearrange("p (c n) -> p c n", c=KC) for s in range(WSLOTS)]
        self.mx = self.at(self.MX, 5120).rearrange("p (c n) -> p c n", c=KC)
        self.ident = self.at(self.MISC, 128)
        self.perm = self.at(self.MISC + 128, 128)
        self.cols = self.at(self.MISC + 256, 126)
        self.mod = [self.at(self.MISC + 384 + 96 * l, 96).rearrange("p (c g) -> p c g", g=2) for l in range(DEPTH)]
        self.silu_c = self.at(self.MISC + 576, 16).rearrange("p (c g) -> p c g", g=2)
        self.scr = self.MISC + 592
        self.w_landed = [self.sem(f"w_landed{s}") for s in range(WSLOTS)]
        self.w_free = self.sem("w_free")
        self.w_seen = 0
        self.r_landed = [self.sem(f"ring_landed{s}") for s in range(3)]
        self.eps = LN_EPS
        self.r_free = self.sem("ring_free")
        self.phase_sems = []

    def at(self, start, size):
        if start < AREA:
            return self.area[:, start - self.area_start:start - self.area_start + size]
        return self.big[:, start - AREA:start - AREA + size]

    @property
    def h(self):
        return self.at(self.H, 5120).rearrange("p (c n) -> p c n", c=KC)

    def tensor(self, stack, name, columns, dtype=F32):
        return stack.enter_context(self.nc.sbuf_tensor(f"{name}_{self.areas}", [P, columns], dtype))

    @property
    def y(self):
        return self.at(self.Y, 5120).rearrange("p (t n) -> p t n", t=TILES)

    def for_mixer(self):
        self.area_stack.close()
        self.areas += 1
        self.area, self.area_start = self.tensor(self.area_stack, "area", AREA), 0

    def for_experts(self):
        self.area_stack.close()
        self.areas += 1
        raw = self.tensor(self.area_stack, "raw", 3 * 4096)
        self.ring = [raw[:, 4096 * s:4096 * s + 4096].rearrange("p (c n) -> p c n", c=KC) for s in range(3)]
        x, h = self.tensor(self.area_stack, "rows_split", 2560, F32R), self.tensor(self.area_stack, "hid_split", 1280, F32R)
        self.xh, self.xl = (x[:, 1280 * j:1280 * j + 1280].rearrange("p (b c n) -> p b c n", b=2, c=KC) for j in range(2))
        self.hidh, self.hidl = (h[:, 640 * j:640 * j + 640].rearrange("p (c n) -> p c n", c=KC) for j in range(2))
        self.x32 = self.tensor(self.area_stack, "rows_whole", 640)[:, 0:640].rearrange("p (c n) -> p c n", c=KC)
        high, low = (self.tensor(self.area_stack, n, 4 * 2048, F32R) for n in ("high", "low"))
        self.high, self.low = ([x[:, 2048 * s:2048 * s + 2048].rearrange("p (c n) -> p c n", c=4) for s in range(4)]
                               for x in (high, low))

    def sem(self, name):
        self.phase_sems.append(self.nc.alloc_semaphore(name))
        return self.phase_sems[-1]

    def clear(self):
        self.nc.all_engine_barrier()
        self.nc.clear_and_free_semaphores(self.phase_sems)
        self.phase_sems = []
        self.nc.all_engine_barrier()

    def bank(self, i):
        return self.pt[i // 2][:, (i % 2) * 512:(i % 2) * 512 + 512]


class Chain:

    def __init__(self, k, engine, name):
        self.sem, self.engine, self.n, self.base = k.sem(name), engine, 0, 0

    def enter(self, i, per):
        self.saved, self.per, self.n0 = self.n, per, self.n
        self.base, self.n = i * per + self.n, 0

    def leave(self, times):
        assert self.n == self.per, (self.n, self.per)
        self.n, self.base = self.saved + times * self.per, 0

    def link(self, instruction):
        instruction.then_inc(self.sem, 1)
        self.n += 1
        self.engine.wait_ge(self.sem, self.base + self.n)


def bcast_rows(ap, offset, dims):
    return bass.AP(tensor=ap.tensor, offset=offset, ap=[[0, P]] + dims)


def w_units(weight, first, count):
    v = weight.rearrange("(c p) (u n) -> u p c n", p=P, n=UNIT)
    return [v[u] for u in range(first, first + count)]


def feed(k, sp, number, source, reader=None):
    if reader:
        sp.wait_ge(*reader)
    sp.dma_start(k.wst[number % WSLOTS], source).then_inc(k.w_landed[number % WSLOTS], 16)


MOD_UNITS = 6 * D // UNIT
N_IN0, N_OUT, N_IN1 = 16, 4, 6
BASE_IN0 = MOD_UNITS
BASE_OUT0 = BASE_IN0 + N_IN0
BASE_IN1 = BASE_OUT0 + N_OUT
BASE_OUT1 = BASE_IN1 + N_IN1


def phase_modulation(k, a):
    nc = k.nc
    rows = k.at(k.scr, 128)
    mrows, bias = k.at(k.RING, 6 * D)[0:2], k.at(k.RING + 6 * D, 6 * D)[0:2]
    sc = k.silu_c
    consts_in, rows_in, x_in = k.sem("consts_in"), k.sem("rows_in"), k.sem("x_in")
    rows_turned, cols_ready, sc_ready = k.sem("rows_turned"), k.sem("cols_ready"), k.sem("sc_ready")
    LEAD = WSLOTS
    bias_in, row_ready, mod_turned, rows_out = (k.sem(n) for n in ("bias_in", "row_ready", "mod_turned", "mod_rows_out"))
    with nc.Block() as block:
        @block.sync
        def _(sp):
            sp.sem_inc(row_ready, LEAD)
            sp.dma_start(k.ident, a["ident"]).then_inc(consts_in, 16)
            sp.dma_start(k.perm, a["perm"]).then_inc(consts_in, 16)
            sp.dma_start(rows[ROW_BMOD:ROW_C], a["b_mod"].rearrange("l (r n) -> (l r) n", n=P)).then_inc(rows_in, 16)
            sp.dma_start(rows[ROW_C:ROW_CCTX], a["c"].rearrange("b (r n) -> (b r) n", n=P)).then_inc(rows_in, 16)
            sp.dma_start(rows[ROW_CCTX:ROW_LB], a["c_ctx"].rearrange("(r n) -> r n", n=P)).then_inc(rows_in, 16)
            sp.dma_start(rows[ROW_LB:ROW_HG],
                         a["hgrn_lb_logits"].rearrange("l (r n) -> (l r) n", n=P)).then_inc(rows_in, 16)
            sp.dma_start(rows[ROW_HG:ROW_DG], a["hgrn_norm_g"]).then_inc(rows_in, 16)
            sp.dma_start(rows[ROW_DG:N_ROWS], a["diff_norm_g"]).then_inc(rows_in, 16)
            for g in range(2):
                sp.dma_start(bias[g:g + 1], a["b_mod"][0:1]).then_inc(bias_in, 16)
            w = a["w_mod"][0].rearrange("(c p) (u n) -> u p c n", p=P, n=UNIT)
            for s in range(WSLOTS):
                feed(k, sp, s, w[s])
            with sp.Fori(1, MOD_UNITS // WSLOTS) as i:
                for s in range(WSLOTS):
                    sp.wait_ge(k.w_free, (i - 1) * WSLOTS + (s + 1))
                    sp.dma_start(k.wst[s], w[i * WSLOTS + s]).then_inc(k.w_landed[s], 16)
            for t in range(LAT_TILES):
                sp.dma_start(k.y[:, t, :], a["x_sample"][0, t * P:(t + 1) * P, :]).then_inc(x_in, 16)
            sp.dma_start(k.y[:, LAT_TILES, :], a["x_prompt"][0]).then_inc(x_in, 16)
            for s, unit in enumerate(in0_units(a)[:WSLOTS]):
                feed(k, sp, BASE_IN0 + s, unit, (k.w_free, MOD_UNITS - WSLOTS + s + 1))
            sp.wait_ge(row_ready, MOD_UNITS + LEAD)
            sp.dma_start(k.dram["mod_rows"][0], mrows).then_inc(rows_out, 16)
            sp.wait_ge(rows_out, 16)
            sp.wait_ge(x_in, 16 * TILES)

        @block.tensor
        def _(pe):
            pe.wait_ge(consts_in, 32)
            pe.wait_ge(rows_in, 96)
            nc.tensor.transpose(k.bank(1)[:, 0:N_ROWS], rows[0:N_ROWS, :], k.ident[0:N_ROWS, 0:N_ROWS]).then_inc(rows_turned, 1)
            pe.wait_ge(sc_ready, 1)
            with pe.Fori(0, MOD_UNITS // WSLOTS) as i:
                for s in range(WSLOTS):
                    pe.wait_ge(k.w_landed[s], i * 16 + 16)
                    pe.wait_ge(row_ready, i * WSLOTS + (s - WSLOTS + 1 + LEAD))
                    for c in range(KC):
                        last = nc.tensor.matmul(k.bank(2 + s)[0:2, 0:UNIT], sc[:, c, :], k.wst[s][:, c, :],
                                                start=(c == 0), stop=(c == KC - 1))
                    last.then_inc(k.w_free, 1)
            pe.wait_ge(row_ready, MOD_UNITS + LEAD)
            for r in range(48):
                last = nc.tensor.transpose(k.bank(0)[:, 2 * r:2 * r + 2], mrows[:, r * P:(r + 1) * P], k.ident[0:2, 0:2])
            last.then_inc(mod_turned, 1)

        @block.scalar
        def _(act):
            act.wait_ge(cols_ready, 1)
            nc.scalar.activation(sc, k.cols[:, ROW_C:ROW_LB].rearrange("p (g c) -> p c g", g=2),
                                 ACT.Silu).then_inc(sc_ready, 1)

        @block.vector
        def _(dve):
            chain = Chain(k, dve, "mod_dve")
            dve.wait_ge(rows_turned, 1)
            nc.vector.tensor_copy(k.cols, k.bank(1)[:, 0:N_ROWS]).then_inc(cols_ready, 1)
            dve.wait_ge(bias_in, 32)
            row_units, bias_units = (x.rearrange("p (u n) -> p u n", n=UNIT) for x in (mrows, bias))
            with dve.Fori(0, MOD_UNITS // WSLOTS) as i:
                for s in range(WSLOTS):
                    dve.wait_ge(k.w_free, i * WSLOTS + (s + 1))
                    nc.vector.tensor_tensor(row_units[:, i * WSLOTS + s, :], k.bank(2 + s)[0:2, 0:UNIT],
                                            bias_units[:, i * WSLOTS + s, :], ALU.add).then_inc(row_ready, 1)
            dve.wait_ge(mod_turned, 1)
            chain.link(nc.vector.tensor_copy(k.mod[0], k.bank(0)[:, 0:96].rearrange("p (c g) -> p c g", g=2)))
            for part in (SC1, SC2):
                nc.vector.tensor_scalar(k.mod[0][:, part:part + KC, :], k.mod[0][:, part:part + KC, :], 1.0, None, ALU.add)


def phase_modulate(k, l, shift, scale, tag):
    nc = k.nc
    turned, lat_out, ctx_out = k.sem(f"turned_{tag}"), k.sem(f"lat_out_{tag}"), k.sem(f"ctx_out_{tag}")
    with nc.Block() as block:
        @block.tensor
        def _(pe):
            for c in range(KC):
                if c >= 2:
                    pe.wait_ge(lat_out, c - 1)
                    pe.wait_ge(ctx_out, c - 1)
                for t in range(LAT_TILES):
                    nc.tensor.transpose(k.bank(c % 2)[:, t * P:(t + 1) * P], k.y[:, t, c * P:(c + 1) * P], k.ident)
                nc.tensor.transpose(k.bank(2 + c % 2)[:, 0:P], k.y[:, LAT_TILES, c * P:(c + 1) * P],
                                    k.ident).then_inc(turned, 1)

        @block.scalar
        def _(act):
            for c in range(KC):
                act.wait_ge(turned, c + 1)
                nc.scalar.activation(k.h[:, c, 0:NS], k.bank(c % 2), ACT.Identity,
                                     scale=k.mod[l][:, scale + c, 0:1], bias=k.mod[l][:, shift + c, 0:1]).then_inc(lat_out, 1)

        @block.vector
        def _(dve):
            for c in range(KC):
                dve.wait_ge(turned, c + 1)
                nc.vector.tensor_scalar(k.h[:, c, NS:NT], k.bank(2 + c % 2)[:, 0:P], k.mod[l][:, scale + c, 1:2],
                                        k.mod[l][:, shift + c, 1:2], ALU.mult, ALU.add).then_inc(ctx_out, 1)


IN0_ORDER = [0, 1, 2, 3, 4, 5, 8, 9, 10, 11, 12, 13, 6, 7, 14, 15]
CQ, CFF, CFB, CG, CQB, CKB = 0, 4, 8, 12, 16, 20


def in0_units(a):
    v = a["w_in_even"][0].rearrange("(c p) (u n) -> u p c n", p=P, n=UNIT)
    return [v[u] for u in IN0_ORDER]


def in1_units(a):
    return w_units(a["w_in_odd"][0], 0, N_IN1)


def project_feature_major(k, pe, w_slot, e, bank_lat, bank_ctx):
    nc = k.nc
    for c in range(KC):
        w = k.wst[w_slot][:, c, e * P:(e + 1) * P]
        nc.tensor.matmul(bank_lat, w, k.h[:, c, 0:NS], start=(c == 0), stop=(c == KC - 1))
        last = nc.tensor.matmul(bank_ctx, w, k.h[:, c, NS:NT], start=(c == 0), stop=(c == KC - 1))
    return last


def phase_project_even(k, a):
    nc = k.nc
    proj = k.at(k.RING, 24 * NT).rearrange("p (c n) -> p c n", n=NT)
    va = k.at(15360, 2560).rearrange("p (t n) -> p t n", t=TILES)
    vb = k.at(17920, 2560).rearrange("p (t n) -> p t n", t=TILES)
    kout = k.at(20480, 512)
    done, lat_out, ctx_out = k.sem("proj_done"), k.sem("proj_lat_out"), k.sem("proj_ctx_out")
    tok_done, tok_out, k_turned, kout_ready, stored = (
        k.sem(n) for n in ("ptok_done", "ptok_out", "k_turned", "kout_ready", "kv_stored"))
    b16 = BASE_IN0 // WSLOTS
    with nc.Block() as block:
        @block.sync
        def _(sp):
            for sem in (lat_out, ctx_out):
                sp.sem_inc(sem, LEAD)
            src = in0_units(a)
            for u in range(WSLOTS, N_IN0):
                feed(k, sp, BASE_IN0 + u, src[u], (done, 2 * (u - WSLOTS) + 2))
            sp.wait_ge(tok_out, 4 * TILES)
            sp.dma_start(a["out_diff_v"].rearrange("h t d -> t h d"),
                         vb[:, LAT_TILES, :].rearrange("p (h d) -> p h d", h=HEADS_B)).then_inc(stored, 16)
            sp.wait_ge(kout_ready, 1)
            sp.dma_start(a["out_diff_k"].rearrange("h t d -> t h d"),
                         kout.rearrange("p (h d) -> p h d", h=HEADS_B)).then_inc(stored, 16)
            sp.wait_ge(stored, 32)

        @block.tensor
        def _(pe):
            with pe.Fori(0, 3) as i:
                for s in range(WSLOTS):
                    pe.wait_ge(k.w_landed[s], i * 16 + 16 * (b16 + 1))
                    for e in range(2):
                        q = 2 * s + e
                        pe.wait_ge(lat_out, i * 8 + max(q - 1, 0) + LEAD)
                        pe.wait_ge(ctx_out, i * 8 + max(q - 1, 0) + LEAD)
                        last = project_feature_major(k, pe, s, e, k.bank(e), k.bank(2 + e)[:, 0:P])
                        last.then_inc(done, 1)
            for s in range(WSLOTS):
                pe.wait_ge(k.w_landed[s], 16 * (b16 + 4))
                for t in range(TILES):
                    g = s * TILES + t
                    if g >= 2:
                        pe.wait_ge(tok_out, g - 1)
                    for c in range(KC):
                        last = nc.tensor.matmul(k.bank(4 + g % 2)[:, 0:UNIT], k.h[:, c, t * P:(t + 1) * P],
                                                k.wst[s][:, c, :], start=(c == 0), stop=(c == KC - 1))
                    last.then_inc(tok_done, 1)
            pe.wait_ge(ctx_out, 24 + LEAD)
            for hd in range(HEADS_B):
                last = nc.tensor.transpose(k.bank(6)[:, hd * P:(hd + 1) * P], proj[:, CKB + hd, NS:NT], k.ident)
            last.then_inc(k_turned, 1)

        @block.scalar
        def _(act):
            with act.Fori(0, 3) as i:
                for q in range(8):
                    act.wait_ge(done, i * 8 + q + 1)
                    nc.scalar.copy(proj[:, i * 8 + q, 0:NS], k.bank(q % 2)).then_inc(lat_out, 1)

        @block.vector
        def _(dve):
            with dve.Fori(0, 3) as i:
                for q in range(8):
                    dve.wait_ge(done, i * 8 + q + 1)
                    nc.vector.tensor_copy(proj[:, i * 8 + q, NS:NT], k.bank(2 + q % 2)[:, 0:P]).then_inc(ctx_out, 1)
            for s in range(WSLOTS):
                for t in range(TILES):
                    g = s * TILES + t
                    dve.wait_ge(tok_done, g + 1)
                    dst = va if s < 2 else vb
                    nc.vector.tensor_copy(dst[:, t, (s % 2) * UNIT:(s % 2 + 1) * UNIT],
                                          k.bank(4 + g % 2)[:, 0:UNIT]).then_inc(tok_out, 1)
            dve.wait_ge(k_turned, 1)
            nc.vector.tensor_copy(kout, k.bank(6)).then_inc(kout_ready, 1)


def phase_hgrn(k, a):
    nc = k.nc
    MOD_HEAD = MOD_UNITS // HEADS_A
    MSLOTS = 3
    LEAD = MSLOTS
    halves_at = {-1: [0, 1, 2, 3], 0: [4], 1: [5], 2: [6], 3: [7], 4: [8], 5: [9], 6: [10], 7: [11]}
    stage = k.at(k.WST + 2048 * MSLOTS, MOD_HEAD * UNIT).rearrange("p (u n) -> p u n", n=UNIT)[0:2]
    proj = k.at(k.RING, 24 * NT).rearrange("p (c n) -> p c n", n=NT)
    va = k.at(15360, 2560).rearrange("p (t h n) -> p t h n", t=TILES, h=HEADS_A)
    NB = NT // CH

    class Dir:
        pass
    dirs = []
    for d, base in enumerate((k.H, 20480)):
        x = Dir()
        x.e, x.qi, x.kh, x.kdec, x.kend, x.qdec = (k.at(base + NT * j, NT) for j in range(6))
        x.z = (CFF, CFB)[d]
        x.a = k.at(base + 6 * NT, NB)
        x.A, x.B = (0, 1) if d == 0 else (1, 0)
        x.end = SUB - 1 if d == 0 else 0
        x.tiles = [0, 1, 2, 3, 4] if d == 0 else [3, 2, 1, 0, 4]
        x.steps = [0, 1, 2, 3] if d == 0 else [3, 2, 1, 0]
        x.S = k.at(k.MX + 2560 + 1024 * d, 1024).rearrange("p (s n) -> p s n", s=8)
        x.S0 = k.at(k.MX + 2560 + 2048 + P * d, P)
        dirs.append(x)
    zero = k.at(k.MX + 2560 + 2304, P)
    ones = k.at(k.MX + 2560 + 2432, P)
    sc0 = k.scr
    keep = k.at(sc0, 641)
    masks = k.at(sc0 + 644, 384).bitcast(I32).rearrange("p (d n) -> p d n", d=2)
    vh = k.at(sc0 + 1028, NT).rearrange("p (t n) -> p t n", t=TILES)
    vblk = k.at(sc0 + 1668, 1024).rearrange("p (b j n) -> p b j n", b=2, j=4)
    scm = k.at(sc0 + 2692, 384).rearrange("p (b n) -> p b n", b=2)
    khT = k.at(sc0 + 3076, 256).rearrange("p (b n) -> p b n", b=2)
    bmask = k.at(sc0 + 3332, 4)
    lbx = k.at(sc0 + 3336, 12).rearrange("p (l h) -> p l h", h=4)
    lbm = k.at(sc0 + 3348, 4)
    lb, oml, lbs = k.at(sc0 + 3352, 8), k.at(sc0 + 3360, 8), k.at(sc0 + 3368, 4)
    lbe = k.at(sc0 + 3372, 12).rearrange("p (l h) -> p l h", h=4)

    names = ("h_const", "h_s0", "h_lbsub", "h_lbexp", "h_lb", "h_sig", "h_f", "h_ln", "h_scan", "h_exp", "h_sub",
             "h_kexp", "h_gates", "h_vh", "h_vblk", "h_sc", "h_and", "h_kt", "h_kht", "h_u", "h_upd", "h_pv",
             "h_inter", "h_state_out", "h_sq", "h_ms", "h_rstd", "h_fin", "h_zero", "h_silu", "h_key", "h_m_landed0", "h_m_landed1", "h_m_landed2", "h_m_done", "h_m_row",
             "h_m_stored")
    S = {n[2:]: k.sem(n) for n in names}
    STEPS = 2 * TILES

    def halves(ap):
        return ap.rearrange("p (c h t) -> p c h t", h=2, t=SUB)

    def step(s):
        d = dirs[s % 2]
        return d, s % 2, s // 2, d.tiles[s // 2]

    def state_before(d, n, j):
        if j:
            return d.S[:, 4 * (n % 2) + j - 1, :]
        if n == 0:
            return d.S0
        if n == LAT_TILES:
            return zero
        return d.S[:, 4 * ((n - 1) % 2) + 3, :]

    with nc.Block() as block:
        @block.sync
        def _(sp):
            for name in ("gates", "m_done", "m_row", "m_stored", "inter", "u", "fin", "state_out", "pv", "and", "kht", "upd", "rstd"):
                sp.sem_inc(S[name], LEAD)
            sp.dma_start(keep, a["keep"]).then_inc(S["const"], 16)
            sp.dma_start(masks, a["hgrn_masks"]).then_inc(S["const"], 16)
            sp.dma_start(bmask, a["bmask"]).then_inc(S["const"], 16)
            wm = a["w_mod"][1].rearrange("(c p) (u n) -> u p c n", p=P, n=UNIT)
            raw = k.dram["mod_raw"].rearrange("g (h u n) -> h g u n", h=HEADS_A, n=UNIT)
            with sp.Fori(0, HEADS_A) as i:
                sp.wait_ge(S["inter"], STEPS * i + LEAD)
                for d in range(2):
                    sp.dma_start(dirs[d].S0, a["state_hgrn"][0, 0, d, i]).then_inc(S["s0"], 16)
                for x in range(MOD_HEAD):
                    sp.wait_ge(S["m_done"], i * MOD_HEAD + (x - MSLOTS + 1 + LEAD))
                    sp.dma_start(k.wst[x % MSLOTS], wm[i * MOD_HEAD + x]).then_inc(S[f"m_landed{x % MSLOTS}"], 16)
                sp.wait_ge(S["m_row"], i * MOD_HEAD + (MOD_HEAD + LEAD))
                sp.dma_start(raw[i], stage).then_inc(S["m_stored"], 16)
                sp.wait_ge(S["upd"], STEPS * i + STEPS + LEAD)
                for d in range(2):
                    sp.dma_start(a["out_state"][d, i], dirs[d].S[:, 3, :]).then_inc(S["state_out"], 16)
            sp.wait_ge(S["state_out"], 32 * HEADS_A + LEAD)
            sp.wait_ge(S["m_stored"], 16 * HEADS_A + LEAD)

        @block.gpsimd
        def _(pool):
            nc.gpsimd.memset(zero, 0.0).then_inc(S["zero"], 1)
            nc.gpsimd.memset(ones, 1.0 / P).then_inc(S["zero"], 1)
            pool.wait_ge(S["const"], 48)
            with pool.Fori(0, HEADS_A) as i:
                pool.wait_ge(S["inter"], STEPS * i + LEAD)
                nc.gpsimd.tensor_copy(vh, va[:, :, i, :]).then_inc(S["vh"], 1)
                pool.wait_ge(S["vh"], i + 1)
                for s in range(STEPS):
                    _, _, _, t = step(s)
                    pool.wait_ge(S["u"], STEPS * i + max(s - 1, 0) + LEAD)
                    nc.gpsimd.tensor_tensor(
                        vblk[:, s % 2], vh[:, t, :].rearrange("p (o n) -> p o n", o=1).broadcast_to([P, 4, P]),
                        bmask.rearrange("p (j o) -> p j o", o=1).broadcast_to([P, 4, P]), ALU.mult).then_inc(S["vblk"], 1)

        @block.scalar
        def _(act):
            act.wait_ge(S["lbsub"], 1)
            nc.scalar.activation(lbe, lbx, ACT.Exp).then_inc(S["lbexp"], 1)
            nc.scalar.activation(proj[:, CG:CG + 4, :], proj[:, CG:CG + 4, :], ACT.Silu).then_inc(S["silu"], 1)

            def sigmoid(i, ahead, d, negative):
                x = dirs[d]
                z = proj[:, i + (x.z + ahead), :]
                if negative:
                    nc.scalar.activation(z, z, ACT.Sigmoid, scale=-1.0).then_inc(S["sig"], 1)
                else:
                    act.wait_ge(S["gates"], 2 * i + (2 * ahead + LEAD))
                    nc.scalar.activation(x.e, z, ACT.Sigmoid).then_inc(S["sig"], 1)

            def log(i, ahead, d):
                act.wait_ge(S["f"], 2 * i + (2 * ahead + d + 1))
                nc.scalar.activation(dirs[d].e, dirs[d].e, ACT.Ln).then_inc(S["ln"], 1)

            for d in range(2):
                sigmoid(0, 0, d, False)
                sigmoid(0, 0, d, True)
            for d in range(2):
                log(0, 0, d)
            with act.Fori(0, HEADS_A) as i:
                act.wait_ge(S["fin"], i + LEAD)
                for d, x in enumerate(dirs):
                    act.wait_ge(S["scan"], 2 * i + d + 1)
                    nc.scalar.activation(x.kdec, x.e, ACT.Exp, scale=-1.0).then_inc(S["exp"], 1)
                    act.wait_ge(S["sub"], 2 * i + d + 1)
                    nc.scalar.activation(x.kend, x.kend, ACT.Exp).then_inc(S["kexp"], 1)
                    nc.scalar.activation(x.e, x.e, ACT.Exp).then_inc(S["exp"], 1)
                for s in range(STEPS):
                    act.wait_ge(S["kt"], STEPS * i + s + 1)
                    act.wait_ge(S["u"], STEPS * i + max(s - 1, 0) + LEAD)
                    nc.scalar.copy(khT[:, s % 2, :], k.bank(4)[:, 0:P]).then_inc(S["kht"], 1)
                    if s in (0, 1, 2, 3):
                        sigmoid(i, 1, s // 2, s % 2 == 1)
                    if s in (5, 6):
                        log(i, 1, s - 5)
                act.wait_ge(S["inter"], STEPS * i + STEPS + LEAD)
                ob, sq = dirs[0].kdec, dirs[1].kdec
                nc.scalar.copy(ob[:, 0:NS], k.bank(0))
                nc.scalar.copy(ob[:, NS:NT], k.bank(1)[:, 0:P])
                nc.scalar.activation(sq[:, 0:NS], k.bank(0), ACT.Square)
                nc.scalar.activation(sq[:, NS:NT], k.bank(1)[:, 0:P], ACT.Square).then_inc(S["sq"], 1)
                act.wait_ge(S["ms"], i + 1)
                act.wait_ge(S["sq"], i + 1)
                rs = dirs[1].qdec
                nc.scalar.activation(rs[:, 0:NS], k.bank(2), ACT.Ln, bias=k.eps).then_inc(S["rstd"], 1)
                nc.scalar.activation(rs[:, NS:NT], k.bank(3)[:, 0:P], ACT.Ln, bias=k.eps).then_inc(S["rstd"], 1)
                act.wait_ge(S["rstd"], 3 * i + 2 + LEAD)
                nc.scalar.activation(rs, rs, ACT.Exp, scale=-0.5).then_inc(S["rstd"], 1)

        @block.vector
        def _(dve):
            c = Chain(k, dve, "hgrn_dve")
            lg = k.cols[:, ROW_LB:ROW_HG].rearrange("p (l h) -> p l h", h=4)
            c.link(nc.vector.tensor_tensor(lbm, lg[:, 0, :], lg[:, 1, :], ALU.max))
            c.link(nc.vector.tensor_tensor(lbm, lbm, lg[:, 2, :], ALU.max))
            for r in range(3):
                last = nc.vector.tensor_tensor(lbx[:, r, :], lg[:, r, :], lbm, ALU.subtract)
            last.then_inc(S["lbsub"], 1)
            dve.wait_ge(S["lbexp"], 1)
            nc.vector.memset(lb, 1.0)
            c.link(nc.vector.memset(oml, 0.0))
            c.link(nc.vector.tensor_tensor(lbs, lbe[:, 0, :], lbe[:, 1, :], ALU.add))
            c.link(nc.vector.tensor_tensor(lbs, lbs, lbe[:, 2, :], ALU.add))
            c.link(nc.vector.reciprocal(lbs, lbs))
            c.link(nc.vector.tensor_tensor(lb[:, 0:4], lbe[:, 0, :], lbs, ALU.mult))
            c.link(nc.vector.tensor_scalar(oml[:, 0:4], lb[:, 0:4], -1.0, 1.0, ALU.mult, ALU.add))
            dve.wait_ge(S["const"], 48)
            dve.wait_ge(S["zero"], 2)

            def forget(i, ahead, d):
                x = dirs[d]
                dve.wait_ge(S["sig"], 4 * i + (4 * ahead + 2 * d + 2))
                head = bass.ds(i + ahead, 1)
                key = proj[:, i + (x.z + ahead), :]
                nc.vector.tensor_scalar(x.e, x.e, oml[:, head], lb[:, head], ALU.mult, ALU.add).then_inc(S["f"], 1)
                nc.vector.tensor_scalar(key, key, oml[:, head], None, ALU.mult).then_inc(S["key"], 1)

            def running_sum(i, ahead, d):
                x = dirs[d]
                dve.wait_ge(S["ln"], 2 * i + (2 * ahead + d + 1))
                if d == 0:
                    op = nc.vector.tensor_tensor_scan(x.e, keep[:, 0:NT], x.e, 0.0, ALU.mult, ALU.add)
                else:
                    op = nc.vector.tensor_tensor_scan(x.e[:, ::-1], keep[:, 1:NT + 1][:, ::-1], x.e[:, ::-1],
                                                      0.0, ALU.mult, ALU.add)
                op.then_inc(S["scan"], 1)

            for d in range(2):
                forget(0, 0, d)
            for d in range(2):
                running_sum(0, 0, d)
            with dve.Fori(0, HEADS_A) as i:
                c.enter(i, 3 * STEPS + 3)
                dve.wait_ge(S["m_stored"], 16 * i + LEAD)

                def modulation_row(x):
                    dve.wait_ge(S["m_done"], i * MOD_HEAD + (x + 1 + LEAD))
                    nc.vector.tensor_copy(stage[:, x, :], k.bank(5)[0:2, 0:UNIT]).then_inc(S["m_row"], 1)

                dve.wait_ge(S["key"], 2 * i + 2)
                for d, x in enumerate(dirs):
                    dve.wait_ge(S["scan"], 2 * i + d + 1)
                    b3 = x.e.rearrange("p (c t) -> p c t", t=SUB)
                    nc.vector.tensor_tensor(x.kend.rearrange("p (c t) -> p c t", t=SUB),
                                            b3[:, :, x.end:x.end + 1].broadcast_to([P, NT // SUB, SUB]), b3,
                                            ALU.subtract).then_inc(S["sub"], 1)
                modulation_row(0)
                for d, x in enumerate(dirs):
                    key = proj[:, i + x.z, :]
                    dve.wait_ge(S["exp"], 4 * i + 2 * d + 2)
                    nc.vector.tensor_tensor(x.qdec, proj[:, CQ + i, :], x.e, ALU.mult)
                    nc.vector.tensor_tensor(x.kdec, x.kdec, key, ALU.mult)
                    dve.wait_ge(S["kexp"], 2 * i + d + 1)
                    c.link(nc.vector.tensor_tensor(x.kend, x.kend, key, ALU.mult))
                    e4, q4, qi4, ke4, kh4 = (halves(v) for v in (x.e, x.qdec, x.qi, x.kend, x.kh))
                    endA = e4[:, :, x.A, x.end:x.end + 1]
                    endB = e4[:, :, x.B, x.end:x.end + 1]
                    nc.vector.tensor_copy(qi4[:, :, x.A, :], q4[:, :, x.A, :])
                    nc.vector.tensor_tensor(qi4[:, :, x.B, :], q4[:, :, x.B, :], endA.broadcast_to([P, NB, SUB]), ALU.mult)
                    nc.vector.tensor_copy(kh4[:, :, x.B, :], ke4[:, :, x.B, :])
                    nc.vector.tensor_tensor(kh4[:, :, x.A, :], ke4[:, :, x.A, :], endB.broadcast_to([P, NB, SUB]), ALU.mult)
                    nc.vector.tensor_tensor(x.a.rearrange("p (c o) -> p c o", o=1), endA, endB,
                                            ALU.mult).then_inc(S["gates"], 1)
                    if d == 0:
                        modulation_row(1)
                dve.wait_ge(S["s0"], 32 * i + 32)
                dve.wait_ge(S["state_out"], 32 * i + LEAD)
                dve.wait_ge(S["gates"], 2 * i + (2 + LEAD))
                for s in range(STEPS):
                    for half in (halves_at.get(s - 1, []) if s else []):
                        if half % 2:
                            modulation_row(half // 2)
                    x, dn, n, t = step(s)
                    dve.wait_ge(S["sc"], STEPS * i + s + 1)
                    dve.wait_ge(S["pv"], STEPS * i + max(s - 1, 0) + LEAD)
                    nc.vector.tensor_tensor(scm[:, s % 2, :].bitcast(I32), k.bank(2 + s % 2)[:, 0:192].bitcast(I32),
                                            masks[:, dn, :], ALU.bitwise_and).then_inc(S["and"], 1)
                    dve.wait_ge(S["u"], STEPS * i + s + 1 + LEAD)
                    dve.wait_ge(S["inter"], STEPS * i + max(s - 3, 0) + LEAD)
                    for j, m in enumerate(x.steps):
                        op = nc.vector.scalar_tensor_tensor(
                            out=x.S[:, 4 * (n % 2) + j, :], in0=state_before(x, n, j),
                            scalar=x.a[:, 4 * t + m:4 * t + m + 1], in1=k.bank(6 + s % 2)[:, m * P:(m + 1) * P],
                            op0=ALU.mult, op1=ALU.add)
                        if j == 3:
                            op.then_inc(S["upd"], 1)
                            dve.wait_ge(S["upd"], STEPS * i + s + 1 + LEAD)
                        else:
                            c.link(op)
                    if s in (2, 4):
                        forget(i, 1, s // 2 - 1)
                    if s in (6, 7):
                        running_sum(i, 1, s - 6)
                ob, rs = dirs[0].kdec, dirs[1].qdec
                dve.wait_ge(S["silu"], 1)
                dve.wait_ge(S["rstd"], 3 * i + 3 + LEAD)
                dve.wait_ge(S["sq"], i + 1)
                c.link(nc.vector.scalar_tensor_tensor(out=ob, in0=ob, scalar=k.cols[:, ROW_HG:ROW_HG + 1], in1=rs,
                                                      op0=ALU.mult, op1=ALU.mult))
                nc.vector.tensor_tensor(k.mx[:, i, :], ob, proj[:, CG + i, :], ALU.mult).then_inc(S["fin"], 1)
                c.leave(HEADS_A)

        @block.tensor
        def _(pe):
            pe.wait_ge(S["zero"], 2)
            with pe.Fori(0, HEADS_A) as i:
                def before(s):
                    x, dn, n, t = step(s)
                    tile = slice(t * P, (t + 1) * P)
                    if s < 2:
                        pe.wait_ge(S["gates"], 2 * i + (s + 1 + LEAD))
                    pe.wait_ge(S["and"], STEPS * i + max(s - 1, 0) + LEAD)
                    nc.tensor.matmul(k.bank(2 + s % 2)[:, 0:P], x.kdec[:, tile], x.qdec[:, tile], start=True, stop=True)
                    qB = halves(x.qdec)[:, 4 * t:4 * t + 4, x.B, :]
                    nc.tensor.matmul(k.bank(2 + s % 2)[:, P:192], x.kend[:, tile], qB,
                                     start=True, stop=True).then_inc(S["sc"], 1)
                    pe.wait_ge(S["kht"], STEPS * i + s + LEAD)
                    nc.tensor.transpose(k.bank(4)[:, 0:P], x.kh[:, tile], k.ident).then_inc(S["kt"], 1)

                def products(s):
                    x, dn, n, t = step(s)
                    pe.wait_ge(S["kht"], STEPS * i + s + 1 + LEAD)
                    pe.wait_ge(S["vblk"], STEPS * i + s + 1)
                    pe.wait_ge(S["upd"], STEPS * i + max(s - 1, 0) + LEAD)
                    nc.tensor.matmul(k.bank(6 + s % 2), khT[:, s % 2, :], vblk[:, s % 2].rearrange("p j n -> p (j n)"),
                                     start=True, stop=True).then_inc(S["u"], 1)
                    pe.wait_ge(S["and"], STEPS * i + s + 1 + LEAD)
                    o = k.bank(0) if t < LAT_TILES else k.bank(1)[:, 0:P]
                    c0 = t * P if t < LAT_TILES else 0
                    nc.tensor.matmul(o[:, c0:c0 + P], vh[:, t, :], scm[:, s % 2, 0:P], start=(s in (0, 8)), stop=False,
                                     skip_group_check=True)
                    oB = o[:, c0:c0 + P].rearrange("p (c h t) -> p c h t", h=2, t=SUB)[:, :, x.B, :]
                    nc.tensor.matmul(oB, vh[:, t, :], scm[:, s % 2, P:192], start=False, stop=False,
                                     skip_group_check=True).then_inc(S["pv"], 1)

                def states(s):
                    x, dn, n, t = step(s)
                    o = k.bank(0) if t < LAT_TILES else k.bank(1)[:, 0:P]
                    c0 = t * P if t < LAT_TILES else 0
                    pe.wait_ge(S["upd"], STEPS * i + s + 1 + LEAD)
                    for j, m in enumerate(x.steps):
                        cols = slice(t * P + m * CH, t * P + (m + 1) * CH)
                        last = nc.tensor.matmul(o[:, c0 + m * CH:c0 + (m + 1) * CH], state_before(x, n, j), x.qi[:, cols],
                                                start=False, stop=(s >= STEPS - 3 and j == 3), skip_group_check=True)
                    last.then_inc(S["inter"], 1)

                def modulation(half):
                    x, part = divmod(half, 2)
                    if part == 0:
                        pe.wait_ge(S[f"m_landed{x % MSLOTS}"], i * 32 + 16 * (x // MSLOTS + 1))
                        pe.wait_ge(S["m_row"], i * MOD_HEAD + (x + LEAD))
                    for c in range(4 * part, 4 * part + 4):
                        last = nc.tensor.matmul(k.bank(5)[0:2, 0:UNIT], k.silu_c[:, c, :], k.wst[x % MSLOTS][:, c, :],
                                                start=(c == 0), stop=(c == KC - 1))
                    if part:
                        last.then_inc(S["m_done"], 1)

                for half in halves_at[-1]:
                    modulation(half)
                pe.wait_ge(S["fin"], i + LEAD)
                pe.wait_ge(S["rstd"], 3 * i + LEAD)
                before(0)
                pe.wait_ge(S["vh"], i + 1)
                for s in range(STEPS):
                    products(s)
                    if s + 1 < STEPS:
                        before(s + 1)
                    for half in halves_at.get(s, []):
                        modulation(half)
                    states(s)
                pe.wait_ge(S["sq"], i + 1)
                sq = dirs[1].kdec
                nc.tensor.matmul(k.bank(2), ones, sq[:, 0:NS], start=True, stop=True)
                nc.tensor.matmul(k.bank(3)[:, 0:P], ones, sq[:, NS:NT], start=True, stop=True).then_inc(S["ms"], 1)


def phase_project_odd(k, a):
    nc = k.nc
    proj = k.at(k.RING, 10 * NT).rearrange("p (c n) -> p c n", n=NT)
    v = k.at(6400, 1280).rearrange("p (t n) -> p t n", t=TILES)
    kout = k.at(7680, 256)
    done, lat_out, ctx_out = k.sem("oproj_done"), k.sem("oproj_lat_out"), k.sem("oproj_ctx_out")
    tok_done, tok_out, k_turned, kout_ready, stored = (
        k.sem(n) for n in ("otok_done", "otok_out", "ok_turned", "okout_ready", "okv_stored"))
    with nc.Block() as block:
        @block.sync
        def _(sp):
            for u, s in enumerate(in1_units(a)):
                if u >= WSLOTS:
                    feed(k, sp, BASE_IN1 + u, s, (done, 2 * (u - WSLOTS) + 2))
            for u, s in enumerate(w_units(a["w_out_odd"][0], 0, 4)):
                feed(k, sp, BASE_OUT1 + u, s, (done, 2 * (u + 2) + 2) if u < 3 else (tok_done, TILES))
            sp.wait_ge(tok_out, TILES)
            sp.dma_start(a["out_win_v"].rearrange("h t d -> t h d"),
                         v[:, LAT_TILES, :].rearrange("p (h d) -> p h d", h=4)).then_inc(stored, 16)
            sp.wait_ge(kout_ready, 1)
            sp.dma_start(a["out_win_k"].rearrange("h t d -> t h d"),
                         kout.rearrange("p (h d) -> p h d", h=4)).then_inc(stored, 16)
            sp.wait_ge(stored, 32)

        @block.tensor
        def _(pe):
            for u in range(N_IN1):
                n = BASE_IN1 + u
                pe.wait_ge(k.w_landed[n % WSLOTS], 16 * (n // WSLOTS + 1))
                if u < 5:
                    for e in range(2):
                        q = 2 * u + e
                        if q >= 2:
                            pe.wait_ge(lat_out, q - 1)
                            pe.wait_ge(ctx_out, q - 1)
                        last = project_feature_major(k, pe, n % WSLOTS, e, k.bank(e), k.bank(2 + e)[:, 0:P])
                        last.then_inc(done, 1)
                else:
                    for t in range(TILES):
                        if t >= 2:
                            pe.wait_ge(tok_out, t - 1)
                        for c in range(KC):
                            last = nc.tensor.matmul(k.bank(4 + t % 2)[:, 0:UNIT], k.h[:, c, t * P:(t + 1) * P],
                                                    k.wst[n % WSLOTS][:, c, :], start=(c == 0), stop=(c == KC - 1))
                        last.then_inc(tok_done, 1)
            pe.wait_ge(ctx_out, 10)
            for c in range(2):
                last = nc.tensor.transpose(k.bank(6)[:, c * P:(c + 1) * P], proj[:, 8 + c, NS:NT], k.ident)
            last.then_inc(k_turned, 1)

        @block.scalar
        def _(act):
            for q in range(10):
                act.wait_ge(done, q + 1)
                nc.scalar.copy(proj[:, q, 0:NS], k.bank(q % 2)).then_inc(lat_out, 1)

        @block.vector
        def _(dve):
            for q in range(10):
                dve.wait_ge(done, q + 1)
                nc.vector.tensor_copy(proj[:, q, NS:NT], k.bank(2 + q % 2)[:, 0:P]).then_inc(ctx_out, 1)
            for t in range(TILES):
                dve.wait_ge(tok_done, t + 1)
                nc.vector.tensor_copy(v[:, t, :], k.bank(4 + t % 2)[:, 0:UNIT]).then_inc(tok_out, 1)
            dve.wait_ge(k_turned, 1)
            nc.vector.tensor_copy(kout, k.bank(6)[:, 0:UNIT]).then_inc(kout_ready, 1)


def phase_rope(k, a, odd):
    nc = k.nc
    tag = "o" if odd else "e"
    proj = k.at(k.RING, (10 if odd else 24) * NT).rearrange("p (c n) -> p c n", n=NT)
    first, count = (0, 10) if odd else (CQB, 8)
    nk = 2 if odd else 4
    cos, sin = k.at(k.scr, 512), k.at(k.scr + 512, 512)
    straight = k.at(k.H, 1024).rearrange("p (b n) -> p b n", b=2)
    kctx = k.at(k.H + 1024, 1024).rearrange("p (c n) -> p c n", n=PAST)
    kraw = k.at(20480, 2 * nk * P).rearrange("p (c t n) -> p c t n", t=2, n=P)
    loaded, kraw_in, turned, swapped, mixed, multiplied, summed, kctx_out = (
        k.sem(f"rope_{n}_{tag}") for n in ("loaded", "kraw_in", "turned", "swapped", "mixed", "multiplied", "summed",
                                           "kctx_out"))
    raw, cols96, rows96 = k.at(k.H + 2048, P)[0:96], k.at(k.H + 2176, 96), k.at(k.H + 2272, P)[0:96]
    raw_in, raw_turned, biased, rows_turned, rows_ready, rows_out = (
        k.sem(f"rope_{n}_{tag}") for n in ("raw_in", "raw_turned", "biased", "mrows_turned", "mrows_ready", "mrows_out"))
    with nc.Block() as block:
        @block.sync
        def _(sp):
            for sem in (multiplied, summed):
                sp.sem_inc(sem, LEAD)
            sp.dma_start(cos, a["cos"]).then_inc(loaded, 16)
            sp.dma_start(sin, a["sin"]).then_inc(loaded, 16)
            for c in range(nk):
                for t in range(2):
                    if odd:
                        src = a["cache_win_k"][0, 0, 2 * c:2 * c + 2, t * P:(t + 1) * P, :].rearrange("h t d -> t h d")
                        dst = kraw[:, c, t, :].rearrange("p (h d) -> p h d", h=2)
                    else:
                        src, dst = a["cache_diff_k"][0, 0, c, t * P:(t + 1) * P, :], kraw[:, c, t, :]
                    sp.dma_start(dst, src).then_inc(kraw_in, 16)
            if not odd:
                sp.dma_start(raw, k.dram["mod_raw"].rearrange("g (c n) -> (g c) n", n=P)).then_inc(raw_in, 16)
                sp.wait_ge(rows_ready, 1)
                sp.dma_start(k.dram["mod_rows"][1].rearrange("g (c n) -> (g c) n", n=P), rows96).then_inc(rows_out, 16)
                sp.wait_ge(rows_out, 16)

        @block.tensor
        def _(pe):
            with pe.Fori(0, count // 2) as i:
                for b in range(2):
                    pe.wait_ge(multiplied, 2 * i + 0 + LEAD)
                    nc.tensor.matmul(k.bank(b), k.perm, proj[:, first + i * 2 + b, 0:NS],
                                     start=True, stop=True).then_inc(swapped, 1)
            pe.wait_ge(kraw_in, 32 * nk)
            for c in range(nk):
                for t in range(2):
                    last = nc.tensor.transpose(k.bank(4 + c // 2)[:, (c % 2) * PAST + t * P:(c % 2) * PAST + (t + 1) * P],
                                               kraw[:, c, t, :], k.ident)
            last.then_inc(turned, 1)
            if not odd:
                pe.wait_ge(raw_in, 16)
                nc.tensor.transpose(k.bank(6)[:, 0:96], raw, k.ident[0:96, 0:96]).then_inc(raw_turned, 1)
                pe.wait_ge(biased, 1)
                nc.tensor.transpose(k.bank(7)[0:96, 0:P], cols96, k.ident).then_inc(rows_turned, 1)

        @block.gpsimd
        def _(pool):
            pool.wait_ge(loaded, 32)
            with pool.Fori(0, count // 2) as i:
                for b in range(2):
                    pool.wait_ge(summed, 2 * i + LEAD)
                    nc.gpsimd.tensor_tensor(straight[:, b, :], proj[:, first + i * 2 + b, 0:NS], cos,
                                            ALU.mult).then_inc(mixed, 1)

        @block.vector
        def _(dve):
            dve.wait_ge(loaded, 32)
            with dve.Fori(0, count // 2) as i:
                for b in range(2):
                    x = proj[:, first + i * 2 + b, 0:NS]
                    dve.wait_ge(swapped, 2 * i + b + 1)
                    dve.wait_ge(mixed, 2 * i + b + 1)
                    nc.vector.tensor_tensor(x, k.bank(b), sin, ALU.mult).then_inc(multiplied, 1)
                    dve.wait_ge(multiplied, 2 * i + b + 1 + LEAD)
                    nc.vector.tensor_tensor(x, x, straight[:, b, :], ALU.add).then_inc(summed, 1)
            dve.wait_ge(turned, 1)
            for c in range(nk):
                nc.vector.tensor_copy(kctx[:, c, :], k.bank(4 + c // 2)[:, (c % 2) * PAST:(c % 2 + 1) * PAST])
            if not odd:
                gc, cg = "p (g c) -> p g c", "p (g c) -> p c g"
                dve.wait_ge(raw_turned, 1)
                nc.vector.tensor_tensor(cols96.rearrange(gc, g=2), k.bank(6)[:, 0:96].rearrange(gc, g=2),
                                        k.cols[:, 48:96].rearrange("p (o c) -> p o c", o=1).broadcast_to([P, 2, 48]),
                                        ALU.add).then_inc(biased, 1)
                dve.wait_ge(biased, 1)
                nc.vector.tensor_copy(k.mod[1], cols96.rearrange(cg, g=2)).then_inc(biased, 1)
                dve.wait_ge(biased, 2)
                for part in (SC1, SC2):
                    nc.vector.tensor_scalar(k.mod[1][:, part:part + KC, :], k.mod[1][:, part:part + KC, :], 1.0, None,
                                            ALU.add)
                dve.wait_ge(rows_turned, 1)
                nc.vector.tensor_copy(rows96, k.bank(7)[0:96, 0:P]).then_inc(rows_ready, 1)


def phase_attention(k, a, odd):
    nc = k.nc
    tag = "o" if odd else "e"
    ITER = 8 if odd else HEADS_B
    proj = k.at(k.RING, (10 if odd else 24) * NT).rearrange("p (c n) -> p c n", n=NT)
    kctx = k.at(k.H + 1024, 1024).rearrange("p (c n) -> p c n", n=PAST)
    free = 10240 if odd else 0
    kr = k.at(free, 2 * NT).rearrange("p (b n) -> p b n", b=2)
    kcr = k.at(free + 2 * NT, 2 * PAST).rearrange("p (b n) -> p b n", b=2)
    qz = k.at(free + 2 * NT + 2 * PAST, 4 * NT).rearrange("p (b m n) -> p b m n", b=2, m=2)
    ob = k.at(k.H + 3328, NT).rearrange("p (t n) -> p t n", t=TILES)
    small = k.H + 3968
    negm = k.at(small, 10)
    rsum = k.at(small + 10, 10)
    rinv = k.at(small + 20, 10)
    top = k.at(small + 30, 10)
    esink = k.at(small + 40, 10)
    ssq = k.at(small + 50, 5)
    rstd = k.at(small + 55, 5)
    neglam = k.at(small + 60, 1)
    dots = k.at(small + 61, 2)
    gdiff = k.at(small + 63, 1)
    lamx = k.at(small + 64, 256).rearrange("p (j n) -> p j n", j=4)
    sink = k.at(small + 320, 16)
    t2 = k.at(small + 336, P)
    junk = k.at(small + 464, P)
    tick = k.at(small + 592, 1)
    halves = k.at(small + 600, 2)
    sinkc = k.at(small + 594, 4).rearrange("p (b n) -> p b n", b=2)
    prob = k.at(k.scr + 1024, 1536).rearrange("p (b n) -> p b n", b=2)
    probT = k.at(k.scr + 2560, 1536).rearrange("p (b n) -> p b n", b=2)
    if odd:
        vlat = k.at(6400, 1280).rearrange("p (t h n) -> p t h n", t=TILES, h=4)
        vctx = k.at(8192, 512).rearrange("p (t h n) -> p t h n", t=2, h=4)
        mask = k.at(8704, 768)
    else:
        vlat = k.at(17920, 2560).rearrange("p (t h n) -> p t h n", t=TILES, h=4)
        vctx = k.at(20480, 1024).rearrange("p (t h n) -> p t h n", t=2, h=4)
    S = {n: k.sem(f"at_{n}_{tag}") for n in ("v_in", "dots", "lam", "lam_ready", "q_in", "qk", "max", "small", "exp", "esink",
                                             "pt", "outd", "outa", "pv", "comb", "fold", "ssq", "rstd", "norm", "turned", "stored")}
    UN = 2 * TILES
    V_IN = 80 if odd else 64
    QIN = 5 if odd else 4

    def unit(u):
        t, m = divmod(u, 2)
        if odd:
            t = (1, 2, 0, 3, LAT_TILES)[t]
        if t == LAT_TILES:
            return (t, m, 256, 384) if odd else (t, m, 0, P)
        if odd:
            return t, m, (128 if t else 256), (768 if t < LAT_TILES - 1 else 640)
        return t, m, 0, 768

    def key_tiles(t):
        if t == LAT_TILES:
            return [("own", LAT_TILES)]
        if not odd:
            return [("ctx", 0), ("ctx", 1)] + [("own", j) for j in range(LAT_TILES)]
        return ([("own", t - 1)] if t else []) + [("ctx", 0), ("ctx", 1), ("own", t)] + (
            [("own", t + 1)] if t < LAT_TILES - 1 else [])

    def split(u):
        t, m, lo, hi = unit(u)
        n = (hi - lo) // P
        return n, max(n // 2, 1)

    def outa(i, u):
        return i * (UN - 2) + min(u, UN - 2)

    with nc.Block() as block:
        @block.sync
        def _(sp):
            for name in ("qk", "exp", "max", "outd", "outa", "pv", "comb", "pt"):
                sp.sem_inc(S[name], LEAD)
            for t in range(2):
                src = a["cache_win_v" if odd else "cache_diff_v"][0, 0, :, t * P:(t + 1) * P, :].rearrange("h t d -> t h d")
                sp.dma_start(vctx[:, t], src).then_inc(S["v_in"], 16)
            sp.dma_start(halves, a["halves"]).then_inc(S["v_in"], 16)
            if not odd:
                for u, s in enumerate(w_units(a["w_out_even"][0], 0, 4)):
                    feed(k, sp, BASE_OUT0 + u, s)
            if odd:
                sp.dma_start(sink, bcast_rows(a["win_sink"], 0, [[1, 16]])).then_inc(S["v_in"], 16)
                sp.dma_start(mask, a["wmask"]).then_inc(S["v_in"], 16)
            else:
                sp.dma_start(lamx, bcast_rows(a["diff_lambda"], 0, [[DH, 4], [1, DH]])).then_inc(S["v_in"], 16)

        @block.gpsimd
        def _(pool):
            pool.wait_ge(S["v_in"], V_IN)
            with pool.Fori(0, ITER // 2) as i:
                for b in range(2):
                    pool.wait_ge(S["qk"], 2 * UN * i + LEAD)
                    chunk = (0 if odd else CQB) + i * 2 + b
                    kchunk = i // 2 if odd else i * 2 + b
                    for m in range(2):
                        nc.gpsimd.tensor_tensor(qz[:, b, m, :], proj[:, chunk, :],
                                                halves[:, m:m + 1].broadcast_to([P, NT]), ALU.mult).then_inc(S["q_in"], 1)
                    nc.gpsimd.tensor_copy(kr[:, b, :], proj[:, (8 if odd else CKB) + kchunk, :]).then_inc(S["q_in"], 1)
                    nc.gpsimd.tensor_copy(kcr[:, b, :], kctx[:, kchunk, :]).then_inc(S["q_in"], 1)
                    if odd:
                        pool.wait_ge(S["exp"], 2 * UN * i + LEAD)
                        nc.gpsimd.tensor_copy(sinkc[:, b, :], sink[:, bass.ds(4 * i + 2 * b, 2)]).then_inc(S["q_in"], 1)

        @block.tensor
        def _(pe):
            pe.wait_ge(S["v_in"], V_IN)

            def finish(i):
                if odd:
                    pe.wait_ge(S["comb"], i * UN + UN + LEAD)
                else:
                    pe.wait_ge(S["norm"], i + 1)
                for t in range(TILES):
                    last = nc.tensor.transpose(k.pt[2][:, t * P:(t + 1) * P], ob[:, t, :], k.ident)
                last.then_inc(S["turned"], 1)
                pe.wait_ge(S["stored"], i + 1)

            with pe.Fori(0, ITER // 2) as i2:
                for b in range(2):
                    i = i2 * 2 + b
                    N = i * UN
                    if odd:
                        kchunk = i2 // 2
                    else:
                        kchunk = i

                    def qk(u):
                        t, m, lo, hi = unit(u)
                        q = qz[:, b, m, t * P:(t + 1) * P]
                        dst = k.pt[m]
                        pe.wait_ge(S["max" if odd else "exp"], N + max(u - 1, 0) + LEAD)
                        keys = kr[:, b]

                        def put(col, cols, rhs):
                            return nc.tensor.matmul(dst[:, col:col + cols], q, rhs, start=True, stop=True)
                        if t == LAT_TILES:
                            last = put(lo, P, keys[:, NS:NT])
                        elif odd:
                            if t:
                                put(128, P, keys[:, (t - 1) * P:t * P])
                            put(256, PAST, kcr[:, b, :])
                            last = put(512, hi - 512, keys[:, t * P:t * P + hi - 512])
                        else:
                            put(0, PAST, kcr[:, b, :])
                            put(256, 256, keys[:, 0:256])
                            last = put(512, 256, keys[:, 256:512])
                        last.then_inc(S["qk"], 1)

                    def turn(u):
                        t, m, lo, hi = unit(u)
                        pe.wait_ge(S["exp"], N + u + 1 + LEAD)
                        pe.wait_ge(S["outd"], N + u + LEAD)
                        pe.wait_ge(S["outa"], outa(i, u) + LEAD)
                        n, h = split(u)
                        for j in range(n):
                            dst = k.bank(4)[:, j * P:(j + 1) * P] if j < h else k.bank(5)[:, (j - h) * P:(j - h + 1) * P]
                            last = nc.tensor.transpose(dst, prob[:, u % 2, j * P:(j + 1) * P], k.ident)
                        last.then_inc(S["pt"], 1)

                    def pv(u):
                        t, m, lo, hi = unit(u)
                        pe.wait_ge(S["outd"], N + u + 1 + LEAD)
                        pe.wait_ge(S["outa"], outa(i, u + 1) + LEAD)
                        pe.wait_ge(S["comb"], N + (u if m == 0 and not odd else max(u - 1, 0)) + LEAD)
                        tiles = key_tiles(t)
                        for j, (kind, vt) in enumerate(tiles):
                            if odd:
                                v = (vctx if kind == "ctx" else vlat)[:, vt, bass.ds(kchunk * 2, 2), :]
                                o = k.bank(6 + m)[:, 0:P]
                            else:
                                v = (vctx if kind == "ctx" else vlat)[:, vt, kchunk, :]
                                o = k.bank(6 + m)[:, 0:P]
                            last = nc.tensor.matmul(o, probT[:, u % 2, j * P:(j + 1) * P], v, start=(j == 0),
                                                    stop=(j == len(tiles) - 1))
                        last.then_inc(S["pv"], 1)

                    pe.wait_ge(S["q_in"], QIN * i + QIN)
                    qk(0)
                    for u in range(UN):
                        if u + 1 < UN:
                            qk(u + 1)
                        if u == 0 and b == 1:
                            finish(i2 * 2)
                        turn(u)
                        if u:
                            pv(u - 1)
                    pv(UN - 1)
                    if b == 1:
                        finish(i)

        @block.scalar
        def _(act):
            if not odd:
                act.wait_ge(S["dots"], 2)
                nc.scalar.activation(dots, dots, ACT.Exp).then_inc(S["lam"], 1)
            else:
                act.wait_ge(S["v_in"], V_IN)
            with act.Fori(0, ITER // 2) as i2:
                for b in range(2):
                    i = i2 * 2 + b
                    N = i * UN

                    def evacuate(u):
                        n, h = split(u)
                        if n > h:
                            act.wait_ge(S["pt"], N + u + 1 + LEAD)
                            act.wait_ge(S["pv"], N + max(u - 1, 0) + LEAD)
                            nc.scalar.copy(probT[:, u % 2, h * P:n * P], k.bank(5)[:, 0:(n - h) * P]).then_inc(S["outa"], 1)

                    if odd:
                        act.wait_ge(S["q_in"], QIN * i + QIN)
                    for u in range(UN):
                        t, m, lo, hi = unit(u)
                        act.wait_ge(S["max"], N + u + 1 + LEAD)
                        act.wait_ge(S["small"], N + u + 1)
                        act.wait_ge(S["pt"], N + max(u - 1, 0) + LEAD)
                        if odd:
                            nc.scalar.activation(esink[:, u:u + 1], sinkc[:, b, m:m + 1], ACT.Exp,
                                                 bias=negm[:, u:u + 1]).then_inc(S["esink"], 1)
                            nc.scalar.activation(prob[:, u % 2, 0:hi - lo], prob[:, u % 2, 0:hi - lo], ACT.Exp,
                                                 bias=negm[:, u:u + 1], accum_out=rsum[:, u:u + 1]).then_inc(S["exp"], 1)
                        else:
                            nc.scalar.activation(prob[:, u % 2, 0:hi - lo], k.pt[m][:, lo:hi], ACT.Exp, scale=SCALE,
                                                 bias=negm[:, u:u + 1], accum_out=rsum[:, u:u + 1]).then_inc(S["exp"], 1)
                        if u:
                            evacuate(u - 1)
                    evacuate(UN - 1)
                    if not odd:
                        act.wait_ge(S["ssq"], i + 1)
                        nc.scalar.activation(rstd, ssq, ACT.Ln, scale=1.0 / P, bias=k.eps).then_inc(S["rstd"], 1)
                        act.wait_ge(S["rstd"], 2 * i + 1)
                        nc.scalar.activation(rstd, rstd, ACT.Exp, scale=-0.5).then_inc(S["rstd"], 1)
                    act.wait_ge(S["turned"], i + 1)
                    dst = k.mx[:, (0 if odd else 4) + i, :]
                    if odd:
                        nc.scalar.copy(dst, k.pt[2][:, 0:NT]).then_inc(S["stored"], 1)
                    else:
                        nc.scalar.activation(dst, k.pt[2][:, 0:NT], ACT.Identity, scale=gdiff).then_inc(S["stored"], 1)

        @block.vector
        def _(dve):
            dve.wait_ge(S["v_in"], V_IN)
            c = Chain(k, dve, f"at_dve_{tag}")
            if not odd:
                for j in range(2):
                    nc.vector.tensor_tensor_reduce(junk[:, DH * j:DH * (j + 1)], lamx[:, 2 * j, :], lamx[:, 2 * j + 1, :], 1.0, 0.0,
                                                   ALU.mult, ALU.add, dots[:, j:j + 1]).then_inc(S["dots"], 1)
                dve.wait_ge(S["lam"], 1)
                c.link(nc.vector.tensor_tensor(neglam, dots[:, 1:2], dots[:, 0:1], ALU.subtract))
                c.link(nc.vector.tensor_scalar(neglam, neglam, -LAM_INIT, None, ALU.add))
                c.link(nc.vector.tensor_scalar(gdiff, k.cols[:, ROW_DG:ROW_DG + 1], 1.0 - LAM_INIT, None, ALU.mult))
            with dve.Fori(0, ITER // 2) as i2:
                c.enter(i2, 4 * UN if odd else 4 * TILES - 2)
                for b in range(2):
                    i = i2 * 2 + b
                    N = i * UN

                    def evacuate(u):
                        n, h = split(u)
                        dve.wait_ge(S["pt"], N + u + 1 + LEAD)
                        dve.wait_ge(S["pv"], N + max(u - 1, 0) + LEAD)
                        nc.vector.tensor_copy(probT[:, u % 2, 0:h * P], k.bank(4)[:, 0:h * P]).then_inc(S["outd"], 1)

                    def combine(u):
                        t, m, lo, hi = unit(u)
                        dve.wait_ge(S["pv"], N + u + 1 + LEAD)
                        if odd:
                            dve.wait_ge(S["esink"], N + u + 1)
                            c.link(nc.vector.tensor_tensor(rsum[:, u:u + 1], rsum[:, u:u + 1], esink[:, u:u + 1], ALU.add))
                            c.link(nc.vector.reciprocal(rinv[:, u:u + 1], rsum[:, u:u + 1]))
                            nc.vector.tensor_scalar(ob[:, t, m * DH:(m + 1) * DH], k.bank(6 + m)[:, m * DH:(m + 1) * DH],
                                                    rinv[:, u:u + 1], None, ALU.mult).then_inc(S["comb"], 1)
                        elif m == 1:
                            c.link(nc.vector.reciprocal(rinv[:, u - 1:u + 1], rsum[:, u - 1:u + 1]))
                            nc.vector.tensor_scalar(t2, k.bank(7)[:, 0:P], rinv[:, u:u + 1], neglam, ALU.mult,
                                                    ALU.mult).then_inc(S["comb"], 1)
                            dve.wait_ge(S["comb"], N + u + LEAD)
                            nc.vector.scalar_tensor_tensor(out=ob[:, t, :], in0=k.bank(6)[:, 0:P],
                                                           scalar=rinv[:, u - 1:u], in1=t2, op0=ALU.mult,
                                                           op1=ALU.add).then_inc(S["comb"], 1)
                            dve.wait_ge(S["comb"], N + u + 1 + LEAD)
                            op = nc.vector.tensor_tensor_reduce(junk, ob[:, t, :], ob[:, t, :], 1.0, 0.0, ALU.mult,
                                                                ALU.add, ssq[:, t:t + 1])
                            if t == LAT_TILES:
                                op.then_inc(S["ssq"], 1)
                                dve.wait_ge(S["ssq"], i + 1)
                            else:
                                c.link(op)

                    if odd:
                        dve.wait_ge(S["q_in"], QIN * i + QIN)
                    for u in range(UN):
                        t, m, lo, hi = unit(u)
                        dve.wait_ge(S["qk"], N + u + 1 + LEAD)
                        if odd:
                            dve.wait_ge(S["pt"], N + max(u - 1, 0) + LEAD)
                            nc.vector.tensor_copy(tick, mask[:, 0:1])
                            nc.vector.tensor_tensor_reduce(prob[:, u % 2, 0:hi - lo], k.pt[m][:, lo:hi], mask[:, lo:hi],
                                                           SCALE, -3e38, ALU.add, ALU.max, top[:, u:u + 1]).then_inc(S["max"], 1)
                            dve.wait_ge(S["max"], N + u + 1 + LEAD)
                            nc.vector.tensor_scalar(negm[:, u:u + 1], top[:, u:u + 1],
                                                    sinkc[:, b, m:m + 1], -1.0, ALU.max,
                                                    ALU.mult).then_inc(S["small"], 1)
                        else:
                            nc.vector.reduce_max(top[:, u:u + 1], k.pt[m][:, lo:hi], AX).then_inc(S["max"], 1)
                            dve.wait_ge(S["max"], N + u + 1 + LEAD)
                            nc.vector.tensor_scalar(negm[:, u:u + 1], top[:, u:u + 1], -SCALE, None,
                                                    ALU.mult).then_inc(S["small"], 1)
                        if u:
                            evacuate(u - 1)
                        if u >= 2:
                            combine(u - 2)
                    evacuate(UN - 1)
                    combine(UN - 2)
                    combine(UN - 1)
                    if not odd:
                        dve.wait_ge(S["rstd"], 2 * i + 2)
                        nc.vector.tensor_tensor(ob, ob, rstd.rearrange("p (t o) -> p t o", o=1).broadcast_to([P, TILES, P]),
                                                ALU.mult).then_inc(S["norm"], 1)
                c.leave(ITER // 2)



def norm_steps(k, tag):
    return {n: k.sem(f"ln_{n}_{tag}") for n in ("rows_in", "done", "read", "stats", "lnvar", "rstd", "shift", "normed",
                                                "scaled", "ready", "out", "y_in")}


def phase_residual_norm(k, a, l, which):
    nc = k.nc
    tag = f"{l}{which}"
    S = norm_steps(k, tag)
    gate_rows = k.at(k.H, 2048).rearrange("p (g n) -> p g n", g=2)
    ln_g, ln_b = k.at(k.H + 2048, D), k.at(k.H + 3072, D)
    tmp = k.at(k.scr, 2048).rearrange("p (b n) -> p b n", b=2)
    st = k.at(k.scr + 2048, 12 * TILES).rearrange("p (t n) -> p t n", t=TILES)
    mv = k.at(k.scr + 2110, 2 * TILES).rearrange("p (t n) -> p t n", t=TILES)
    rstd = k.at(k.scr + 2120, TILES)
    shift = k.at(k.scr + 2125, TILES)
    part = GA1 if which == 0 else GA2
    base = BASE_OUT0 if l == 0 else BASE_OUT1
    last_norm = l == DEPTH - 1 and which == 1
    with nc.Block() as block:
        @block.sync
        def _(sp):
            for g in range(2):
                off = (2 * l + g) * 6 * D + part * P
                sp.dma_start(gate_rows[:, g, :], bcast_rows(k.dram["mod_rows"], off, [[1, D]])).then_inc(S["rows_in"], 16)
            off = (2 * l + which) * D
            sp.dma_start(ln_g, bcast_rows(a["ln_g"], off, [[1, D]])).then_inc(S["rows_in"], 16)
            sp.dma_start(ln_b, bcast_rows(a["ln_b"], off, [[1, D]])).then_inc(S["rows_in"], 16)
            if which == 1 and l == 0:
                for u in range(WSLOTS):
                    feed(k, sp, BASE_IN1 + u, in1_units(a)[u])
            if which == 1:
                sp.dma_start(k.y, k.dram["y_rows"].rearrange("(t p) n -> p t n", p=P)).then_inc(S["y_in"], 16)
            for t in range(TILES):
                sp.wait_ge(S["ready"], t + 1)
                if last_norm:
                    dst = a["y_sample"][t * P:(t + 1) * P, :] if t < LAT_TILES else a["y_prompt"]
                else:
                    dst = k.dram["y_rows"][t * P:(t + 1) * P, :]
                sp.dma_start(dst, k.y[:, t, :]).then_inc(S["out"], 16)
            sp.wait_ge(S["out"], 16 * TILES)

        @block.tensor
        def _(pe):
            if which == 1:
                return
            for s in range(4):
                n = base + s
                pe.wait_ge(k.w_landed[n % WSLOTS], 16 * (n // WSLOTS + 1))
                for t in range(TILES):
                    g = s * TILES + t
                    if g >= 8:
                        pe.wait_ge(S["read"], g - 7)
                    for c in range(KC):
                        last = nc.tensor.matmul(k.bank(g % 8)[:, 0:UNIT], k.mx[:, c, t * P:(t + 1) * P],
                                                k.wst[n % WSLOTS][:, c, :], start=(c == 0), stop=(c == KC - 1))
                    last.then_inc(S["done"], 1)

        @block.scalar
        def _(act):
            for t in range(TILES):
                act.wait_ge(S["stats"], t + 1)
                nc.scalar.activation(rstd[:, t:t + 1], mv[:, t, 1:2], ACT.Ln, bias=k.eps).then_inc(S["lnvar"], 1)
                act.wait_ge(S["lnvar"], t + 1)
                nc.scalar.activation(rstd[:, t:t + 1], rstd[:, t:t + 1], ACT.Exp, scale=-0.5).then_inc(S["rstd"], 1)
                act.wait_ge(S["shift"], t + 1)
                act.wait_ge(S["rstd"], t + 1)
                nc.scalar.activation(k.y[:, t, :], k.y[:, t, :], ACT.Identity, scale=rstd[:, t:t + 1],
                                     bias=shift[:, t:t + 1]).then_inc(S["normed"], 1)

        @block.gpsimd
        def _(pool):
            for t in range(TILES):
                pool.wait_ge(S["scaled"], t + 1)
                nc.gpsimd.tensor_tensor(k.y[:, t, :], k.y[:, t, :], ln_b, ALU.add).then_inc(S["ready"], 1)

        @block.vector
        def _(dve):
            c = Chain(k, dve, f"ln_dve_{tag}")
            dve.wait_ge(S["rows_in"], 64)
            if which == 1:
                dve.wait_ge(S["y_in"], 16)

            def statistics(t):
                nc.vector.bn_stats(st[:, t, 0:6], k.y[:, t, 0:512])
                c.link(nc.vector.bn_stats(st[:, t, 6:12], k.y[:, t, 512:1024]))
                nc.vector.bn_aggr(mv[:, t, :], st[:, t, :]).then_inc(S["stats"], 1)

            def finish(t):
                dve.wait_ge(S["rstd"], t + 1)
                dve.wait_ge(S["stats"], t + 1)
                nc.vector.tensor_scalar(shift[:, t:t + 1], mv[:, t, 0:1], rstd[:, t:t + 1], -1.0, ALU.mult,
                                        ALU.mult).then_inc(S["shift"], 1)

            def scale(t):
                dve.wait_ge(S["normed"], t + 1)
                nc.vector.tensor_tensor(k.y[:, t, :], k.y[:, t, :], ln_g, ALU.mult).then_inc(S["scaled"], 1)

            if which == 0:
                for s in range(4):
                    for t in range(TILES):
                        g = s * TILES + t
                        cols = slice(s * UNIT, (s + 1) * UNIT)
                        dve.wait_ge(S["done"], g + 1)
                        x = tmp[:, g % 2, 0:UNIT]
                        nc.vector.tensor_tensor(x, k.bank(g % 8)[:, 0:UNIT], gate_rows[:, t // LAT_TILES, cols],
                                                ALU.mult).then_inc(S["read"], 1)
                        dve.wait_ge(S["read"], g + 1)
                        c.link(nc.vector.scalar_tensor_tensor(out=k.y[:, t, cols], in0=k.y[:, t, cols], scalar=ALPHA,
                                                              in1=x, op0=ALU.mult, op1=ALU.add))
            for t in range(TILES):
                if which == 1:
                    c.link(nc.vector.tensor_tensor(tmp[:, t % 2, :], k.moe[:, t, :], gate_rows[:, t // LAT_TILES, :], ALU.mult))
                    c.link(nc.vector.scalar_tensor_tensor(out=k.y[:, t, :], in0=k.y[:, t, :], scalar=ALPHA,
                                                          in1=tmp[:, t % 2, :], op0=ALU.mult, op1=ALU.add))
                statistics(t)
                if t:
                    finish(t - 1)
                if t >= 2:
                    scale(t - 2)
            finish(TILES - 1)
            scale(TILES - 2)
            scale(TILES - 1)


def load_half(k, sp, a, l, e, s, slot):
    if s < 4:
        name = ("w_exp_gate", "w_exp_up")[s % 2]
        src, dst = a[name][l].rearrange("e (c p) (h n) -> e h p c n", p=P, h=2)[e, s // 2], k.ring[slot]
    else:
        src = a["w_exp_down"][l].rearrange("e (h c p) n -> e h p c n", p=P, h=2)[e, s - 4]
        dst = k.ring[slot].rearrange("p c n -> p (c n)").rearrange("p (c n) -> p c n", c=4)
    sp.dma_start(dst, src).then_inc(k.r_landed[slot], 16)


def moe_views(k):
    w, s = k.WST, k.scr
    v = {}
    v["xs"] = k.at(w, 2048).rearrange("p (b n) -> p b n", b=2)
    v["rows"] = k.at(w + 2048, 2048).rearrange("p (b n) -> p b n", b=2)
    v["rowsc"] = k.at(w + 4096, D)
    v["hot"] = k.at(w + 5120, 1024).rearrange("p (b n) -> p b n", b=2)
    v["hotc"] = k.at(w + 6144, P)
    v["scale"] = k.at(w + 6272, 640).rearrange("p (c n) -> p c n", c=KC)
    v["shift"] = k.at(w + 6912, 640).rearrange("p (c n) -> p c n", c=KC)
    v["iota"] = k.at(s, NT)
    v["idx_pair"] = k.at(s + 640, E // 2)
    v["idx_ctx"] = k.at(s + 648, E // 4)
    v["idx80"] = k.at(s + 652, E + 1)
    v["gate80"] = k.at(s + 669, E + 1)
    v["icol"] = k.at(s + 686, 2)
    v["gcol"] = k.at(s + 688, 2)
    v["tick"] = k.at(s + 690, 1)
    v["hid"] = k.at(s + 700, FF)
    v["sg"] = k.at(s + 700 + FF, FF)
    return v


def phase_router(k, a, l):
    nc = k.nc
    v = moe_views(k)
    s0 = k.scr + 700
    wr = k.at(s0, 128).rearrange("p (c n) -> p c n", c=KC)
    top = k.at(s0 + 128, TILES)
    tot = k.at(s0 + 133, TILES)
    aff = k.at(s0 + 140, 80).rearrange("p (t n) -> p t n", t=TILES)
    affT = k.at(s0 + 220, NT)[0:E]
    vals = k.at(s0 + 860, SLOTS)[0:E]
    idx = k.at(s0 + 940, SLOTS).bitcast(U32)[0:E]
    idf = k.at(s0 + 1020, SLOTS)[0:E]
    S = {n: k.sem(f"ro_{n}_{l}") for n in ("w_in", "logits", "sub", "exp", "aff", "turned", "picked", "kept", "laid", "cleared")}
    lg = k.bank(4)[:, 0:80].rearrange("p (t n) -> p t n", t=TILES)
    with nc.Block() as block:
        @block.sync
        def _(sp):
            sp.dma_start(wr, a["w_router"][l].rearrange("(c p) n -> p c n", p=P)).then_inc(S["w_in"], 16)
            sp.dma_start(v["iota"], a["iota"]).then_inc(S["w_in"], 16)
            sp.wait_ge(S["picked"], 1)
            dv, di = k.dram["gates"], k.dram["index"]
            ns = E * CAP_S
            for dst, src in ((dv, vals), (di, idf)):
                sp.dma_start(dst[0:ns].rearrange("(e s) -> e s", s=CAP_S), src[:, 0:CAP_S]).then_inc(S["kept"], 16)
                sp.dma_start(dst[ns:].rearrange("(e s) -> e s", s=CAP_P), src[:, CAP_S:SLOTS]).then_inc(S["kept"], 16)
            sp.wait_ge(S["kept"], 64)
            sp.wait_ge(S["cleared"], 1)
            with nc.allow_non_contiguous_dma(reason="slot tables of a few hundred words"):
                for dst, src in (("idx80", di), ("gate80", dv)):
                    sp.dma_start(v[dst][0:CAP_S, 0:E], src[0:ns].rearrange("(e s) -> s e", s=CAP_S)).then_inc(S["laid"], 16)
                    sp.dma_start(v[dst][CAP_S:SLOTS, 0:E],
                                 src[ns:].rearrange("(e s) -> s e", s=CAP_P)).then_inc(S["laid"], 16)
                sp.dma_start(v["idx_pair"], di[0:ns].rearrange("(e s) -> s e", s=P)).then_inc(S["laid"], 16)
                for j in range(4):
                    sp.dma_start(v["idx_ctx"][32 * j:32 * j + CAP_P],
                                 di[ns:].rearrange("(g j s) -> j s g", j=4, s=CAP_P)[j]).then_inc(S["laid"], 16)
            sp.wait_ge(S["laid"], 144)

        @block.tensor
        def _(pe):
            pe.wait_ge(S["w_in"], 32)
            for t in range(TILES):
                for c in range(KC):
                    last = nc.tensor.matmul(lg[:, t, :], k.h[:, c, t * P:(t + 1) * P], wr[:, c, :], start=(c == 0),
                                            stop=(c == KC - 1))
            last.then_inc(S["logits"], 1)
            pe.wait_ge(S["aff"], 1)
            for t in range(TILES):
                last = nc.tensor.transpose(k.pt[0][0:E, t * P:(t + 1) * P], aff[:, t, :], k.ident)
            last.then_inc(S["turned"], 1)

        @block.scalar
        def _(act):
            act.wait_ge(S["sub"], 1)
            nc.scalar.activation(aff, aff, ACT.Exp).then_inc(S["exp"], 1)

        @block.gpsimd
        def _(pool):
            nc.gpsimd.memset(v["idx_ctx"], -1.0)
            nc.gpsimd.memset(v["gate80"][:, E:E + 1], 0.0)
            nc.gpsimd.memset(v["idx80"][:, E:E + 1], 0.0).then_inc(S["cleared"], 1)
            nc.gpsimd.memset(k.mx, 0.0)
            nc.gpsimd.memset(v["rows"][:, 1], 0.0)
            nc.gpsimd.memset(v["rowsc"], 0.0)
            nc.gpsimd.memset(v["hot"][:, 1], 0.0)
            nc.gpsimd.memset(v["hotc"], 0.0)

        @block.vector
        def _(dve):
            c = Chain(k, dve, f"ro_dve_{l}")
            for name, part in (("scale", SC2), ("shift", SH2)):
                for g, (lo, hi) in enumerate(((0, CAP_S), (CAP_S, SLOTS))):
                    nc.vector.tensor_copy(v[name][:, :, lo:hi],
                                          k.mod[l][:, part:part + KC, g:g + 1].broadcast_to([P, KC, hi - lo]))
            dve.wait_ge(S["logits"], 1)
            c.link(nc.vector.reduce_max(top, lg, AX))
            nc.vector.tensor_tensor(aff, lg, top.rearrange("p (t o) -> p t o", o=1).broadcast_to([P, TILES, E]),
                                    ALU.subtract).then_inc(S["sub"], 1)
            dve.wait_ge(S["exp"], 1)
            c.link(nc.vector.reduce_sum(tot, aff, AX))
            c.link(nc.vector.reciprocal(tot, tot))
            nc.vector.tensor_tensor(aff, aff, tot.rearrange("p (t o) -> p t o", o=1).broadcast_to([P, TILES, E]),
                                    ALU.mult).then_inc(S["aff"], 1)
            dve.wait_ge(S["turned"], 1)
            c.link(nc.vector.tensor_copy(affT, k.pt[0][0:E, 0:NT]))
            for lo, hi, first, rounds in ((0, NS, 0, CAP_S // 8), (NS, NT, CAP_S, CAP_P // 8)):
                row = affT[:, lo:hi]
                for r in range(rounds):
                    sl = slice(first + 8 * r, first + 8 * r + 8)
                    c.link(nc.vector.max(vals[:, sl], row))
                    c.link(nc.vector.max_index(idx[:, sl], vals[:, sl], row))
                    if r < rounds - 1:
                        c.link(nc.vector.match_replace(row, vals[:, sl], row, -1.0))
            nc.vector.tensor_copy(idf[:, 0:CAP_S], idx[:, 0:CAP_S])
            nc.vector.tensor_scalar(idf[:, CAP_S:SLOTS], idx[:, CAP_S:SLOTS], float(NS), None,
                                    ALU.add).then_inc(S["picked"], 1)


def phase_experts(k, a, l):
    nc = k.nc
    v = moe_views(k)
    v.update(x32=k.x32, xh=k.xh, xl=k.xl, hidh=k.hidh, hidl=k.hidl)
    S = {n: k.sem(f"ex_{n}_{l}") for n in ("icol", "gathered0", "gathered1", "xturned", "xmul", "xsum", "xhigh", "xlow",
                                           "silu", "hid", "hturned", "hhigh", "hlow", "rows", "hot", "sum", "acc",
                                           "high", "low_dve", "low_pool", "passed")}
    GATHERED = (S["gathered0"], S["gathered1"])
    LEAD = 4
    ROUNDS = E // 4
    SUMS = 4 * 4 + 2
    G, U, O = (2, 4), (3, 5), (6, 7)
    sg, hid = v["sg"][0:SLOTS], v["hid"][0:SLOTS]
    NP = 12
    POOL_PIECES = (1, 5, 9)
    DVE_PIECES = [p for p in range(NP) if p not in POOL_PIECES]
    base = NP * E * l

    def side(x):
        return x.rearrange("p (c n) -> p c n", n=SLOTS)

    def landed(eng, i, q, s):
        eng.wait_ge(k.r_landed[s % 3], 128 * i + 16 * (2 * E * l + 2 * q + s // 3 + 1))

    def piece(p):
        s, h = divmod(p, 2)
        slot = k.ring[s % 3]
        if s < 4:
            raw = slot[:, 4 * h:4 * h + 4, :]
        else:
            raw = slot.rearrange("p c n -> p (c n)").rearrange("p (c n) -> p c n", c=4)[:, :, 512 * h:512 * h + 512]
        return raw, k.high[p % 4], k.low[p % 4]

    def split(eng, i, q, p):
        n, name = (POOL_PIECES, "low_pool") if p in POOL_PIECES else (DVE_PIECES, "low_dve")
        eng.wait_ge(S[name], 4 * len(n) * i + (len(n) * q + n.index(p) + 1 + LEAD))

    def sums(q):
        pair = 1 if q < 2 else 0
        out = [("pair", pair, t, hf) for t in ((0, 1) if q % 2 == 0 else (2, 3)) for hf in range(2)]
        return out + ([("ctx", 0, LAT_TILES, hf) for hf in range(2)] if q == 0 else [])

    def sums_before(q):
        return sum(len(sums(x)) for x in range(q))

    def rounds(engine, body):
        with engine.Fori(0, ROUNDS - 1) as i:
            body(i, False)
        body(ROUNDS - 1, True)

    with nc.Block() as block:
        @block.sync
        def _(sp):
            for s in S.values():
                if s not in GATHERED:
                    sp.sem_inc(s, LEAD)

            for s in range(3):
                load_half(k, sp, a, l, 0, s, s)

            def loads(i, last):
                for j in range(3, 24 if last else 27):
                    q, s = divmod(j - 3, 6)
                    split(sp, i, q, 2 * s + 1)
                    sp.sem_inc(S["passed"], 1)
                    load_half(k, sp, a, l, i * 4 + j // 6, j % 6, j % 3)
            rounds(sp, loads)

        @block.gpsimd
        def _(pool):
            def gather(i, q):
                e, b = 4 * i + q, q % 2
                pool.wait_ge(S["xturned"], e + (LEAD - 1))
                pool.wait_ge(S["rows"], 2 * e + (LEAD - 2))
                nc.gpsimd.tensor_copy(v["gcol"][0:SLOTS, b:b + 1], v["gate80"][0:SLOTS, bass.ds(e, 1)])
                nc.gpsimd.tensor_copy(v["icol"][0:SLOTS, b:b + 1].bitcast(U32),
                                      v["idx80"][0:SLOTS, bass.ds(e, 1)]).then_inc(S["icol"], 1)
                pool.wait_ge(S["icol"], e + (LEAD + 1))
                nc.gpsimd.tensor_tensor(v["tick"], v["iota"][:, 0:1], v["iota"][:, 0:1],
                                        ALU.add)
                nc.gpsimd.indirect_dma_start(
                    v["xs"][0:SLOTS, b, :], None, k.dram["y_rows"],
                    bass.IndirectOffsetOnAxis(ap=v["icol"][0:SLOTS, b:b + 1].bitcast(U32), axis=0)).then_inc(GATHERED[b], 16)

            def low(i, q, p):
                raw, high, out = piece(p)
                split(pool, i, q, p - 1)
                pool.wait_ge(S["high"], NP * (4 * i + q) + (p + 1 + LEAD))
                nc.gpsimd.tensor_tensor(out, raw, high, ALU.subtract).then_inc(S["low_pool"], 1)

            def body(i, last):
                for q in range(4):
                    more = not (last and q == 3)
                    j, r = (i, q + 1) if q < 3 else (i + 1, 0)
                    low(i, q, 5)
                    if more:
                        gather(j, r)
                    low(i, q, 9)
                    if more:
                        low(j, r, 1)

            gather(0, 0)
            low(0, 0, 1)
            rounds(pool, body)

        @block.tensor
        def _(pe):
            def turn_rows(b):
                for c in range(KC):
                    last = nc.tensor.transpose(k.bank(c // 4)[:, (c % 4) * SLOTS:(c % 4 + 1) * SLOTS],
                                               v["xs"][0:SLOTS, b, c * P:(c + 1) * P], k.ident[0:SLOTS, 0:SLOTS])
                last.then_inc(S["xturned"], 1)

            def turn_hidden(hf):
                for f in range(4):
                    col = hf * 512 + f * P
                    last = nc.tensor.transpose(k.bank(hf)[:, f * SLOTS:(f + 1) * SLOTS], hid[:, col:col + P],
                                               k.ident[0:SLOTS, 0:SLOTS])
                last.then_inc(S["hturned"], 1)

            def product(i, q, p, bank, xh, xl):
                h = p % 2 if p < 8 else (p - 8) // 2
                _, high, low = piece(p)
                split(pe, i, q, p)
                for c in range(4):
                    x, lo = xh[:, 4 * h + c, :], xl[:, 4 * h + c, :]
                    out = k.bank(bank)[0:SLOTS, :]
                    nc.tensor.matmul(out, x, high[:, c, :], start=(h == 0 and c == 0), stop=False)
                    nc.tensor.matmul(out, x, low[:, c, :], start=False, stop=False)
                    last = nc.tensor.matmul(out, lo, high[:, c, :], start=False, stop=(h == 1 and c == 3))
                last.then_inc(k.r_free, 1)

            def add_rows(what, b, t, hf, bank):
                if what == "pair":
                    lhs, rows = v["hot"][:, b, t * P:(t + 1) * P], v["rows"][:, b, hf * 512:(hf + 1) * 512]
                else:
                    lhs, rows = v["hotc"], v["rowsc"][:, hf * 512:(hf + 1) * 512]
                nc.tensor.matmul(k.bank(bank), lhs, rows, start=True, stop=True).then_inc(S["sum"], 1)

            def body(i, last_round):
                for q in range(4):
                    b = q % 2
                    e = 4 * i + q
                    pe.wait_ge(S["xlow"], e + (LEAD + 1))
                    pe.wait_ge(S["acc"], SUMS * i + (sums_before(q) + LEAD))
                    for p in range(8):
                        product(i, q, p, (G, U)[p // 2 % 2][p // 4], v["xh"][:, b], v["xl"][:, b])
                    pe.wait_ge(S["hid"], 2 * e + (LEAD + 1))
                    turn_hidden(0)
                    pe.wait_ge(S["rows"], 2 * e + LEAD)
                    pe.wait_ge(S["hot"], 3 * i + ((0, 0, 1, 1)[q] + LEAD))
                    for n, (what, pair, t, hf) in enumerate(sums(q)):
                        if n == 2:
                            pe.wait_ge(S["hid"], 2 * e + (LEAD + 2))
                        if n >= 4:
                            pe.wait_ge(S["acc"], SUMS * i + (sums_before(q) + n - 3 + LEAD))
                        add_rows(what, pair, t, hf, 2 + n % 4)
                    turn_hidden(1)
                    for part in range(2):
                        pe.wait_ge(S["hlow"], 2 * e + (LEAD + 1 + part))
                        if part == 1 and not (last_round and q == 3):
                            pe.wait_ge(GATHERED[1 - b], i * 32 + 16 * ((q + 1) // 2 + 1))
                            turn_rows(1 - b)
                        for hd in range(2):
                            product(i, q, 8 + 2 * part + hd, O[hd], v["hidh"], v["hidl"])

            pe.wait_ge(GATHERED[0], 16)
            turn_rows(0)
            rounds(pe, body)
            pe.wait_ge(S["rows"], 2 * E + LEAD)
            pe.wait_ge(S["hot"], 3 * ROUNDS + LEAD)
            for n, (what, pair, t, hf) in enumerate(sums(0) + sums(1)):
                pe.wait_ge(S["acc"], SUMS * ROUNDS + max(n - 3, 0) + LEAD)
                add_rows(what, pair, t, hf, 2 + n % 4)

        @block.scalar
        def _(act):
            def high(i, q, p):
                raw, dst, _ = piece(p)
                e = 4 * i + q
                landed(act, i, q, p // 2)
                if not (isinstance(e, int) and e == 0 and p < 4):
                    act.wait_ge(k.r_free, NP * e + (p - 3 + base))
                nc.scalar.copy(dst, raw).then_inc(S["high"], 1)

            def silu(i, q, hf):
                e = 4 * i + q
                act.wait_ge(k.r_free, NP * e + (4 * hf + 2 + base))
                act.wait_ge(S["hid"], 2 * e + (hf - 1 + LEAD))
                nc.scalar.activation(sg[:, hf * 512:(hf + 1) * 512], k.bank(G[hf])[0:SLOTS, :],
                                     ACT.Silu).then_inc(S["silu"], 1)

            def hidden(i, q, hf):
                e = 4 * i + q
                act.wait_ge(S["hturned"], 2 * e + (hf + 1 + LEAD))
                nc.scalar.copy(v["hidh"][:, 4 * hf:4 * hf + 4, :],
                               side(k.bank(hf)[:, 0:320])).then_inc(S["hhigh"], 1)

            def stationary(i, q):
                e = 4 * i + q
                act.wait_ge(S["xsum"], e + (1 + LEAD))
                nc.scalar.copy(v["xh"][:, q % 2], v["x32"]).then_inc(S["xhigh"], 1)

            def rows(i, q, hd):
                e = 4 * i + q
                gate = v["gcol"][:, q % 2:q % 2 + 1]
                lo = CAP_S * (q % 2)
                act.wait_ge(k.r_free, NP * e + (11 + hd + base))
                act.wait_ge(S["icol"], e + (LEAD + 1))
                cols = slice(hd * 512, (hd + 1) * 512)
                nc.scalar.activation(v["rows"][lo:lo + CAP_S, q // 2, cols], k.bank(O[hd])[0:CAP_S, :], ACT.Copy,
                                     scale=gate[0:CAP_S])
                nc.scalar.activation(v["rowsc"][32 * q:32 * q + CAP_P, cols], k.bank(O[hd])[CAP_S:SLOTS, :],
                                     ACT.Copy, scale=gate[CAP_S:SLOTS]).then_inc(S["rows"], 1)

            def body(i, last):
                for q in range(4):
                    more = not (last and q == 3)
                    j, r = (i, q + 1) if q < 3 else (i + 1, 0)
                    for p in range(4, 7):
                        high(i, q, p)
                    silu(i, q, 0)
                    high(i, q, 7)
                    high(i, q, 8)
                    silu(i, q, 1)
                    high(i, q, 9)
                    high(i, q, 10)
                    hidden(i, q, 0)
                    high(i, q, 11)
                    hidden(i, q, 1)
                    if more:
                        high(j, r, 0)
                        high(j, r, 1)
                        stationary(j, r)
                    rows(i, q, 0)
                    if more:
                        high(j, r, 2)
                    rows(i, q, 1)
                    if more:
                        high(j, r, 3)

            stationary(0, 0)
            for p in range(4):
                high(0, 0, p)
            rounds(act, body)

        @block.vector
        def _(dve):
            def modulate(i, q):
                e = 4 * i + q
                dve.wait_ge(S["xturned"], e + (1 + LEAD))
                dve.wait_ge(S["xlow"], e + LEAD)
                for hf in range(2):
                    chunks = slice(4 * hf, 4 * hf + 4)
                    nc.vector.tensor_tensor(v["x32"][:, chunks, :], side(k.bank(hf)[:, 0:320]), v["scale"][:, chunks, :],
                                            ALU.mult).then_inc(S["xmul"], 1)
                dve.wait_ge(S["xmul"], 2 * e + (2 + LEAD))
                nc.vector.tensor_tensor(v["x32"], v["x32"], v["shift"], ALU.add).then_inc(S["xsum"], 1)

            def stationary_low(i, q):
                dve.wait_ge(S["xhigh"], 4 * i + (q + 1 + LEAD))
                nc.vector.tensor_tensor(v["xl"][:, q % 2], v["x32"], v["xh"][:, q % 2],
                                        ALU.subtract).then_inc(S["xlow"], 1)

            def low(i, q, p):
                raw, high, out = piece(p)
                dve.wait_ge(S["high"], NP * (4 * i + q) + (p + 1 + LEAD))
                nc.vector.tensor_tensor(out, raw, high, ALU.subtract).then_inc(S["low_dve"], 1)

            def hidden(i, q, hf):
                e = 4 * i + q
                dve.wait_ge(S["silu"], 2 * e + (hf + 1 + LEAD))
                dve.wait_ge(k.r_free, NP * e + (4 * hf + 4 + base))
                dve.wait_ge(S["hturned"], 2 * e + (hf - 1 + LEAD))
                nc.vector.tensor_tensor(hid[:, hf * 512:(hf + 1) * 512], sg[:, hf * 512:(hf + 1) * 512],
                                        k.bank(U[hf])[0:SLOTS, :], ALU.mult).then_inc(S["hid"], 1)

            def hidden_low(i, q, hf):
                chunks = slice(4 * hf, 4 * hf + 4)
                dve.wait_ge(S["hhigh"], 2 * (4 * i + q) + (hf + 1 + LEAD))
                nc.vector.tensor_tensor(v["hidl"][:, chunks, :], side(k.bank(hf)[:, 0:320]),
                                        v["hidh"][:, chunks, :], ALU.subtract).then_inc(S["hlow"], 1)

            def add_sum(i, q, n):
                _, _, t, hf = (sums(0) + sums(1) if q is None else sums(q))[n]
                dve.wait_ge(S["sum"], SUMS * i + ((sums_before(q) if q is not None else 0) + n + 1 + LEAD))
                acc = k.moe[:, t, hf * 512:(hf + 1) * 512]
                nc.vector.tensor_tensor(acc, acc, k.bank(2 + n % 4), ALU.add).then_inc(S["acc"], 1)

            def body(i, last):
                for q in range(4):
                    more = not (last and q == 3)
                    j, r = (i, q + 1) if q < 3 else (i + 1, 0)
                    for p in (4, 6, 7):
                        low(i, q, p)
                    hidden(i, q, 0)
                    low(i, q, 8)
                    hidden(i, q, 1)
                    add_sum(i, q, 0)
                    add_sum(i, q, 1)
                    hidden_low(i, q, 0)
                    low(i, q, 10)
                    for n in range(2, len(sums(q))):
                        add_sum(i, q, n)
                    hidden_low(i, q, 1)
                    low(i, q, 11)
                    if more:
                        modulate(j, r)
                        low(j, r, 0)
                        stationary_low(j, r)
                        low(j, r, 2)
                    if q % 2:
                        nc.vector.tensor_scalar(v["hot"][:, q // 2, :], v["iota"][:, 0:NS],
                                                v["idx_pair"][:, bass.ds(2 * i + q // 2, 1)], None,
                                                ALU.is_equal).then_inc(S["hot"], 1)
                    if q == 3:
                        nc.vector.tensor_scalar(v["hotc"], v["iota"][:, NS:NT], v["idx_ctx"][:, bass.ds(i, 1)], None,
                                                ALU.is_equal).then_inc(S["hot"], 1)
                    if more:
                        low(j, r, 3)

            modulate(0, 0)
            stationary_low(0, 0)
            for p in (0, 2, 3):
                low(0, 0, p)
            rounds(dve, body)
            for n in range(8 + 2):
                add_sum(ROUNDS, None, n)


def build(nc, a, last=None):
    with ExitStack() as stack:
        dram = {
            "mod_rows": nc.dram_tensor("mod_rows", (DEPTH, 2, 6 * D), F32, kind="Internal").ap(),
            "mod_raw": nc.dram_tensor("mod_raw", (2, 6 * D), F32, kind="Internal").ap(),
            "y_rows": nc.dram_tensor("y_rows", (NT, D), F32, kind="Internal").ap(),
            "gates": nc.dram_tensor("slot_gates", (E * SLOTS,), F32, kind="Internal").ap(),
            "index": nc.dram_tensor("slot_index", (E * SLOTS,), F32, kind="Internal").ap(),
        }
        k = Ctx(nc, stack, dram)
        k.moe = k.mx.rearrange("p c n -> p (c n)").rearrange("p (t n) -> p t n", t=TILES)
        phases = [
            ("area0", k.for_mixer),
            ("mod", lambda: phase_modulation(k, a)),
            ("h0", lambda: phase_modulate(k, 0, SH1, SC1, "00")),
            ("proj0", lambda: phase_project_even(k, a)),
            ("hgrn", lambda: phase_hgrn(k, a)),
            ("clear0", k.clear),
            ("rope0", lambda: phase_rope(k, a, False)),
            ("att0", lambda: phase_attention(k, a, False)),
            ("ln00", lambda: phase_residual_norm(k, a, 0, 0)),
            ("h0b", lambda: phase_modulate(k, 0, SH2, SC2, "01")),
            ("router0", lambda: phase_router(k, a, 0)),
            ("area_moe0", k.for_experts),
            ("moe0", lambda: phase_experts(k, a, 0)),
            ("area_ln01", k.for_mixer),
            ("ln01", lambda: phase_residual_norm(k, a, 0, 1)),
            ("clear", k.clear),
            ("h1", lambda: phase_modulate(k, 1, SH1, SC1, "10")),
            ("proj1", lambda: phase_project_odd(k, a)),
            ("rope1", lambda: phase_rope(k, a, True)),
            ("att1", lambda: phase_attention(k, a, True)),
            ("ln10", lambda: phase_residual_norm(k, a, 1, 0)),
            ("h1b", lambda: phase_modulate(k, 1, SH2, SC2, "11")),
            ("router1", lambda: phase_router(k, a, 1)),
            ("area_moe1", k.for_experts),
            ("moe1", lambda: phase_experts(k, a, 1)),
            ("area_ln11", k.for_mixer),
            ("ln11", lambda: phase_residual_norm(k, a, 1, 1)),
        ]
        for name, phase in phases:
            phase()
            if last and name == last[0]:
                last[1](k)
                break
        k.area_stack.close()


_OUTS = {
    "y_prompt": (1, 128, 1024), "y_sample": (1, 512, 1024), "out_state": (1, 1, 2, 4, 128, 128),
    "out_diff_k": (1, 1, 4, 128, 128), "out_diff_v": (1, 1, 4, 128, 128),
    "out_win_k": (1, 1, 4, 128, 64), "out_win_v": (1, 1, 4, 128, 64),
}


def constants():
    t = np.arange(NS)
    quarter = DH // 4
    inv = (10000.0 ** (-np.arange(quarter, dtype=np.float32) / quarter)).astype(np.float32)
    angle = np.zeros((P, NS), np.float32)
    perm = np.zeros((P, P), np.float32)
    for d in range(P):
        half, j = divmod(d % DH, DH // 2)
        pos = (t // 64 if half == 0 else t % 64).astype(np.float32)
        angle[d] = pos * inv[j % quarter]
        if j < quarter:
            perm[d + quarter, d] = -1.0
        else:
            perm[d - quarter, d] = 1.0
    r = np.arange(P)
    masks = np.zeros((P, 2, 192), np.int32)
    for d in range(2):
        same = (r[:, None] // SUB) == (r[None, :] // SUB)
        order = (r[:, None] <= r[None, :]) if d == 0 else (r[:, None] >= r[None, :])
        masks[:, d, 0:P] = np.where(same & order, -1, 0)
        cols = r.reshape(4, 2, SUB)[:, 1 - d, :].reshape(-1)
        pair = (r[:, None] // CH) == (cols[None, :] // CH)
        first = (r[:, None] // SUB) % 2 == d
        masks[:, d, P:192] = np.where(pair & first, -1, 0)
    keep = np.ones((P, NT + 1), np.float32)
    keep[:, ::SUB] = 0.0
    wmask = np.zeros((P, 768), np.float32)
    wmask[:, 128:256] = np.where(r[:, None] <= r[None, :], 0.0, NEG)
    wmask[:, 640:768] = np.where(r[None, :] <= r[:, None], 0.0, NEG)
    return {
        "ident": np.eye(P, dtype=np.float32), "perm": perm, "cos": np.cos(angle), "sin": np.sin(angle),
        "hgrn_masks": masks, "keep": keep, "wmask": wmask,
        "bmask": (r[:, None] // CH == np.arange(4)[None, :]).astype(np.float32),
        "halves": (r[:, None] // DH == np.arange(2)[None, :]).astype(np.float32),
        "iota": np.broadcast_to(np.arange(NT, dtype=np.float32), (P, NT)).copy(),
    }


PAIRED = [h for m in range(8) for h in ((m, 4 + m) if m < 4 else (4 + m, 8 + m))]


def kernel(**inputs):
    import concourse.bacc as _bacc
    from concourse.bass_utils import run_bass_kernel_spmd as _run

    nc = _bacc.Bacc("TRN2", target_bir_lowering=False, num_devices=1)
    arrays = {n: np.ascontiguousarray(x) for n, x in inputs.items()}
    w = arrays["w_in_odd"]
    q = w[:, :, :1024].reshape(1, D, 16, DH)[:, :, PAIRED, :].reshape(1, D, 1024)
    arrays["w_in_odd"] = np.concatenate([q, w[:, :, 1024:]], axis=2)
    arrays["w_out_odd"] = arrays["w_out_odd"].reshape(1, 16, DH, D)[:, PAIRED].reshape(1, D, D)
    arrays["win_sink"] = np.ascontiguousarray(arrays["win_sink"][:, PAIRED])
    arrays.update(constants())
    arrays = {f"in_{n}": x for n, x in arrays.items()}
    a = {n[3:]: nc.dram_tensor(n, x.shape, mybir.dt.from_np(x.dtype), kind="ExternalInput").ap() for n, x in arrays.items()}
    for n, shape in _OUTS.items():
        a[n] = nc.dram_tensor(f"res_{n}", shape, F32, kind="ExternalOutput").ap()
    for n in ("y_prompt", "y_sample"):
        a[n] = a[n][0]
    for n in ("out_state", "out_diff_k", "out_diff_v", "out_win_k", "out_win_v"):
        a[n] = a[n][0, 0]
    build(nc, a)
    r = _run(nc, [arrays], core_ids=[0])
    return tuple(r.results[0][f"res_{n}"] for n in _OUTS)
```
